# Optimizing a Trainium2 kernel written in Bass

```python
import math
import jax, jax.numpy as jnp
from jax import lax
import numpy as np

D_MODEL = 1024
BATCH = 1
SEQ = 256
DEPTH = 2

D_CONV = 256
CONV_WIDTH = 3
D_SSM = 256
SSM_GROUP = 16
N_SSM_GROUPS = D_SSM // SSM_GROUP
SSM_STATE = 64
DT_MIN = 1e-3
DT_MAX = 1e-1
N_Q_HEADS = 8
N_KV_HEADS = 2
HEAD_DIM = 64
D_ATTN = N_Q_HEADS * HEAD_DIM
D_KV = N_KV_HEADS * HEAD_DIM
WINDOW = 128
BLOCK = 128
N_BRANCH = 3
D_FF = 2816
ALPHA = (2 * DEPTH) ** 0.25
BETA = (8 * DEPTH) ** -0.25
LN_EPS = 1e-5
D_IN = 3 * D_CONV + D_SSM + D_ATTN + 2 * D_KV + N_BRANCH * D_MODEL

kernel_name = 'hybrid_gated_conv_s5_swa_macaron_deepnorm'

def layer_norm(x, g, b):
    xf = x.astype(jnp.float32)
    mu = jnp.mean(xf, axis=-1, keepdims=True)
    var = jnp.mean(jnp.square(xf - mu), axis=-1, keepdims=True)
    y = (xf - mu) * lax.rsqrt(var + LN_EPS)
    return (y * g.astype(jnp.float32) + b.astype(jnp.float32)).astype(x.dtype)

def swiglu(x, w_gate, w_up, w_down):
    return (jax.nn.silu(x @ w_gate) * (x @ w_up)) @ w_down

def short_conv_mixer(b_gate, c_gate, h, conv_w, conv_b):
    z = c_gate * h
    kern = conv_w[:, None, :].astype(z.dtype)
    y = lax.conv_general_dilated(z, kern, window_strides=(1,), padding=[(CONV_WIDTH - 1, 0)],
                                 dimension_numbers=('NWC', 'WIO', 'NWC'), feature_group_count=D_CONV)
    return b_gate * (y + conv_b)

def s5_mixer(u, a_re, a_im, log_dt, b_re, b_im, c_re, c_im, d_skip, w_glu):
    f32 = jnp.float32
    bsz, s, _ = u.shape
    uf = u.astype(f32).reshape(bsz, s, N_SSM_GROUPS, SSM_GROUP)
    lr = a_re.astype(f32)
    li = a_im.astype(f32)
    dt = jnp.exp(log_dt.astype(f32))[:, None]
    mag = jnp.exp(lr * dt)
    ang = li * dt
    abar_re = mag * jnp.cos(ang)
    abar_im = mag * jnp.sin(ang)
    nr = abar_re - 1.0
    ni = abar_im
    den = lr * lr + li * li
    coef_re = (nr * lr + ni * li) / den
    coef_im = (ni * lr - nr * li) / den
    br = b_re.astype(f32)
    bi = b_im.astype(f32)
    bbar_re = coef_re[..., None] * br - coef_im[..., None] * bi
    bbar_im = coef_re[..., None] * bi + coef_im[..., None] * br
    bu_re = jnp.einsum('bsgc,gpc->bsgp', uf, bbar_re)
    bu_im = jnp.einsum('bsgc,gpc->bsgp', uf, bbar_im)
    aa_re = jnp.broadcast_to(abar_re, bu_re.shape)
    aa_im = jnp.broadcast_to(abar_im, bu_im.shape)

    def combine(e1, e2):
        a1r, a1i, b1r, b1i = e1
        a2r, a2i, b2r, b2i = e2
        return (a2r * a1r - a2i * a1i,
                a2r * a1i + a2i * a1r,
                a2r * b1r - a2i * b1i + b2r,
                a2r * b1i + a2i * b1r + b2i)

    _, _, xs_re, xs_im = lax.associative_scan(combine, (aa_re, aa_im, bu_re, bu_im), axis=1)
    y = (jnp.einsum('bsgp,gcp->bsgc', xs_re, c_re.astype(f32))
         - jnp.einsum('bsgp,gcp->bsgc', xs_im, c_im.astype(f32)))
    y = y + d_skip.astype(f32).reshape(N_SSM_GROUPS, SSM_GROUP) * uf
    y = jax.nn.gelu(y.reshape(bsz, s, D_SSM))
    y = y * jax.nn.sigmoid(y @ w_glu.astype(f32))
    return y.astype(u.dtype)

def sliding_window_attention(q, k, v, sinks):
    f32 = jnp.float32
    bsz, s, _ = q.shape
    nb = s // BLOCK
    grp = N_Q_HEADS // N_KV_HEADS
    qb = q.astype(f32).reshape(bsz, nb, BLOCK, N_KV_HEADS, grp, HEAD_DIM) * (HEAD_DIM ** -0.5)
    kb = k.astype(f32).reshape(bsz, nb, BLOCK, N_KV_HEADS, HEAD_DIM)
    vb = v.astype(f32).reshape(bsz, nb, BLOCK, N_KV_HEADS, HEAD_DIM)
    pad = ((0, 0), (1, 0), (0, 0), (0, 0), (0, 0))
    kk = jnp.concatenate([jnp.pad(kb, pad)[:, :-1], kb], axis=2)
    vv = jnp.concatenate([jnp.pad(vb, pad)[:, :-1], vb], axis=2)
    scores = jnp.einsum('bnqhgd,bnkhd->bnhgqk', qb, kk)
    qpos = jnp.arange(BLOCK)[:, None] + BLOCK
    kpos = jnp.arange(2 * BLOCK)[None, :]
    diff = qpos - kpos
    band = (diff >= 0) & (diff < WINDOW)
    has_prev = (jnp.arange(nb) > 0)[:, None, None] | (kpos >= BLOCK)[None]
    mask = band[None] & has_prev
    scores = jnp.where(mask[None, :, None, None], scores, -jnp.inf)
    sink = sinks.astype(f32).reshape(N_KV_HEADS, grp)[None, None, :, :, None, None]
    m = jnp.maximum(jnp.max(scores, axis=-1, keepdims=True), sink)
    p = jnp.exp(scores - m)
    probs = p / (jnp.sum(p, axis=-1, keepdims=True) + jnp.exp(sink - m))
    out = jnp.einsum('bnhgqk,bnkhd->bnqhgd', probs, vv)
    return out.reshape(bsz, s, D_ATTN).astype(q.dtype)

def hybrid_mixer(x, w_in, conv_w, conv_b, ssm_a_re, ssm_a_im, ssm_log_dt, ssm_b_re, ssm_b_im,
                 ssm_c_re, ssm_c_im, ssm_d, ssm_w_glu, attn_sinks, w_br_conv, w_br_ssm, w_br_attn, w_out):
    bsz, s, _ = x.shape
    proj = x @ w_in
    widths = [D_CONV, D_CONV, D_CONV, D_SSM, D_ATTN, D_KV, D_KV]
    offs = [int(o) for o in np.cumsum(widths)]
    b_g, c_g, h, u, q, k, v, gates = jnp.split(proj, offs, axis=-1)
    y_conv = short_conv_mixer(b_g, c_g, h, conv_w, conv_b) @ w_br_conv
    y_ssm = s5_mixer(u, ssm_a_re, ssm_a_im, ssm_log_dt, ssm_b_re, ssm_b_im,
                     ssm_c_re, ssm_c_im, ssm_d, ssm_w_glu) @ w_br_ssm
    y_attn = sliding_window_attention(q, k, v, attn_sinks) @ w_br_attn
    g = jax.nn.sigmoid(gates).reshape(bsz, s, N_BRANCH, D_MODEL)
    merged = g[:, :, 0] * y_conv + g[:, :, 1] * y_ssm + g[:, :, 2] * y_attn
    return merged @ w_out

def setup_inputs(seed: int = 0) -> dict:
    key = jax.random.key(seed)
    ks = jax.random.split(key, 32)
    L = DEPTH

    def nrm(k, shape, scale):
        return jax.random.normal(k, shape, jnp.float32) * scale

    def gain(k):
        return 1.0 + nrm(k, (L, D_MODEL), 0.01)

    n_idx = jnp.arange(SSM_STATE, dtype=jnp.float32)
    return {
        'x': nrm(ks[0], (BATCH, SEQ, D_MODEL), 1.0),
        'ffn1_w_gate': nrm(ks[1], (L, D_MODEL, D_FF), D_MODEL ** -0.5),
        'ffn1_w_up': nrm(ks[2], (L, D_MODEL, D_FF), D_MODEL ** -0.5),
        'ffn1_w_down': nrm(ks[3], (L, D_FF, D_MODEL), BETA * D_FF ** -0.5),
        'ln1_g': gain(ks[4]),
        'ln1_b': nrm(ks[5], (L, D_MODEL), 0.01),
        'w_in': nrm(ks[6], (L, D_MODEL, D_IN), D_MODEL ** -0.5),
        'conv_w': nrm(ks[7], (L, CONV_WIDTH, D_CONV), CONV_WIDTH ** -0.5),
        'conv_b': nrm(ks[8], (L, D_CONV), 0.01),
        'ssm_a_re': -0.5 + nrm(ks[9], (L, N_SSM_GROUPS, SSM_STATE), 0.01),
        'ssm_a_im': jnp.pi * n_idx + nrm(ks[10], (L, N_SSM_GROUPS, SSM_STATE), 0.01),
        'ssm_log_dt': jax.random.uniform(ks[11], (L, N_SSM_GROUPS), jnp.float32,
                                         math.log(DT_MIN), math.log(DT_MAX)),
        'ssm_b_re': nrm(ks[12], (L, N_SSM_GROUPS, SSM_STATE, SSM_GROUP), (2 * SSM_GROUP) ** -0.5),
        'ssm_b_im': nrm(ks[13], (L, N_SSM_GROUPS, SSM_STATE, SSM_GROUP), (2 * SSM_GROUP) ** -0.5),
        'ssm_c_re': nrm(ks[14], (L, N_SSM_GROUPS, SSM_GROUP, SSM_STATE), SSM_STATE ** -0.5),
        'ssm_c_im': nrm(ks[15], (L, N_SSM_GROUPS, SSM_GROUP, SSM_STATE), SSM_STATE ** -0.5),
        'ssm_d': nrm(ks[16], (L, D_SSM), 1.0),
        'ssm_w_glu': nrm(ks[17], (L, D_SSM, D_SSM), D_SSM ** -0.5),
        'attn_sinks': nrm(ks[18], (L, N_Q_HEADS), 0.5),
        'w_br_conv': nrm(ks[19], (L, D_CONV, D_MODEL), D_CONV ** -0.5),
        'w_br_ssm': nrm(ks[20], (L, D_SSM, D_MODEL), D_SSM ** -0.5),
        'w_br_attn': nrm(ks[21], (L, D_ATTN, D_MODEL), D_ATTN ** -0.5),
        'w_out': nrm(ks[22], (L, D_MODEL, D_MODEL), BETA * D_MODEL ** -0.5),
        'ln2_g': gain(ks[23]),
        'ln2_b': nrm(ks[24], (L, D_MODEL), 0.01),
        'ffn2_w_gate': nrm(ks[25], (L, D_MODEL, D_FF), D_MODEL ** -0.5),
        'ffn2_w_up': nrm(ks[26], (L, D_MODEL, D_FF), D_MODEL ** -0.5),
        'ffn2_w_down': nrm(ks[27], (L, D_FF, D_MODEL), BETA * D_FF ** -0.5),
        'ln3_g': gain(ks[28]),
        'ln3_b': nrm(ks[29], (L, D_MODEL), 0.01),
    }

def reference(x, ffn1_w_gate, ffn1_w_up, ffn1_w_down, ln1_g, ln1_b, w_in, conv_w, conv_b,
              ssm_a_re, ssm_a_im, ssm_log_dt, ssm_b_re, ssm_b_im, ssm_c_re, ssm_c_im, ssm_d,
              ssm_w_glu, attn_sinks, w_br_conv, w_br_ssm, w_br_attn, w_out, ln2_g, ln2_b,
              ffn2_w_gate, ffn2_w_up, ffn2_w_down, ln3_g, ln3_b):
    for l in range(DEPTH):
        x = layer_norm(ALPHA * x + 0.5 * swiglu(x, ffn1_w_gate[l], ffn1_w_up[l], ffn1_w_down[l]),
                       ln1_g[l], ln1_b[l])
        mix = hybrid_mixer(x, w_in[l], conv_w[l], conv_b[l], ssm_a_re[l], ssm_a_im[l], ssm_log_dt[l],
                           ssm_b_re[l], ssm_b_im[l], ssm_c_re[l], ssm_c_im[l], ssm_d[l], ssm_w_glu[l],
                           attn_sinks[l], w_br_conv[l], w_br_ssm[l], w_br_attn[l], w_out[l])
        x = layer_norm(ALPHA * x + mix, ln2_g[l], ln2_b[l])
        x = layer_norm(ALPHA * x + 0.5 * swiglu(x, ffn2_w_gate[l], ffn2_w_up[l], ffn2_w_down[l]),
                       ln3_g[l], ln3_b[l])
    return x


_drawn_inputs = setup_inputs


def setup_inputs(seed=0):
    import zlib

    import numpy as np

    out = dict(_drawn_inputs(seed))
    spreads = {}
    factors = {'ln1_g': 3.669,
     'ln1_b': 3.439,
     'conv_b': 29.411,
     'ssm_a_re': 64.0,
     'ssm_a_im': 60.688,
     'ssm_log_dt': 62.656,
     'ssm_b_re': 64.0,
     'ssm_b_im': 64.0,
     'ssm_c_re': 64.0,
     'ssm_c_im': 64.0,
     'attn_sinks': 61.76,
     'ln2_g': 3.932,
     'ln2_b': 3.821,
     'ln3_g': 3.776,
     'ln3_b': 3.771}
    for name, (base, spread) in spreads.items():
        noise = np.random.default_rng([zlib.crc32(name.encode()), seed]).standard_normal(out[name].shape)
        drawn = base * np.exp(spread * noise) if base else spread * noise
        out[name] = __import__('jax').numpy.asarray(drawn.astype(out[name].dtype))
    for name, factor in factors.items():
        out[name] = (out[name] * factor).astype(out[name].dtype)
    return out
```

```python
import math
from contextlib import ExitStack

import concourse.bass as bass
from concourse import mybir

F32 = mybir.dt.float32
F32R = mybir.dt.float32r
BF16 = mybir.dt.bfloat16
ALU = mybir.AluOpType
ACT = mybir.ActivationFunctionType
AX = mybir.AxisListType

P = 128
DEPTH, D, SEQ, DFF = 2, 1024, 256, 2816
KC = D // P
NT = SEQ // P
ALPHA = (2 * DEPTH) ** 0.25
EPS = 1e-5
SLOTS = 3
CHUNK = 2048
STEPS = DFF // 256
FFN_CHUNKS = 3 * STEPS
PROJ_CHUNKS = 19
MIX_CHUNKS = PROJ_CHUNKS + 8
LAYER_CHUNKS = 2 * FFN_CHUNKS + MIX_CHUNKS
MIX0 = FFN_CHUNKS
FFN0 = (0, FFN_CHUNKS + MIX_CHUNKS)
KV, QA, QB, UU, CC, HH, BB, GATE0 = range(8)
BRANCH = (19, 20, 22, 24)
OUT = (21, 23, 25, 26)
OFF_B, OFF_C, OFF_H, OFF_U, OFF_Q, OFF_K, OFF_G = 0, 256, 512, 768, 1024, 1536, 1792
HD, HEADS = 64, 8
STATE_TILES = 8
MASKED = -3.0e38
TWO_PI_A = 6.28125
TWO_PI_B = 1.934051513671875e-3
TWO_PI_C = 2 * 3.141592653589793 - TWO_PI_A - TWO_PI_B
ROUND = 1.5 * 2.0 ** 23
DMAS = [1] * LAYER_CHUNKS
for _k in (QA, QB):
    DMAS[MIX0 + _k] = 4
for _k in BRANCH:
    DMAS[MIX0 + _k] = 4
LANDED = [16 * sum(DMAS[_j] for _j in range(_k % SLOTS, _k + 1, SLOTS)) for _k in range(LAYER_CHUNKS)]
LANDED_LAYER = [16 * sum(DMAS[_s::SLOTS]) for _s in range(SLOTS)]
N_LN = 96
ROW_ARE, ROW_AIM, ROW_DT, ROW_CW, ROW_CB, ROW_D, N_SMALL = 0, 16, 32, 48, 60, 64, 68


POOL_LINKS, DVE_LINKS = 82, 40


class Events:

    def __init__(self, sem, layer, before=0, unit=1):
        self.sem, self.layer, self.before, self.unit = sem, layer, before, unit

    def at(self, l, n):
        return l * (self.layer * self.unit) + (n + self.before) * self.unit


class Chain:

    def __init__(self, layer):
        self.layer, self.n, self.base = layer, 0, 0

    def enter(self, l):
        self.before = self.n
        self.base = l * self.layer

    def leave(self):
        assert self.n - self.before == self.layer, (self.n - self.before, self.layer)

    def next(self):
        self.n += 1
        return self.base + self.n


def trunk(nc, x, ffn1_w_gate, ffn1_w_up, ffn1_w_down, ln1_g, ln1_b, w_in, conv_w, conv_b,
          ssm_a_re, ssm_a_im, ssm_log_dt, ssm_b_re, ssm_b_im, ssm_c_re, ssm_c_im, ssm_d,
          ssm_w_glu, attn_sinks, w_br_conv, w_br_ssm, w_br_attn, w_out, ln2_g, ln2_b,
          ffn2_w_gate, ffn2_w_up, ffn2_w_down, ln3_g, ln3_b, out):
    ctx = ExitStack()
    with ctx:
        def sb(name, shape, dt=F32):
            return ctx.enter_context(nc.sbuf_tensor(name, shape, dt))

        def overlay(first, second):
            size = [sum(4 * math.prod(shape[1:]) for _, shape, _ in s) for s in (first, second)]
            held, brief = (second, first) if size[1] >= size[0] else (first, second)
            with ExitStack() as own:
                over = [own.enter_context(nc.sbuf_tensor(*a)) for a in brief]
            kept = [sb(*a) for a in held]
            return over + kept if held is second else kept + over

        raw = [sb(f"raw{s}", [P, CHUNK]) for s in range(SLOTS)]
        w_hi = [sb(f"w_hi{s}", [P, CHUNK], F32R) for s in range(SLOTS)]
        w_lo = [sb(f"w_lo{s}", [P, CHUNK], F32R) for s in range(SLOTS)]
        xT = sb("xT", [P, KC, 2, SEQ], F32R)
        ax = sb("ax", [P, NT, D])
        gates, res, xTf, gb = overlay(
            [("gates", [P, 3, KC, SEQ], F32)],
            [("res", [P, NT, D], F32), ("xTf", [P, KC, SEQ], F32), ("gb", [P, 2, D], F32)])
        probsT, rows_hi, rows_lo = overlay(
            [("probsT", [P, 2 * HEADS, P], F32)],
            [("rows_hi", [P, 2, 2, SEQ], F32R), ("rows_lo", [P, 2, 2, SEQ], F32R)])
        S1, y_attn = overlay([("S1", [P, HEADS, 2 * P], F32)], [("y_attn", [P, 4, 2, SEQ], F32R)])
        S0, b_in, b_blk, c_in = overlay(
            [("S0", [P, HEADS, P], F32)],
            [("b_in", [P, 2, STATE_TILES, 16], F32), ("b_blk", [P, 2, STATE_TILES, 32], F32),
             ("c_in", [P, 2, 2, 2, HD], F32)])
        bTz, y_cs = overlay([("bTz", [P, STATE_TILES, 2, P], F32)], [("y_cs", [P, 4, 2, SEQ], F32R)])
        td, act, hid = overlay([("td", [P, 2, 2, SEQ], F32)], [("act", [P, 2, SEQ], F32), ("hid", [P, 2, SEQ], F32)])
        qT, cv_c, cv_h = overlay([("qT", [P, 4, SEQ], F32)], [("cv_c", [P, 2, SEQ], F32), ("cv_h", [P, 2, SEQ], F32)])
        kz = sb("kz", [P, 2, SEQ])
        vz = sb("vz", [P, 2, 2, P])
        mask = sb("mask", [P, 2 * P])
        sinks = sb("sinks", [P, HEADS])
        mx = sb("mx", [P, 2, HEADS])
        negm = sb("negm", [P, 2, HEADS])
        esink = sb("esink", [P, 2, HEADS])
        psum_p = sb("psum_p", [P, 2, HEADS])
        rden = sb("rden", [P, 2, HEADS])
        rot_c = sb("rot_c", [P, STATE_TILES, SEQ])
        rot_s = sb("rot_s", [P, STATE_TILES, SEQ])
        bu = sb("bu", [P, 2, 2, SEQ])
        sw = sb("sw", [P, 2, 2, SEQ])
        tp = sb("tp", [P, 2, 2, SEQ])
        uT = sb("uT", [P, 2, SEQ])
        cTz = sb("cTz", [P, STATE_TILES, 2, P])
        cv_b, w_glu = overlay([("cv_b", [P, 2, SEQ], F32)], [("w_glu", [P, 2, 256], F32)])
        cv_z = sb("cv_z", [P, 2, SEQ + 2])
        ln_rows = td[:, 0].rearrange("p a t -> p (a t)")[0:N_LN, 0:P]
        small_rows = td[:, 1].rearrange("p a t -> p (a t)")[0:N_SMALL, 0:P]
        dt_rows = td[:, 1].rearrange("p a t -> p (a t)")[ROW_DT:ROW_DT + 16, P:P + 2]
        lnT = sb("lnT", [P, 6, DEPTH, KC])
        smallT = sb("smallT", [P, N_SMALL])
        stat = sb("stat", [P, 5, DEPTH, STATE_TILES])
        sc, bnst, mv, veps, rstd = overlay(
            [("sc", [P, 8, DEPTH * STATE_TILES], F32)],
            [("bnst", [P, NT, 2, 6], F32), ("mv", [P, NT, 2], F32), ("veps", [P, NT], F32), ("rstd", [P, NT], F32)])
        ln_cur = sb("ln_cur", [P, 6, KC])
        st_cur = sb("st_cur", [P, 5, STATE_TILES])
        cw_cur = sb("cw_cur", [P, 3, 2])
        cb_cur = sb("cb_cur", [P, 2])
        d_cur = sb("d_cur", [P, 2])
        ident = sb("ident", [P, P])
        zero_b = sb("zero_b", [P, 512], BF16)
        mhalf, alpha = sb("mhalf", [P, 1]), sb("alpha", [P, 1])

        ps = ctx.enter_context(nc.psum_tensor("ps", [P, 8, 512], F32))
        acc = ps[:, 0:4, :].rearrange("p (t h) n -> p t h n", t=NT)

        def sem(name):
            return ctx.enter_context(nc.semaphore(name))

        x_landed, small_landed, out_stored = sem("x_landed"), sem("small_landed"), sem("out_stored")
        landed = [sem(f"landed{s}") for s in range(SLOTS)]
        layer_landed = Events(sem("layer_landed"), 7, unit=16)
        glu_landed = Events(sem("glu_landed"), 1, unit=16)
        zeros_made = Events(sem("zeros_made"), 1)
        gb_landed = Events(sem("gb_landed"), 6, unit=16)
        consts_made = sem("consts_made")
        rows_made, pro_tp, pro_small, state_act, state_dve = (
            sem("rows_made"), sem("pro_tp"), sem("pro_small"), sem("state_act"), sem("state_dve"))
        hi_made = Events(sem("hi_made"), LAYER_CHUNKS)
        lo_made = Events(sem("lo_made"), LAYER_CHUNKS, before=SLOTS)
        used = Events(sem("used"), LAYER_CHUNKS, before=SLOTS)
        silu_made = Events(sem("silu_made"), 2 * STEPS)
        h_made = Events(sem("h_made"), 2 * STEPS)
        h_hi = Events(sem("h_hi"), 2 * STEPS)
        h_lo = Events(sem("h_lo"), 2 * STEPS)
        res_made = Events(sem("res_made"), 3 * NT)
        var_made = Events(sem("var_made"), 3 * NT)
        rstd_made = Events(sem("rstd_made"), 3 * NT)
        xn_made = Events(sem("xn_made"), 3 * NT)
        tp_made = Events(sem("tp_made"), 3 * NT, before=NT)
        xTf_dve = Events(sem("xTf_dve"), 3 * NT, before=NT)
        xTf_act = Events(sem("xTf_act"), 3 * NT, before=NT)
        x_hi = Events(sem("x_hi"), 3 * NT, before=NT)
        x_lo = Events(sem("x_lo"), 3 * NT, before=NT)
        ax_made = Events(sem("ax_made"), 3 * NT, before=NT)
        cur_made = Events(sem("cur_made"), 1)
        bblk_made = Events(sem("bblk_made"), 1)
        bcT_done = Events(sem("bcT_done"), 1)
        bcT_made = Events(sem("bcT_made"), 1)
        rot_made = Events(sem("rot_made"), 1)
        proj_read = Events(sem("proj_read"), PROJ_CHUNKS)
        scores_done = Events(sem("scores_done"), 2)
        s_made = Events(sem("s_made"), 2)
        negm_made = Events(sem("negm_made"), 1)
        exp_made = Events(sem("exp_made"), 1)
        rden_made = Events(sem("rden_made"), 1)
        probs_made = Events(sem("probs_made"), 2)
        pT_done = Events(sem("pT_done"), 6)
        pT_made = Events(sem("pT_made"), 6)
        pv_done = Events(sem("pv_done"), 2)
        ya_hi = Events(sem("ya_hi"), 2)
        ya_lo = Events(sem("ya_lo"), 2)
        bu_done = Events(sem("bu_done"), 4)
        bu_made = Events(sem("bu_made"), 4)
        wim_made = Events(sem("wim_made"), 4)
        z_made = Events(sem("z_made"), 4)
        xre_made = Events(sem("xre_made"), 4)
        xim_made = Events(sem("xim_made"), 4)
        c_done = Events(sem("c_done"), 4)
        yd_made = Events(sem("yd_made"), 1)
        gelu_made = Events(sem("gelu_made"), 1)
        glu_done = Events(sem("glu_done"), 1)
        glu_sig = Events(sem("glu_sig"), 1)
        ys_made = Events(sem("ys_made"), 1)
        ys_hi = Events(sem("ys_hi"), 1)
        ys_lo = Events(sem("ys_lo"), 1)
        cz_made = Events(sem("cz_made"), 1)
        yc_made = Events(sem("yc_made"), 1)
        yc_hi = Events(sem("yc_hi"), 1)
        yc_lo = Events(sem("yc_lo"), 1)
        br_read = Events(sem("br_read"), 12)
        sum_made = Events(sem("sum_made"), 4)
        sum_hi = Events(sem("sum_hi"), 4)
        sum_lo = Events(sem("sum_lo"), 4)
        asked = sem("asked")
        dve_chain, pool_chain = sem("dve_chain"), sem("pool_chain")

        def cols(slot):
            return slot[:, :].rearrange("p (c n) -> p c n", c=KC)

        def wide(slot):
            return slot[:, :].rearrange("p (c n) -> p c n", c=2)

        block = ctx.enter_context(nc.Block())

        @block.sync
        def _(sp):
            sp.dma_start(res[:, :, :], x[0].rearrange("(t p) d -> p t d", p=P)).then_inc(x_landed, 16)
            sp.sem_inc(lo_made.sem, SLOTS)
            sp.sem_inc(used.sem, SLOTS)
            for n, v in enumerate((ln1_g, ln1_b, ln2_g, ln2_b, ln3_g, ln3_b)):
                sp.dma_start(ln_rows[16 * n:16 * n + 16, :],
                             v.rearrange("l (c p) -> (l c) p", p=P)).then_inc(small_landed, 16)
            sp.dma_start(dt_rows[:, :], ssm_log_dt.rearrange("l (t g) -> (l t) g", g=2)).then_inc(small_landed, 16)
            for row, v in ((ROW_ARE, ssm_a_re), (ROW_AIM, ssm_a_im)):
                sp.dma_start(small_rows[row:row + 16, :],
                             v.rearrange("l (t g) s -> (l t) (g s)", g=2)).then_inc(small_landed, 16)
            sp.dma_start(small_rows[ROW_CW:ROW_CW + 12, :],
                         conv_w.rearrange("l w (c p) -> (l w c) p", p=P)).then_inc(small_landed, 16)
            for row, v in ((ROW_CB, conv_b), (ROW_D, ssm_d)):
                sp.dma_start(small_rows[row:row + 4, :],
                             v.rearrange("l (c p) -> (l c) p", p=P)).then_inc(small_landed, 16)

            def load(l, k, parts, slot=None):
                slot = k % SLOTS if slot is None else slot
                sp.wait_ge(lo_made.sem, lo_made.at(l, k - SLOTS + 1))
                sp.sem_inc(asked, 1)
                for dst, src in parts(raw[slot]):
                    sp.dma_start(dst, src).then_inc(landed[slot], 16)

            def at_layer(w, l):
                return w[bass.ds(l, 1)].rearrange("a r n -> (a r) n")

            def columns(w, l, c0):
                return lambda r: [(cols(r), at_layer(w, l).rearrange("(c p) n -> p c n", p=P)[:, :, bass.ds(c0, 256)])]

            def rows(w, l, r0):
                return lambda r: [(wide(r), at_layer(w, l)[bass.ds(r0, 256)].rearrange("(c p) n -> p c n", p=P))]

            def load_norm(l, g, b):
                for n, v in enumerate((g, b)):
                    sp.dma_start(gb[:, n, :], v[bass.ds(l, 1)].to_broadcast([P, D])).then_inc(gb_landed.sem, 16)

            def load_ffn(l, f, w_gate, w_up, w_down, middle):
                k0 = FFN0[f]
                load(l, k0, columns(w_gate, l, 0))
                load(l, k0 + 1, columns(w_up, l, 0))
                with sp.Fori(1, STEPS) as i:
                    load(l, k0 + i * 3 - 1, columns(w_gate, l, i * 256), 2)
                    load(l, k0 + i * 3, columns(w_up, l, i * 256), 0)
                    load(l, k0 + i * 3 + 1, rows(w_down, l, i * 256 - 256), 1)
                middle()
                load(l, k0 + FFN_CHUNKS - 1, rows(w_down, l, DFF - 256))

            def q_columns(l, a):
                def parts(r):
                    src = at_layer(w_in, l).rearrange("(c p) n -> p c n", p=P)
                    for m in range(2):
                        for hf in range(2):
                            c0, to = OFF_Q + (4 * hf + 2 * a + m) * HD, (2 * m + hf) * HD
                            yield cols(r)[:, :, to:to + HD], src[:, :, c0:c0 + HD]
                return parts

            def branch_columns(l, j):
                def parts(r):
                    n = slice(256 * j, 256 * j + 256)
                    yield cols(r)[:, 0:2, :], at_layer(w_br_conv, l).rearrange("(c p) n -> p c n", p=P)[:, :, n]
                    yield cols(r)[:, 2:4, :], at_layer(w_br_ssm, l).rearrange("(c p) n -> p c n", p=P)[:, :, n]
                    for hf in range(2):
                        src = at_layer(w_br_attn, l)[hf * 256:hf * 256 + 256]
                        yield cols(r)[hf * HD:hf * HD + HD, 4:8, :], src.rearrange("(m p) n -> p m n", p=HD)[:, :, n]
                return parts

            with sp.Fori(0, DEPTH) as l:
                def params_and_norm1():
                    sp.wait_ge(ax_made.sem, ax_made.at(l, 0))
                    small = layer_landed.sem
                    for n, v in enumerate((ssm_b_re, ssm_b_im)):
                        sp.dma_start(b_in[:, n], v[bass.ds(l, 1)].rearrange(
                            "a (t g) s c -> (a g s) t c", g=2)).then_inc(small, 16)
                    for n, v in enumerate((ssm_c_re, ssm_c_im)):
                        for twice in range(2):
                            sp.dma_start(c_in[:, :, n, twice, :], v[bass.ds(l, 1)].rearrange(
                                "a (u g) c s -> (a g c) u s", u=2)).then_inc(small, 16)
                    sp.dma_start(sinks[:, :], attn_sinks[bass.ds(l, 1)].to_broadcast([P, HEADS])).then_inc(small, 16)
                    load_norm(l, ln1_g, ln1_b)

                params_and_norm1()
                load_ffn(l, 0, ffn1_w_gate, ffn1_w_up, ffn1_w_down, lambda: None)
                for k, c0 in ((KV, OFF_K), (QA, None), (QB, None), (UU, OFF_U), (CC, OFF_C), (HH, OFF_H), (BB, OFF_B)):
                    load(l, MIX0 + k, q_columns(l, k - QA) if c0 is None else columns(w_in, l, c0))
                for g in range(12):
                    load(l, MIX0 + GATE0 + g, columns(w_in, l, OFF_G + 256 * g))
                    if g == 7:
                        sp.wait_ge(yc_made.sem, yc_made.at(l, 1))
                        sp.dma_start(w_glu[:, :, :], at_layer(ssm_w_glu, l).rearrange(
                            "(c p) n -> p c n", p=P)).then_inc(glu_landed.sem, 16)
                for k in range(PROJ_CHUNKS, MIX_CHUNKS):
                    if k in BRANCH:
                        load(l, MIX0 + k, branch_columns(l, BRANCH.index(k)))
                    else:
                        load(l, MIX0 + k, rows(w_out, l, 256 * OUT.index(k)))
                sp.wait_ge(sum_made.sem, sum_made.at(l, 4))
                load_norm(l, ln2_g, ln2_b)

                def norm3():
                    sp.wait_ge(ax_made.sem, ax_made.at(l, 2 * NT))
                    load_norm(l, ln3_g, ln3_b)
                load_ffn(l, 1, ffn2_w_gate, ffn2_w_up, ffn2_w_down, norm3)

            sp.wait_ge(ax_made.sem, ax_made.at(DEPTH - 1, 3 * NT))
            sp.dma_start(out[0].rearrange("(t p) d -> p t d", p=P), res[:, :, :]).then_inc(out_stored, 16)
            sp.wait_ge(out_stored, 16)

        @block.tensor
        def _(pe):
            mm = nc.tensor.matmul

            def take(l, k):
                pe.wait_ge(lo_made.sem, lo_made.at(l, k + 1))

            def project(slot, bank, done=None):
                h, w = cols(w_hi[slot]), cols(w_lo[slot])
                for m in range(2):
                    o = ps[:, bank, m * SEQ:m * SEQ + SEQ]
                    for c in range(KC):
                        n = slice(m * P, m * P + P)
                        mm(o, h[:, c, n], xT[:, c, 0, :], start=c == 0, stop=False)
                        mm(o, h[:, c, n], xT[:, c, 1, :], start=False, stop=False)
                        last = mm(o, w[:, c, n], xT[:, c, 0, :], start=False, stop=c == KC - 1)
                last.then_inc(used.sem, 1)

            def accumulate(slot, buf, start=False, stop=False, tiles=range(NT)):
                h, w = wide(w_hi[slot]), wide(w_lo[slot])
                for c in range(2):
                    for t in range(NT):
                        tok = slice(t * P, t * P + P)
                        for left, right, first in ((rows_hi, h, True), (rows_hi, w, False), (rows_lo, h, False)):
                            for n in range(2):
                                last = mm(acc[:, t, n, :], left[:, buf, c, tok], right[:, c, n * 512:n * 512 + 512],
                                          start=start and first and c == 0, stop=stop and left is rows_lo and c == 1,
                                          skip_group_check=True)
                last.then_inc(used.sem, 1)

            def transposes(l, norm, t, src):
                b = 6 - 2 * t
                for c in range(KC):
                    last = nc.tensor.transpose(ps[:, b + c // 4, (c % 4) * P:(c % 4) * P + P],
                                               src[:, t, c * P:c * P + P], ident[:, :])
                last.then_inc(tp_made.sem, 1)

            def open_acc(l, n):
                pe.wait_ge(res_made.sem, res_made.at(l, n))
                for t in range(NT):
                    for h in range(2):
                        mm(acc[:, t, h, :], zero_b[:, 0:P], zero_b[:, :], start=True, stop=False,
                           skip_group_check=True)

            def ffn(l, f, norm):
                k0, s0 = FFN0[f], f * STEPS
                take(l, k0)
                pe.wait_ge(x_lo.sem, x_lo.at(l, norm * NT))
                project(0, 4)
                take(l, k0 + 1)
                project(1, 5)
                with pe.Fori(1, STEPS) as i:
                    take(l, k0 + i * 3 - 1)
                    pe.wait_ge(silu_made.sem, silu_made.at(l, s0 + i))
                    project(2, 4)
                    take(l, k0 + i * 3)
                    pe.wait_ge(h_made.sem, h_made.at(l, s0 + i))
                    project(0, 5)
                    take(l, k0 + i * 3 + 1)
                    pe.wait_ge(h_lo.sem, h_lo.at(l, s0 + i))
                    accumulate(1, 0)
                take(l, k0 + FFN_CHUNKS - 1)
                pe.wait_ge(h_lo.sem, h_lo.at(l, s0 + STEPS))
                accumulate(2, 0, stop=True)

            def norm_transposes(l, norm):
                for t in range(NT):
                    pe.wait_ge(xn_made.sem, xn_made.at(l, norm * NT + t + 1))
                    transposes(l, norm, t, res)

            pe.wait_ge(x_landed, 16)
            pe.wait_ge(consts_made, 1)
            for t in range(NT):
                transposes(0, 0, t, res)
            pe.wait_ge(rows_made, 1)
            pe.wait_ge(small_landed, 16 * 12)
            nc.tensor.transpose(ps[:, 0, 0:N_LN], ln_rows, ident[0:N_LN, 0:N_LN])
            nc.tensor.transpose(ps[:, 0, P:P + N_SMALL], small_rows, ident[0:N_SMALL, 0:N_SMALL]).then_inc(pro_tp, 1)
            pe.wait_ge(pro_small, 1)
            for t in range(NT):
                for h in range(2):
                    mm(acc[:, t, h, :], zero_b[:, 0:P], zero_b[:, :], start=True, stop=False, skip_group_check=True)

            with pe.Fori(0, DEPTH) as l:
                ffn(l, 0, 0)
                norm_transposes(l, 0)
                def chunk(k):
                    take(l, MIX0 + k)
                    if k >= 2:
                        pe.wait_ge(proj_read.sem, proj_read.at(l, k - 1))
                    if k != KV:
                        project((MIX0 + k) % SLOTS, 4 + k % 2)

                def project_kv(slot, bank):
                    h, w = cols(w_hi[slot]), cols(w_lo[slot])
                    o = ps[:, bank, 0:SEQ]
                    for c in range(KC):
                        mm(o, h[:, c, 0:P], xT[:, c, 0, :], start=c == 0, stop=False)
                        mm(o, h[:, c, 0:P], xT[:, c, 1, :], start=False, stop=False)
                        mm(o, w[:, c, 0:P], xT[:, c, 0, :], start=False, stop=c == KC - 1)
                    for t in range(NT):
                        o = ps[:, bank, SEQ + t * P:SEQ + t * P + P]
                        tok = slice(t * P, t * P + P)
                        for c in range(KC):
                            mm(o, xT[:, c, 0, tok], h[:, c, P:2 * P], start=c == 0, stop=False)
                            mm(o, xT[:, c, 0, tok], w[:, c, P:2 * P], start=False, stop=False)
                            last = mm(o, xT[:, c, 1, tok], h[:, c, P:2 * P], start=False, stop=c == KC - 1)
                    last.then_inc(used.sem, 1)

                def input_states(q):
                    if q >= 1:
                        pe.wait_ge(bu_made.sem, bu_made.at(l, q))
                    for t in range(2 * q, 2 * q + 2):
                        for ri in range(2):
                            last = mm(ps[:, t % 2, ri * SEQ:ri * SEQ + SEQ], bTz[:, t, ri, :], uT[:, t // 4, :],
                                      start=True, stop=True)
                    last.then_inc(bu_done.sem, 1)

                def output_states(q):
                    pe.wait_ge(xre_made.sem, xre_made.at(l, q + 1))
                    pe.wait_ge(xim_made.sem, xim_made.at(l, q + 1))
                    ct = q // 2
                    for t in range(2 * q, 2 * q + 2):
                        for ri in range(2):
                            last = mm(ps[:, 2, ct * SEQ:ct * SEQ + SEQ], cTz[:, t, ri, :], sw[:, ri, t % 2, :],
                                      start=t % 4 == 0 and ri == 0, stop=t % 4 == 3 and ri == 1)
                    last.then_inc(c_done.sem, 1)

                def transpose_probs(S, parts, g0, first):
                    for g in range(parts):
                        if g0 + g >= 2:
                            pe.wait_ge(pT_made.sem, pT_made.at(l, g0 + g - 1))
                        b = 6 + (g0 + g) % 2
                        for n in range(4):
                            i = 4 * g + n
                            src = S[:, i // 2, (i % 2) * P:(i % 2) * P + P] if parts == 4 else S[:, i, :]
                            last = nc.tensor.transpose(ps[:, b, n * P:n * P + P], src, ident[:, :])
                        last.then_inc(pT_done.sem, 1)

                def attend(blk):
                    pe.wait_ge(pT_made.sem, pT_made.at(l, 4 if blk else 6))
                    for m in range(4):
                        terms = [(j, kb) for j in range(2) for kb in range(blk + 1)]
                        for n, (j, kb) in enumerate(terms):
                            head = m + 4 * j
                            i = 2 * head + kb if blk else head
                            last = mm(ps[:, 3, m * P:m * P + P], vz[:, kb, j, :], probsT[:, i, :],
                                      start=n == 0, stop=n == len(terms) - 1)
                    last.then_inc(pv_done.sem, 1)

                pe.wait_ge(x_lo.sem, x_lo.at(l, NT))
                chunk(KV)
                project_kv((MIX0 + KV) % SLOTS, 4)
                pe.wait_ge(bblk_made.sem, bblk_made.at(l, 1))
                pe.wait_ge(layer_landed.sem, layer_landed.at(l, 7))
                for u in range(2):
                    for ri in range(2):
                        n = (2 * u + ri) * P
                        nc.tensor.transpose(ps[:, 0, n:n + P], b_blk[:, ri, 4 * u:4 * u + 4, :], ident[:, :])
                        last = nc.tensor.transpose(ps[:, 1, n:n + P], c_in[:, u, ri, :, :], ident[:, :])
                last.then_inc(bcT_done.sem, 1)
                chunk(QA)
                chunk(QB)
                chunk(UU)
                pe.wait_ge(proj_read.sem, proj_read.at(l, QB + 1))
                pe.wait_ge(bcT_made.sem, bcT_made.at(l, 1))
                for head in range(HEADS):
                    last = mm(ps[:, head // 2, (head % 2) * SEQ:(head % 2) * SEQ + SEQ],
                              qT[:, head % 4, P:2 * P], kz[:, head // 4, :], start=True, stop=True)
                last.then_inc(scores_done.sem, 1)
                for head in range(HEADS):
                    last = mm(ps[:, 6 + head // 4, (head % 4) * P:(head % 4) * P + P],
                              qT[:, head % 4, 0:P], kz[:, head // 4, 0:P], start=True, stop=True)
                last.then_inc(scores_done.sem, 1)
                chunk(CC)
                chunk(HH)
                pe.wait_ge(s_made.sem, s_made.at(l, 2))
                input_states(0)
                chunk(BB)
                chunk(7)
                input_states(1)
                chunk(8)
                output_states(0)
                chunk(9)
                input_states(2)
                pe.wait_ge(probs_made.sem, probs_made.at(l, 1))
                transpose_probs(S1, 4, 0, 0)
                chunk(10)
                output_states(1)
                attend(1)
                chunk(11)
                input_states(3)
                pe.wait_ge(probs_made.sem, probs_made.at(l, 2))
                transpose_probs(S0, 2, 4, 16)
                chunk(12)
                output_states(2)
                pe.wait_ge(ya_lo.sem, ya_lo.at(l, 1))
                attend(0)
                chunk(13)
                chunk(14)
                output_states(3)
                chunk(15)
                pe.wait_ge(gelu_made.sem, gelu_made.at(l, 1))
                pe.wait_ge(glu_landed.sem, glu_landed.at(l, 1))
                for co in range(2):
                    for c in range(2):
                        last = mm(ps[:, 0, co * SEQ:co * SEQ + SEQ], w_glu[:, c, co * P:co * P + P], sw[:, 0, c, :],
                                  start=c == 0, stop=c == 1)
                last.then_inc(glu_done.sem, 1)
                chunk(16)
                chunk(17)
                chunk(18)

                def branch(j):
                    k = MIX0 + BRANCH[j]
                    take(l, k)
                    h, w = cols(w_hi[k % SLOTS]), cols(w_lo[k % SLOTS])
                    for b, (y, kc, yc) in enumerate(((y_cs, (0, 1), 0), (y_cs, (2, 3), 0), (y_attn, (4, 5, 6, 7), 4))):
                        if j == 0:
                            pe.wait_ge((yc_lo, ys_lo, ya_lo)[b].sem, (yc_lo, ys_lo, ya_lo)[b].at(l, 2 if b == 2 else 1))
                        else:
                            pe.wait_ge(br_read.sem, br_read.at(l, 3 * (j - 1) + b + 1))
                        for m in range(2):
                            o = ps[:, 4 + b, m * SEQ:m * SEQ + SEQ]
                            n = slice(m * P, m * P + P)
                            for c in kc:
                                mm(o, h[:, c, n], y[:, c - yc, 0, :], start=c == kc[0], stop=False)
                                mm(o, h[:, c, n], y[:, c - yc, 1, :], start=False, stop=False)
                                last = mm(o, w[:, c, n], y[:, c - yc, 0, :], start=False, stop=c == kc[-1])
                    last.then_inc(used.sem, 1)

                def output(j):
                    k = MIX0 + OUT[j]
                    take(l, k)
                    pe.wait_ge(sum_lo.sem, sum_lo.at(l, j + 1))
                    accumulate(k % SLOTS, j % 2, start=j == 0, stop=j == 3)

                pe.wait_ge(proj_read.sem, proj_read.at(l, PROJ_CHUNKS))
                branch(0)
                branch(1)
                output(0)
                branch(2)
                output(1)
                branch(3)
                output(2)
                output(3)
                norm_transposes(l, 1)
                open_acc(l, 2 * NT)
                ffn(l, 1, 2)
                norm_transposes(l, 2)
                open_acc(l, 3 * NT)

        @block.scalar
        def _(sc_):
            act_ = nc.scalar.activation

            def split(l, k, slot=None, land=None):
                s = k % SLOTS if slot is None else slot
                n = LANDED[k] if land is None else land
                sc_.wait_ge(landed[s], l * LANDED_LAYER[s] + n)
                sc_.wait_ge(used.sem, used.at(l, k - SLOTS + 1))
                nc.scalar.copy(w_hi[s][:, :], raw[s][:, :]).then_inc(hi_made.sem, 1)

            def silu(l, n, k):
                sc_.wait_ge(used.sem, used.at(l, k + 1))
                act_(act[:, :, :], ps[:, 4, :].rearrange("p (m t) -> p m t", m=2), ACT.Silu).then_inc(silu_made.sem, 1)

            def hidden_hi(l, n, k):
                sc_.wait_ge(h_made.sem, h_made.at(l, n))
                sc_.wait_ge(used.sem, used.at(l, k + 1))
                nc.scalar.copy(rows_hi[:, 0], hid[:, :, :]).then_inc(h_hi.sem, 1)

            def ffn(l, f, ahead):
                k0, s0 = FFN0[f], f * STEPS
                if not ahead:
                    split(l, k0)
                    split(l, k0 + 1)
                split(l, k0 + 2)
                if not f:
                    sc_.wait_ge(bblk_made.sem, bblk_made.at(l, 1))
                silu(l, 1, k0)
                split(l, k0 + 3)

                def step(i, last):
                    hidden_hi(l, s0 + i, k0 + i * 3 - 2)
                    split(l, k0 + i * 3 + 1, 1, LANDED[k0 + 1] + i * 16)
                    silu(l, i + 1, k0 + i * 3 - 1)
                    split(l, k0 + i * 3 + 2, 2, LANDED[k0 + 2] + i * 16)
                    if not last:
                        split(l, k0 + i * 3 + 3, 0, LANDED[k0] + i * 16 + 16)

                with sc_.Fori(1, STEPS - 1) as i:
                    step(i, False)
                step(STEPS - 1, True)
                hidden_hi(l, s0 + STEPS, k0 + FFN_CHUNKS - 2)

            def x_split(l, n, t):
                sc_.wait_ge(xTf_dve.sem, xTf_dve.at(l, n))
                sc_.wait_ge(xTf_act.sem, xTf_act.at(l, n))
                tok = slice(t * P, t * P + P)
                nc.scalar.copy(xT[:, :, 0, tok], xTf[:, :, tok]).then_inc(x_hi.sem, 1)

            def norm(l, n0, norm_):
                for t in range(NT):
                    n = norm_ * NT + t + 1
                    sc_.wait_ge(tp_made.sem, tp_made.at(l, n))
                    for c in range(4, KC):
                        last = act_(xTf[:, c, t * P:t * P + P], ps[:, 7 - 2 * t, (c - 4) * P:(c - 3) * P], ACT.Identity,
                                    scale=ln_cur[:, 2 * norm_, c:c + 1], bias=ln_cur[:, 2 * norm_ + 1, c:c + 1])
                    last.then_inc(xTf_act.sem, 1)
                    x_split(l, n, t)

            for t in range(NT):
                sc_.wait_ge(tp_made.sem, tp_made.at(0, t + 1 - NT))
                nc.scalar.copy(xTf[:, 4:KC, t * P:t * P + P],
                               ps[:, 7 - 2 * t, :].rearrange("p (c n) -> p c n", c=4)).then_inc(xTf_act.sem, 1)
                x_split(0, t + 1 - NT, t)
            sc_.wait_ge(pro_small, 1)
            act_(sc[:, 0, :], smallT[:, ROW_DT:ROW_DT + 16], ACT.Exp).then_inc(state_act, 1)
            sc_.wait_ge(state_dve, 1)
            act_(stat[:, 0].rearrange("p l t -> p (l t)"), sc[:, 1, :], ACT.Exp).then_inc(state_act, 1)
            sc_.wait_ge(state_dve, 2)
            act_(stat[:, 2].rearrange("p l t -> p (l t)"), sc[:, 2, :], ACT.Sin).then_inc(state_act, 1)
            act_(sc[:, 3, :], sc[:, 2, :], ACT.Sin, scale=0.5).then_inc(state_act, 1)

            with sc_.Fori(0, DEPTH) as l:
                ffn(l, 0, False)
                split(l, MIX0)
                split(l, MIX0 + 1)
                norm(l, 0, 0)
                def bank(k):
                    return ps[:, 4 + k % 2, :]

                def read(k, dst):
                    sc_.wait_ge(used.sem, used.at(l, MIX0 + k + 1))
                    nc.scalar.copy(dst, bank(k).rearrange("p (m t) -> p m t", m=2)).then_inc(proj_read.sem, 1)

                def gate(k):
                    sc_.wait_ge(used.sem, used.at(l, MIX0 + k + 1))
                    g = k - GATE0
                    act_(gates[:, g // 4, 2 * (g % 4):2 * (g % 4) + 2, :], bank(k).rearrange("p (m t) -> p m t", m=2),
                         ACT.Sigmoid).then_inc(proj_read.sem, 1)

                def states(q):
                    sc_.wait_ge(bu_done.sem, bu_done.at(l, q + 1))
                    if q:
                        sc_.wait_ge(xre_made.sem, xre_made.at(l, q))
                        sc_.wait_ge(xim_made.sem, xim_made.at(l, q))
                    nc.scalar.copy(bu[:, :, :, :], ps[:, 0:2, :].rearrange("p b (r t) -> p b r t", r=2)
                                   ).then_inc(bu_made.sem, 1)

                def probs_out(g0, n):
                    for g in range(g0, g0 + n):
                        sc_.wait_ge(pT_done.sem, pT_done.at(l, g + 1))
                        i = 4 * (g - g0)
                        nc.scalar.copy(probsT[:, i:i + 4, :], ps[:, 6 + g % 2, :].rearrange("p (c n) -> p c n", c=4)
                                       ).then_inc(pT_made.sem, 1)

                def attn_hi(n, blk):
                    sc_.wait_ge(pv_done.sem, pv_done.at(l, n))
                    nc.scalar.copy(y_attn[:, :, 0, blk * P:blk * P + P], ps[:, 3, :].rearrange("p (m q) -> p m q", m=4)
                                   ).then_inc(ya_hi.sem, 1)

                split(l, MIX0 + 2)
                sc_.wait_ge(used.sem, used.at(l, MIX0 + KV + 1))
                nc.scalar.copy(kz[0:HD, 0, :], ps[0:HD, 4, 0:SEQ])
                nc.scalar.copy(kz[HD:P, 1, :], ps[HD:P, 4, 0:SEQ])
                v = ps[:, 4, SEQ:2 * SEQ].rearrange("p (b n) -> p b n", b=2)
                nc.scalar.copy(vz[:, :, 0, 0:HD], v[:, :, 0:HD])
                nc.scalar.copy(vz[:, :, 1, HD:P], v[:, :, HD:P]).then_inc(proj_read.sem, 1)
                split(l, MIX0 + 3)
                sc_.wait_ge(bcT_done.sem, bcT_done.at(l, 1))
                b_ps = ps[:, 0, :].rearrange("p (u r s) -> p u r s", u=2, r=2)
                c_ps = ps[:, 1, :].rearrange("p (u r q h c) -> p u r q h c", u=2, r=2, q=4, h=2)
                for q in range(4):
                    rows_ = slice(32 * q, 32 * q + 32)
                    nc.scalar.copy(bTz[rows_, q::4, :, :], b_ps[rows_])
                for u in range(2):
                    for q in range(4):
                        for h in range(2):
                            half, n = slice(HD * h, HD * h + HD), 32 * q + 16 * h
                            nc.scalar.copy(cTz[half, 4 * u + q, 0, n:n + 16], c_ps[half, u, 0, q, h, :])
                            last = nc.scalar.mul(cTz[half, 4 * u + q, 1, n:n + 16], c_ps[half, u, 1, q, h, :], -1.0)
                last.then_inc(bcT_made.sem, 1)
                read(QA, qT[:, 0:2, :])
                split(l, MIX0 + 4)
                read(QB, qT[:, 2:4, :])
                split(l, MIX0 + 5)
                read(UU, uT[:, :, :])
                split(l, MIX0 + 6)
                read(CC, cv_c[:, :, :])
                split(l, MIX0 + 7)
                sc_.wait_ge(negm_made.sem, negm_made.at(l, 1))
                for blk, S in ((1, S1), (0, S0)):
                    for head in range(HEADS):
                        act_(S[:, head, :], S[:, head, :], ACT.Exp, bias=negm[:, blk, head:head + 1],
                             accum_out=psum_p[:, blk, head:head + 1])
                    if blk:
                        read(HH, cv_h[:, :, :])
                        split(l, MIX0 + 8)
                        states(0)
                act_(esink[:, :, :], esink[:, :, :], ACT.Exp).then_inc(exp_made.sem, 1)
                sc_.wait_ge(ax_made.sem, ax_made.at(l, NT))
                read(BB, cv_b[:, :, :])
                split(l, MIX0 + 9)
                gate(7)
                split(l, MIX0 + 10)
                states(1)
                gate(8)
                split(l, MIX0 + 11)
                gate(9)
                split(l, MIX0 + 12)
                probs_out(0, 4)
                states(2)
                gate(10)
                split(l, MIX0 + 13)
                attn_hi(1, 1)
                gate(11)
                split(l, MIX0 + 14)
                probs_out(4, 2)
                gate(12)
                split(l, MIX0 + 15)
                states(3)
                attn_hi(2, 0)
                gate(13)
                split(l, MIX0 + 16)
                sc_.wait_ge(yc_made.sem, yc_made.at(l, 1))
                nc.scalar.copy(y_cs[:, 0:2, 0, :], cv_h[:, :, :]).then_inc(yc_hi.sem, 1)
                gate(14)
                split(l, MIX0 + 17)
                sc_.wait_ge(yd_made.sem, yd_made.at(l, 1))
                act_(sw[:, 0], td[:, 0], ACT.Gelu_apprx_tanh).then_inc(gelu_made.sem, 1)
                gate(15)
                split(l, MIX0 + 18)
                sc_.wait_ge(glu_done.sem, glu_done.at(l, 1))
                act_(td[:, 0], ps[:, 0, :].rearrange("p (m t) -> p m t", m=2), ACT.Sigmoid).then_inc(glu_sig.sem, 1)
                gate(16)
                split(l, MIX0 + 19)
                sc_.wait_ge(ys_made.sem, ys_made.at(l, 1))
                nc.scalar.copy(y_cs[:, 2:4, 0, :], td[:, 1]).then_inc(ys_hi.sem, 1)
                gate(17)
                split(l, MIX0 + 20)
                gate(18)
                split(l, MIX0 + 21)

                def sum_hi_(j):
                    sc_.wait_ge(sum_made.sem, sum_made.at(l, j + 1))
                    if j >= 2:
                        sc_.wait_ge(used.sem, used.at(l, MIX0 + OUT[j - 2] + 1))
                    nc.scalar.copy(rows_hi[:, j % 2], hid[:, :, :]).then_inc(sum_hi.sem, 1)
                split(l, MIX0 + 22)
                sum_hi_(0)
                split(l, MIX0 + 23)
                sum_hi_(1)
                split(l, MIX0 + 24)
                split(l, MIX0 + 25)
                sum_hi_(2)
                split(l, MIX0 + 26)
                split(l, FFN0[1])
                sum_hi_(3)
                split(l, FFN0[1] + 1)
                norm(l, 0, 1)
                ffn(l, 1, True)
                norm(l, 0, 2)

        @block.gpsimd
        def _(pool):
            links = Chain(POOL_LINKS)
            tt, memset = nc.gpsimd.tensor_tensor, nc.gpsimd.memset

            for tile in (ident[:, :], mask[:, :], zero_b[:, :], kz[:, :, :], vz[:, :, :, :],
                         cTz[:, :, :, :], cv_z[:, :, :]):
                memset(tile, 0.0).then_inc(pool_chain, 1)
                pool.wait_ge(pool_chain, links.next())
            memset(mhalf[:, :], -0.5).then_inc(pool_chain, 1)
            pool.wait_ge(pool_chain, links.next())
            nc.gpsimd.affine_select(out=ident[:, :], in_=ident[:, :], compare_op=ALU.not_equal, fill=1.0,
                                    base=0, pattern=[[-1, P]], channel_multiplier=1).then_inc(pool_chain, 1)
            pool.wait_ge(pool_chain, links.next())
            nc.gpsimd.affine_select(out=mask[:, :], in_=mask[:, :], compare_op=ALU.is_ge, fill=MASKED,
                                    base=-1, pattern=[[1, 2 * P]], channel_multiplier=-1).then_inc(pool_chain, 1)
            pool.wait_ge(pool_chain, links.next())
            nc.gpsimd.affine_select(out=mask[:, :], in_=mask[:, :], compare_op=ALU.is_ge, fill=MASKED,
                                    base=P, pattern=[[-1, 2 * P]], channel_multiplier=1).then_inc(pool_chain, 1)
            pool.wait_ge(pool_chain, links.next())
            pool.sem_inc(consts_made, 1)
            pool.wait_ge(x_landed, 16)
            memset(alpha[:, :], ALPHA).then_inc(pool_chain, 1)
            pool.wait_ge(pool_chain, links.next())
            for t in range(NT):
                nc.gpsimd.tensor_scalar(ax[:, t, :], res[:, t, :], ALPHA, None, ALU.mult).then_inc(ax_made.sem, 1)

            def norm(l, norm_):
                for t in range(NT):
                    pool.wait_ge(var_made.sem, var_made.at(l, norm_ * NT + t + 1))
                    tt(rstd[:, t:t + 1], veps[:, t:t + 1], mhalf[:, :], ALU.pow).then_inc(rstd_made.sem, 1)
                pool.wait_ge(gb_landed.sem, gb_landed.at(l, 2 * norm_ + 2))
                for t in range(NT):
                    pool.wait_ge(tp_made.sem, tp_made.at(l, norm_ * NT + t + 1))
                    tt(res[:, t, :], res[:, t, :], gb[:, 0, :], ALU.mult).then_inc(pool_chain, 1)
                    pool.wait_ge(pool_chain, links.next())
                    tt(res[:, t, :], res[:, t, :], gb[:, 1, :], ALU.add).then_inc(pool_chain, 1)
                    pool.wait_ge(pool_chain, links.next())
                    tt(ax[:, t, :], res[:, t, :], alpha[:, :].to_broadcast([P, D]), ALU.mult).then_inc(ax_made.sem, 1)

            with pool.Fori(0, DEPTH) as l:
                links.enter(l)
                pool.wait_ge(cur_made.sem, cur_made.at(l, 1))
                n = 1
                while n < SEQ:
                    k = min(STATE_TILES, 512 // n)
                    for t in range(0, STATE_TILES, k):
                        tl = slice(t, t + k)
                        c, s = rot_c[:, tl, 0:n], rot_s[:, tl, 0:n]
                        cn = rot_c[:, tl, n - 1:n].to_broadcast([P, k, n])
                        sn = rot_s[:, tl, n - 1:n].to_broadcast([P, k, n])
                        t0, t1 = (tp[:, i].rearrange("p a t -> p (a t)")[:, 0:k * n].rearrange("p (k n) -> p k n", k=k)
                                  for i in range(2))
                        tt(t0, c, cn, ALU.mult).then_inc(pool_chain, 1)
                        pool.wait_ge(pool_chain, links.next())
                        tt(t1, s, sn, ALU.mult).then_inc(pool_chain, 1)
                        pool.wait_ge(pool_chain, links.next())
                        tt(rot_c[:, tl, n:2 * n], t0, t1, ALU.subtract).then_inc(pool_chain, 1)
                        pool.wait_ge(pool_chain, links.next())
                        tt(t0, s, cn, ALU.mult).then_inc(pool_chain, 1)
                        pool.wait_ge(pool_chain, links.next())
                        tt(t1, c, sn, ALU.mult).then_inc(pool_chain, 1)
                        pool.wait_ge(pool_chain, links.next())
                        tt(rot_s[:, tl, n:2 * n], t0, t1, ALU.add).then_inc(pool_chain, 1)
                        pool.wait_ge(pool_chain, links.next())
                    n *= 2
                pool.sem_inc(rot_made.sem, 1)
                norm(l, 0)

                def turn_in(q):
                    tl = slice(2 * q, 2 * q + 2)
                    pool.wait_ge(bu_made.sem, bu_made.at(l, q + 1))
                    tt(tp[:, 0], bu[:, :, 1, :], rot_c[:, tl, :], ALU.mult).then_inc(pool_chain, 1)
                    pool.wait_ge(pool_chain, links.next())
                    tt(tp[:, 1], bu[:, :, 0, :], rot_s[:, tl, :], ALU.mult).then_inc(pool_chain, 1)
                    pool.wait_ge(pool_chain, links.next())
                    if q:
                        pool.wait_ge(c_done.sem, c_done.at(l, q))
                    tt(sw[:, 1], tp[:, 0], tp[:, 1], ALU.subtract).then_inc(wim_made.sem, 1)

                def turn_out(q):
                    tl = slice(2 * q, 2 * q + 2)
                    pool.wait_ge(z_made.sem, z_made.at(l, q + 1))
                    tt(tp[:, 0], bu[:, :, 0, :], rot_s[:, tl, :], ALU.mult).then_inc(pool_chain, 1)
                    pool.wait_ge(pool_chain, links.next())
                    tt(tp[:, 1], bu[:, :, 1, :], rot_c[:, tl, :], ALU.mult).then_inc(pool_chain, 1)
                    pool.wait_ge(pool_chain, links.next())
                    tt(sw[:, 1], tp[:, 0], tp[:, 1], ALU.add).then_inc(xim_made.sem, 1)

                def normalise(S, blk, n):
                    tt(S[:, :, :], S[:, :, :], rden[:, blk, :].rearrange("p (h o) -> p h o", o=1)
                       .to_broadcast([P, HEADS, n]), ALU.mult).then_inc(probs_made.sem, 1)

                pool.wait_ge(proj_read.sem, proj_read.at(l, HH + 1))
                tt(cv_z[:, :, 2:SEQ + 2], cv_c[:, :, :], cv_h[:, :, :], ALU.mult).then_inc(cz_made.sem, 1)
                turn_in(0)
                turn_out(0)
                pool.wait_ge(rden_made.sem, rden_made.at(l, 1))
                normalise(S1, 1, 2 * P)
                turn_in(1)
                normalise(S0, 0, P)
                turn_out(1)
                for q in (2, 3):
                    turn_in(q)
                    turn_out(q)
                norm(l, 1)
                norm(l, 2)
                links.leave()

        @block.vector
        def _(dve):
            links = Chain(DVE_LINKS)
            tt, ts, stt = nc.vector.tensor_tensor, nc.vector.tensor_scalar, nc.vector.scalar_tensor_tensor
            copy = nc.vector.tensor_copy

            def f32(t):
                return t.bitcast(F32)

            def rest(l, k, slot=None):
                s = k % SLOTS if slot is None else slot
                dve.wait_ge(hi_made.sem, hi_made.at(l, k + 1))
                tt(w_lo[s][:, :], raw[s][:, :], f32(w_hi[s][:, :]), ALU.subtract).then_inc(lo_made.sem, 1)

            def hidden(l, n, k, waits=True):
                dve.wait_ge(used.sem, used.at(l, k + 1))
                if waits:
                    dve.wait_ge(h_lo.sem, h_lo.at(l, n - 1))
                dve.wait_ge(silu_made.sem, silu_made.at(l, n))
                tt(hid[:, :, :], act[:, :, :], ps[:, 5, :].rearrange("p (m t) -> p m t", m=2), ALU.mult
                   ).then_inc(h_made.sem, 1)

            def hidden_lo(l, n):
                dve.wait_ge(h_hi.sem, h_hi.at(l, n))
                tt(rows_lo[:, 0], hid[:, :, :], f32(rows_hi[:, 0]), ALU.subtract).then_inc(h_lo.sem, 1)

            def ffn(l, f, ahead):
                k0, s0 = FFN0[f], f * STEPS
                if not ahead:
                    rest(l, k0)
                    rest(l, k0 + 1)
                rest(l, k0 + 2)
                rest(l, k0 + 3)
                hidden(l, s0 + 1, k0 + 1, False)

                def step(i, last):
                    hidden_lo(l, s0 + i)
                    rest(l, k0 + i * 3 + 1, 1)
                    rest(l, k0 + i * 3 + 2, 2)
                    hidden(l, s0 + 1 + i, k0 + i * 3)
                    if not last:
                        rest(l, k0 + i * 3 + 3, 0)

                with dve.Fori(1, STEPS - 1) as i:
                    step(i, False)
                step(STEPS - 1, True)
                hidden_lo(l, s0 + STEPS)

            def x_rest(l, n, t):
                dve.wait_ge(x_hi.sem, x_hi.at(l, n))
                tok = slice(t * P, t * P + P)
                tt(xT[:, :, 1, tok], xTf[:, :, tok], f32(xT[:, :, 0, tok]), ALU.subtract).then_inc(x_lo.sem, 1)

            def norm(l, norm_, k, scale):
                dve.wait_ge(used.sem, used.at(l, k + 1))

                def residual(t):
                    dve.wait_ge(ax_made.sem, ax_made.at(l, norm_ * NT + t + 1 - NT))
                    stt(res[:, t, :], ps[:, 2 * t:2 * t + 2, :].rearrange("p b n -> p (b n)"), scale, ax[:, t, :],
                        ALU.mult, ALU.add).then_inc(res_made.sem, 1)

                def statistics(t):
                    dve.wait_ge(res_made.sem, res_made.at(l, norm_ * NT + t + 1))
                    for h in range(2):
                        last = nc.vector.bn_stats(bnst[:, t, h, :], res[:, t, h * 512:h * 512 + 512])
                    last.then_inc(dve_chain, 1)
                    dve.wait_ge(dve_chain, links.next())

                def variance(t):
                    ts(veps[:, t:t + 1], mv[:, t, 1:2], EPS, None, ALU.add).then_inc(var_made.sem, 1)

                residual(0)
                statistics(0)
                residual(1)
                nc.vector.bn_aggr(mv[:, 0, :], bnst[:, 0, :, :]).then_inc(dve_chain, 1)
                dve.wait_ge(dve_chain, links.next())
                statistics(1)
                variance(0)
                nc.vector.bn_aggr(mv[:, 1, :], bnst[:, 1, :, :]).then_inc(dve_chain, 1)
                dve.wait_ge(dve_chain, links.next())
                variance(1)
                for t in range(NT):
                    dve.wait_ge(rstd_made.sem, rstd_made.at(l, norm_ * NT + t + 1))
                    ts(res[:, t, :], res[:, t, :], mv[:, t, 0:1], rstd[:, t:t + 1], ALU.subtract, ALU.mult
                       ).then_inc(xn_made.sem, 1)
                for t in range(NT):
                    n = norm_ * NT + t + 1
                    dve.wait_ge(tp_made.sem, tp_made.at(l, n))
                    for c in range(4):
                        last = ts(xTf[:, c, t * P:t * P + P], ps[:, 6 - 2 * t, c * P:c * P + P],
                                  ln_cur[:, 2 * norm_, c:c + 1], ln_cur[:, 2 * norm_ + 1, c:c + 1], ALU.mult, ALU.add)
                    last.then_inc(xTf_dve.sem, 1)
                    x_rest(l, n, t)

            dve.wait_ge(small_landed, 16 * 12)
            for g in range(2):
                last = copy(small_rows[ROW_DT:ROW_DT + 16, g * HD:g * HD + HD], dt_rows[:, g:g + 1].to_broadcast([16, HD]))
            last.then_inc(rows_made, 1)
            for t in range(NT):
                dve.wait_ge(tp_made.sem, tp_made.at(0, t + 1 - NT))
                copy(xTf[:, 0:4, t * P:t * P + P], ps[:, 6 - 2 * t, :].rearrange("p (c n) -> p c n", c=4)
                     ).then_inc(xTf_dve.sem, 1)
                x_rest(0, t + 1 - NT, t)
            dve.wait_ge(pro_tp, 1)
            copy(lnT[:, :, :, :].rearrange("p n l c -> p (n l c)"), ps[:, 0, 0:N_LN])
            copy(smallT[:, :], ps[:, 0, P:P + N_SMALL]).then_inc(pro_small, 1)
            dve.wait_ge(pro_small, 1)
            lr, li = smallT[:, ROW_ARE:ROW_ARE + 16], smallT[:, ROW_AIM:ROW_AIM + 16]
            mag, cos, sin, coef_r, coef_i = (stat[:, n].rearrange("p l t -> p (l t)") for n in range(5))
            dve.wait_ge(state_act, 1)
            tt(sc[:, 1, :], lr, sc[:, 0, :], ALU.mult).then_inc(state_dve, 1)
            tt(sc[:, 4, :], li, sc[:, 0, :], ALU.mult).then_inc(dve_chain, 1)
            dve.wait_ge(dve_chain, links.next())
            ts(sc[:, 5, :], sc[:, 4, :], 1.0 / (2 * 3.141592653589793), ROUND, ALU.mult, ALU.add).then_inc(dve_chain, 1)
            dve.wait_ge(dve_chain, links.next())
            ts(sc[:, 5, :], sc[:, 5, :], ROUND, None, ALU.subtract).then_inc(dve_chain, 1)
            dve.wait_ge(dve_chain, links.next())
            for part in (TWO_PI_A, TWO_PI_B, TWO_PI_C):
                stt(sc[:, 4, :], sc[:, 5, :], -part, sc[:, 4, :], ALU.mult, ALU.add).then_inc(dve_chain, 1)
                dve.wait_ge(dve_chain, links.next())
            ts(sc[:, 2, :], sc[:, 4, :], 3.1415925, -3.1415925, ALU.min, ALU.max).then_inc(state_dve, 1)
            dve.wait_ge(state_act, 4)
            tt(sc[:, 5, :], sc[:, 3, :], sc[:, 3, :], ALU.mult).then_inc(dve_chain, 1)
            dve.wait_ge(dve_chain, links.next())
            ts(cos, sc[:, 5, :], -2.0, 1.0, ALU.mult, ALU.add).then_inc(dve_chain, 1)
            dve.wait_ge(dve_chain, links.next())
            tt(sc[:, 5, :], mag, cos, ALU.mult).then_inc(dve_chain, 1)
            dve.wait_ge(dve_chain, links.next())
            ts(sc[:, 5, :], sc[:, 5, :], 1.0, None, ALU.subtract).then_inc(dve_chain, 1)
            dve.wait_ge(dve_chain, links.next())
            tt(sc[:, 6, :], mag, sin, ALU.mult).then_inc(dve_chain, 1)
            dve.wait_ge(dve_chain, links.next())
            tt(sc[:, 0, :], lr, lr, ALU.mult).then_inc(dve_chain, 1)
            dve.wait_ge(dve_chain, links.next())
            tt(sc[:, 1, :], li, li, ALU.mult).then_inc(dve_chain, 1)
            dve.wait_ge(dve_chain, links.next())
            tt(sc[:, 0, :], sc[:, 0, :], sc[:, 1, :], ALU.add).then_inc(dve_chain, 1)
            dve.wait_ge(dve_chain, links.next())
            nc.vector.reciprocal(sc[:, 7, :], sc[:, 0, :]).then_inc(dve_chain, 1)
            dve.wait_ge(dve_chain, links.next())
            for o, a, b, op in ((coef_r, 5, 6, ALU.add), (coef_i, 6, 5, ALU.subtract)):
                tt(sc[:, 0, :], sc[:, a, :], lr, ALU.mult).then_inc(dve_chain, 1)
                dve.wait_ge(dve_chain, links.next())
                tt(sc[:, 1, :], sc[:, b, :], li, ALU.mult).then_inc(dve_chain, 1)
                dve.wait_ge(dve_chain, links.next())
                tt(sc[:, 0, :], sc[:, 0, :], sc[:, 1, :], op).then_inc(dve_chain, 1)
                dve.wait_ge(dve_chain, links.next())
                tt(o, sc[:, 0, :], sc[:, 7, :], ALU.mult).then_inc(dve_chain, 1)
                dve.wait_ge(dve_chain, links.next())

            with dve.Fori(0, DEPTH) as l:
                links.enter(l)
                copy(ln_cur[:, :, :], lnT[:, :, bass.ds(l, 1), :].rearrange("p n a c -> p n (a c)"))
                copy(cw_cur[:, :, :].rearrange("p w c -> p (w c)"), smallT[:, bass.ds(l * 6 + ROW_CW, 6)])
                copy(cb_cur[:, :], smallT[:, bass.ds(l * 2 + ROW_CB, 2)])
                copy(d_cur[:, :], smallT[:, bass.ds(l * 2 + ROW_D, 2)])
                copy(st_cur[:, :, :], stat[:, :, bass.ds(l, 1), :].rearrange("p n a t -> p n (a t)")).then_inc(dve_chain, 1)
                dve.wait_ge(dve_chain, links.next())
                copy(rot_c[:, :, 0], st_cur[:, 1, :])
                copy(rot_s[:, :, 0], st_cur[:, 2, :]).then_inc(cur_made.sem, 1)
                nc.vector.memset(b_blk[:, :, :, :], 0.0)
                nc.vector.memset(bTz[:, :, :, :], 0.0).then_inc(zeros_made.sem, 1)
                rest(l, 0)
                rest(l, 1)
                dve.wait_ge(cur_made.sem, cur_made.at(l, 1))
                dve.wait_ge(layer_landed.sem, layer_landed.at(l, 7))
                dve.wait_ge(zeros_made.sem, zeros_made.at(l, 1))
                prod = [td[:, i, j, 0:P].rearrange("p (t c) -> p t c", t=STATE_TILES) for i in range(2) for j in range(2)]
                cre, cim = (st_cur[:, n, :].rearrange("p (t o) -> p t o", o=1).to_broadcast([P, STATE_TILES, 16])
                            for n in (3, 4))
                tt(prod[0], b_in[:, 0], cre, ALU.mult)
                tt(prod[1], b_in[:, 1], cim, ALU.mult)
                tt(prod[2], b_in[:, 1], cre, ALU.mult)
                tt(prod[3], b_in[:, 0], cim, ALU.mult).then_inc(dve_chain, 1)
                dve.wait_ge(dve_chain, links.next())
                for g in range(2):
                    half = slice(HD * g, HD * g + HD)
                    tt(b_blk[half, 0, :, 16 * g:16 * g + 16], prod[0][half], prod[1][half], ALU.subtract)
                    last = tt(b_blk[half, 1, :, 16 * g:16 * g + 16], prod[2][half], prod[3][half], ALU.add)
                last.then_inc(bblk_made.sem, 1)
                ffn(l, 0, True)
                rest(l, MIX0)
                rest(l, MIX0 + 1)
                norm(l, 0, MIX0 - 1, 0.5)

                def turn_in(q):
                    tl = slice(2 * q, 2 * q + 2)
                    if not q:
                        dve.wait_ge(rot_made.sem, rot_made.at(l, 1))
                    dve.wait_ge(bu_made.sem, bu_made.at(l, q + 1))
                    tt(td[:, 0], bu[:, :, 0, :], rot_c[:, tl, :], ALU.mult)
                    tt(td[:, 1], bu[:, :, 1, :], rot_s[:, tl, :], ALU.mult).then_inc(dve_chain, 1)
                    dve.wait_ge(dve_chain, links.next())
                    if q:
                        dve.wait_ge(c_done.sem, c_done.at(l, q))
                    tt(sw[:, 0], td[:, 0], td[:, 1], ALU.add).then_inc(dve_chain, 1)
                    dve.wait_ge(dve_chain, links.next())

                def scan(q):
                    dve.wait_ge(wim_made.sem, wim_made.at(l, q + 1))
                    for ri in range(2):
                        for t in range(2):
                            last = nc.vector.tensor_tensor_scan(
                                bu[:, t, ri, :], st_cur[:, 0, 2 * q + t:2 * q + t + 1].to_broadcast([P, SEQ]),
                                sw[:, ri, t, :], 0.0, ALU.mult, ALU.add)
                    last.then_inc(z_made.sem, 1)

                def turn_out(q):
                    tl = slice(2 * q, 2 * q + 2)
                    dve.wait_ge(z_made.sem, z_made.at(l, q + 1))
                    tt(td[:, 0], bu[:, :, 0, :], rot_c[:, tl, :], ALU.mult)
                    tt(td[:, 1], bu[:, :, 1, :], rot_s[:, tl, :], ALU.mult).then_inc(dve_chain, 1)
                    dve.wait_ge(dve_chain, links.next())
                    tt(sw[:, 0], td[:, 0], td[:, 1], ALU.subtract).then_inc(xre_made.sem, 1)

                def scaled_scores(S, n, bank, keys):
                    dve.wait_ge(scores_done.sem, scores_done.at(l, n))
                    k = keys.stop - keys.start
                    band = mask[:, keys].rearrange("p (o k) -> p o k", o=1).to_broadcast([P, HEADS, k])
                    src = ps[:, bank:bank + HEADS * k // 512, :].rearrange("p b (h k) -> p (b h) k", k=k)
                    stt(S[:, :, :], src, HD ** -0.5, band, ALU.mult, ALU.add).then_inc(s_made.sem, 1)

                def attn_rest(n, blk):
                    dve.wait_ge(ya_hi.sem, ya_hi.at(l, n))
                    tok = slice(blk * P, blk * P + P)
                    tt(y_attn[:, :, 1, tok], ps[:, 3, :].rearrange("p (m q) -> p m q", m=4),
                       f32(y_attn[:, :, 0, tok]), ALU.subtract).then_inc(ya_lo.sem, 1)

                def branch_sum(j):
                    dve.wait_ge(used.sem, used.at(l, MIX0 + BRANCH[j] + 1))
                    if j:
                        dve.wait_ge(sum_lo.sem, sum_lo.at(l, j))
                    g = gates[:, :, 2 * j:2 * j + 2, :]
                    y = [ps[:, 4 + b, :].rearrange("p (m t) -> p m t", m=2) for b in range(3)]
                    tt(hid[:, :, :], g[:, 0], y[0], ALU.mult).then_inc(br_read.sem, 1)
                    tt(act[:, :, :], g[:, 1], y[1], ALU.mult).then_inc(br_read.sem, 1)
                    dve.wait_ge(br_read.sem, br_read.at(l, 3 * j + 2))
                    tt(hid[:, :, :], hid[:, :, :], act[:, :, :], ALU.add).then_inc(dve_chain, 1)
                    dve.wait_ge(dve_chain, links.next())
                    tt(act[:, :, :], g[:, 2], y[2], ALU.mult).then_inc(br_read.sem, 1)
                    dve.wait_ge(br_read.sem, br_read.at(l, 3 * j + 3))
                    tt(hid[:, :, :], hid[:, :, :], act[:, :, :], ALU.add).then_inc(sum_made.sem, 1)

                def sum_rest(j):
                    dve.wait_ge(sum_hi.sem, sum_hi.at(l, j + 1))
                    tt(rows_lo[:, j % 2], hid[:, :, :], f32(rows_hi[:, j % 2]), ALU.subtract).then_inc(sum_lo.sem, 1)

                def lo(k):
                    rest(l, MIX0 + k)

                for k in range(2, 6):
                    lo(k)
                scaled_scores(S1, 1, 0, slice(0, 2 * P))
                scaled_scores(S0, 2, 6, slice(P, 2 * P))
                dve.wait_ge(s_made.sem, s_made.at(l, 2))
                nc.vector.tensor_reduce(mx[:, 1, :], S1[:, :, :], AX.X, ALU.max)
                lo(6)
                nc.vector.tensor_reduce(mx[:, 0, :], S0[:, :, :], AX.X, ALU.max).then_inc(dve_chain, 1)
                dve.wait_ge(dve_chain, links.next())
                both = sinks[:, :].rearrange("p (o h) -> p o h", o=1).to_broadcast([P, 2, HEADS])
                tt(mx[:, :, :], mx[:, :, :], both, ALU.max).then_inc(dve_chain, 1)
                dve.wait_ge(dve_chain, links.next())
                ts(negm[:, :, :], mx[:, :, :], -1.0, None, ALU.mult).then_inc(dve_chain, 1)
                dve.wait_ge(dve_chain, links.next())
                tt(esink[:, :, :], both, negm[:, :, :], ALU.add).then_inc(negm_made.sem, 1)
                lo(7)
                lo(8)
                turn_in(0)
                scan(0)
                turn_out(0)
                dve.wait_ge(exp_made.sem, exp_made.at(l, 1))
                tt(psum_p[:, :, :], psum_p[:, :, :], esink[:, :, :], ALU.add).then_inc(dve_chain, 1)
                dve.wait_ge(dve_chain, links.next())
                nc.vector.reciprocal(rden[:, :, :], psum_p[:, :, :]).then_inc(rden_made.sem, 1)
                lo(9)
                lo(10)
                turn_in(1)
                scan(1)
                lo(11)
                turn_out(1)
                dve.wait_ge(cz_made.sem, cz_made.at(l, 1))
                dve.wait_ge(proj_read.sem, proj_read.at(l, BB + 1))
                for c in range(2):
                    y = cv_c[:, c, :]
                    ts(y, cv_z[:, c, 0:SEQ], cw_cur[:, 0, c:c + 1], cb_cur[:, c:c + 1], ALU.mult, ALU.add).then_inc(dve_chain, 1)
                    dve.wait_ge(dve_chain, links.next())
                    for w in (1, 2):
                        stt(y, cv_z[:, c, w:w + SEQ], cw_cur[:, w, c:c + 1], y, ALU.mult, ALU.add).then_inc(dve_chain, 1)
                        dve.wait_ge(dve_chain, links.next())
                tt(cv_h[:, :, :], cv_c[:, :, :], cv_b[:, :, :], ALU.mult).then_inc(yc_made.sem, 1)
                lo(12)
                turn_in(2)
                scan(2)
                lo(13)
                turn_out(2)
                attn_rest(1, 1)
                lo(14)
                turn_in(3)
                scan(3)
                lo(15)
                turn_out(3)
                attn_rest(2, 0)
                lo(16)
                dve.wait_ge(yc_hi.sem, yc_hi.at(l, 1))
                tt(y_cs[:, 0:2, 1, :], cv_h[:, :, :], f32(y_cs[:, 0:2, 0, :]), ALU.subtract).then_inc(yc_lo.sem, 1)
                dve.wait_ge(c_done.sem, c_done.at(l, 4))
                for c in range(2):
                    last = stt(td[:, 0, c, :], uT[:, c, :], d_cur[:, c:c + 1], ps[:, 2, c * SEQ:c * SEQ + SEQ],
                               ALU.mult, ALU.add)
                last.then_inc(yd_made.sem, 1)
                lo(17)
                lo(18)
                dve.wait_ge(glu_sig.sem, glu_sig.at(l, 1))
                tt(td[:, 1], sw[:, 0], td[:, 0], ALU.mult).then_inc(ys_made.sem, 1)
                lo(19)
                dve.wait_ge(ys_hi.sem, ys_hi.at(l, 1))
                tt(y_cs[:, 2:4, 1, :], td[:, 1], f32(y_cs[:, 2:4, 0, :]), ALU.subtract).then_inc(ys_lo.sem, 1)
                lo(20)
                lo(21)
                dve.wait_ge(proj_read.sem, proj_read.at(l, PROJ_CHUNKS))
                branch_sum(0)
                lo(22)
                sum_rest(0)
                lo(23)
                branch_sum(1)
                sum_rest(1)
                lo(24)
                lo(25)
                branch_sum(2)
                sum_rest(2)
                lo(26)
                branch_sum(3)
                rest(l, FFN0[1])
                sum_rest(3)
                rest(l, FFN0[1] + 1)
                norm(l, 1, FFN0[1] - 1, 1.0)
                ffn(l, 1, True)
                norm(l, 2, LAYER_CHUNKS - 1, 0.5)
                links.leave()


_INPUTS = ["x", "ffn1_w_gate", "ffn1_w_up", "ffn1_w_down", "ln1_g", "ln1_b", "w_in", "conv_w", "conv_b",
           "ssm_a_re", "ssm_a_im", "ssm_log_dt", "ssm_b_re", "ssm_b_im", "ssm_c_re", "ssm_c_im", "ssm_d",
           "ssm_w_glu", "attn_sinks", "w_br_conv", "w_br_ssm", "w_br_attn", "w_out", "ln2_g", "ln2_b",
           "ffn2_w_gate", "ffn2_w_up", "ffn2_w_down", "ln3_g", "ln3_b"]


def kernel(**inputs):
    import numpy as np
    import concourse.bacc as bacc
    from concourse.bass_utils import run_bass_kernel_spmd

    nc = bacc.Bacc("TRN2", target_bir_lowering=False, num_devices=1)
    arrays, args = {}, []
    for name in _INPUTS:
        a = np.ascontiguousarray(inputs[name])
        arrays[f"in_{name}"] = a
        args.append(nc.dram_tensor(f"in_{name}", a.shape, mybir.dt.from_np(a.dtype), kind="ExternalInput").ap())
    args.append(nc.dram_tensor("out", (1, SEQ, D), F32, kind="ExternalOutput").ap())
    trunk(nc, *args)
    return run_bass_kernel_spmd(nc, [arrays], core_ids=[0]).results[0]["out"]
```

```python
import math
from contextlib import ExitStack

import concourse.bass as bass
from concourse import mybir

F32 = mybir.dt.float32
F32R = mybir.dt.float32r
BF16 = mybir.dt.bfloat16
ALU = mybir.AluOpType
ACT = mybir.ActivationFunctionType
AX = mybir.AxisListType

P = 128
DEPTH, D, SEQ, DFF = 2, 1024, 256, 2816
KC = D // P
NT = SEQ // P
ALPHA = (2 * DEPTH) ** 0.25
EPS = 1e-5
SLOTS = 3
CHUNK = 2048
STEPS = DFF // 256
FFN_CHUNKS = 3 * STEPS
PROJ_CHUNKS = 19
MIX_CHUNKS = PROJ_CHUNKS + 8
LAYER_CHUNKS = 2 * FFN_CHUNKS + MIX_CHUNKS
MIX0 = FFN_CHUNKS
FFN0 = (0, FFN_CHUNKS + MIX_CHUNKS)
KV, QA, QB, UU, CC, HH, BB, GATE0 = range(8)
BRANCH = (19, 20, 22, 24)
OUT = (21, 23, 25, 26)
OFF_B, OFF_C, OFF_H, OFF_U, OFF_Q, OFF_K, OFF_G = 0, 256, 512, 768, 1024, 1536, 1792
HD, HEADS = 64, 8
STATE_TILES = 8
MASKED = -3.0e38
TWO_PI_A = 6.28125
TWO_PI_B = 1.934051513671875e-3
TWO_PI_C = 2 * 3.141592653589793 - TWO_PI_A - TWO_PI_B
ROUND = 1.5 * 2.0 ** 23
DMAS = [1] * LAYER_CHUNKS
for _k in (QA, QB):
    DMAS[MIX0 + _k] = 4
for _k in BRANCH:
    DMAS[MIX0 + _k] = 4
LANDED = [16 * sum(DMAS[_j] for _j in range(_k % SLOTS, _k + 1, SLOTS)) for _k in range(LAYER_CHUNKS)]
LANDED_LAYER = [16 * sum(DMAS[_s::SLOTS]) for _s in range(SLOTS)]
N_LN = 96
ROW_ARE, ROW_AIM, ROW_DT, ROW_CW, ROW_CB, ROW_D, N_SMALL = 0, 16, 32, 48, 60, 64, 68


POOL_LINKS, DVE_LINKS = 76, 42


class Events:

    def __init__(self, sem, layer, before=0, unit=1):
        self.sem, self.layer, self.before, self.unit = sem, layer, before, unit

    def at(self, l, n):
        return l * (self.layer * self.unit) + (n + self.before) * self.unit


class Chain:

    def __init__(self, layer):
        self.layer, self.n, self.base = layer, 0, 0

    def enter(self, l):
        self.before = self.n
        self.base = l * self.layer

    def leave(self):
        assert self.n - self.before == self.layer, (self.n - self.before, self.layer)

    def next(self):
        self.n += 1
        return self.base + self.n


def trunk(nc, x, ffn1_w_gate, ffn1_w_up, ffn1_w_down, ln1_g, ln1_b, w_in, conv_w, conv_b,
          ssm_a_re, ssm_a_im, ssm_log_dt, ssm_b_re, ssm_b_im, ssm_c_re, ssm_c_im, ssm_d,
          ssm_w_glu, attn_sinks, w_br_conv, w_br_ssm, w_br_attn, w_out, ln2_g, ln2_b,
          ffn2_w_gate, ffn2_w_up, ffn2_w_down, ln3_g, ln3_b, out):
    ctx = ExitStack()
    with ctx:
        def sb(name, shape, dt=F32):
            return ctx.enter_context(nc.sbuf_tensor(name, shape, dt))

        def overlay(first, second):
            size = [sum(4 * math.prod(shape[1:]) for _, shape, _ in s) for s in (first, second)]
            held, brief = (second, first) if size[1] >= size[0] else (first, second)
            with ExitStack() as own:
                over = [own.enter_context(nc.sbuf_tensor(*a)) for a in brief]
            kept = [sb(*a) for a in held]
            return over + kept if held is second else kept + over

        raw = [sb(f"raw{s}", [P, CHUNK]) for s in range(SLOTS)]
        w_hi = [sb(f"w_hi{s}", [P, CHUNK], F32R) for s in range(SLOTS)]
        w_lo = [sb(f"w_lo{s}", [P, CHUNK], F32R) for s in range(SLOTS)]
        xT = sb("xT", [P, KC, 2, SEQ], F32R)
        ax = sb("ax", [P, NT, D])
        gates, res, xTf, gb = overlay(
            [("gates", [P, 3, KC, SEQ], F32)],
            [("res", [P, NT, D], F32), ("xTf", [P, KC, SEQ], F32), ("gb", [P, 2, D], F32)])
        probsT, rows_hi, rows_lo = overlay(
            [("probsT", [P, 2 * HEADS, P], F32)],
            [("rows_hi", [P, 2, 2, SEQ], F32R), ("rows_lo", [P, 2, 2, SEQ], F32R)])
        S1, y_attn = overlay([("S1", [P, HEADS, 2 * P], F32)], [("y_attn", [P, 4, 2, SEQ], F32R)])
        S0, b_in, b_blk, c_in = overlay(
            [("S0", [P, HEADS, P], F32)],
            [("b_in", [P, 2, STATE_TILES, 16], F32), ("b_blk", [P, 2, STATE_TILES, 32], F32),
             ("c_in", [P, 2, 2, 2, HD], F32)])
        bTz, y_cs = overlay([("bTz", [P, STATE_TILES, 2, P], F32)], [("y_cs", [P, 4, 2, SEQ], F32R)])
        td, act, hid = overlay([("td", [P, 2, 2, SEQ], F32)], [("act", [P, 2, SEQ], F32), ("hid", [P, 2, SEQ], F32)])
        qT, cv_c, cv_h = overlay([("qT", [P, 4, SEQ], F32)], [("cv_c", [P, 2, SEQ], F32), ("cv_h", [P, 2, SEQ], F32)])
        kz = sb("kz", [P, 2, SEQ])
        vz = sb("vz", [P, 2, 2, P])
        mask = sb("mask", [P, 2 * P])
        sinks = sb("sinks", [P, HEADS])
        mx = sb("mx", [P, 2, HEADS])
        negm = sb("negm", [P, 2, HEADS])
        esink = sb("esink", [P, 2, HEADS])
        psum_p = sb("psum_p", [P, 2, HEADS])
        rden = sb("rden", [P, 2, HEADS])
        rot_c = sb("rot_c", [P, STATE_TILES, SEQ])
        rot_s = sb("rot_s", [P, STATE_TILES, SEQ])
        bu = sb("bu", [P, 2, 2, SEQ])
        sw = sb("sw", [P, 2, 2, SEQ])
        tp = sb("tp", [P, 2, 2, SEQ])
        uT = sb("uT", [P, 2, SEQ])
        cTz = sb("cTz", [P, STATE_TILES, 2, P])
        cv_b, w_glu = overlay([("cv_b", [P, 2, SEQ], F32)], [("w_glu", [P, 2, 256], F32)])
        cv_z = sb("cv_z", [P, 2, SEQ + 2])
        ln_rows = td[:, 0].rearrange("p a t -> p (a t)")[0:N_LN, 0:P]
        small_rows = td[:, 1].rearrange("p a t -> p (a t)")[0:N_SMALL, 0:P]
        dt_rows = td[:, 1].rearrange("p a t -> p (a t)")[ROW_DT:ROW_DT + 16, P:P + 2]
        lnT = sb("lnT", [P, 6, DEPTH, KC])
        smallT = sb("smallT", [P, N_SMALL])
        stat = sb("stat", [P, 6, DEPTH, STATE_TILES])
        sc, bnst, mv, veps, rstd = overlay(
            [("sc", [P, 7, DEPTH * STATE_TILES], F32)],
            [("bnst", [P, NT, 2, 6], F32), ("mv", [P, NT, 2], F32), ("veps", [P, NT], F32), ("rstd", [P, NT], F32)])
        ln_cur = sb("ln_cur", [P, 6, KC])
        st_cur = sb("st_cur", [P, 6, STATE_TILES])
        cw_cur = sb("cw_cur", [P, 3, 2])
        cb_cur = sb("cb_cur", [P, 2])
        d_cur = sb("d_cur", [P, 2])
        ident = sb("ident", [P, P])
        zero_b = sb("zero_b", [P, 512], BF16)
        powers = sb("powers", [P, 2])
        mhalf, alpha = powers[:, 0:1], powers[:, 1:2]

        ps = ctx.enter_context(nc.psum_tensor("ps", [P, 8, 512], F32))
        acc = ps[:, 0:4, :].rearrange("p (t h) n -> p t h n", t=NT)

        def sem(name):
            return ctx.enter_context(nc.semaphore(name))

        x_landed, small_landed, out_stored = sem("x_landed"), sem("small_landed"), sem("out_stored")
        landed = [sem(f"landed{s}") for s in range(SLOTS)]
        layer_landed = Events(sem("layer_landed"), 7, unit=16)
        glu_landed = Events(sem("glu_landed"), 1, unit=16)
        zeros_made = Events(sem("zeros_made"), 1)
        gb_landed = Events(sem("gb_landed"), 6, unit=16)
        consts_made = sem("consts_made")
        rows_made, pro_tp, pro_small, state_act, state_pool, stat_made = (
            sem("rows_made"), sem("pro_tp"), sem("pro_small"), sem("state_act"), sem("state_pool"), sem("stat_made"))
        hi_made = Events(sem("hi_made"), LAYER_CHUNKS)
        lo_made = Events(sem("lo_made"), LAYER_CHUNKS, before=SLOTS)
        used = Events(sem("used"), LAYER_CHUNKS, before=SLOTS)
        silu_made = Events(sem("silu_made"), 2 * STEPS)
        h_made = Events(sem("h_made"), 2 * STEPS)
        h_hi = Events(sem("h_hi"), 2 * STEPS)
        h_lo = Events(sem("h_lo"), 2 * STEPS)
        res_made = Events(sem("res_made"), 3 * NT)
        var_made = Events(sem("var_made"), 3 * NT)
        rstd_made = Events(sem("rstd_made"), 3 * NT)
        xn_made = Events(sem("xn_made"), 3 * NT)
        tp_made = Events(sem("tp_made"), 3 * NT, before=NT)
        xTf_dve = Events(sem("xTf_dve"), 3, before=NT)
        xTf_act = Events(sem("xTf_act"), 3 * NT, before=NT)
        x_hi = Events(sem("x_hi"), 3 * NT, before=NT)
        x_lo = Events(sem("x_lo"), 3 * NT, before=NT)
        x_made = Events(sem("x_made"), 3 * NT)
        acc_done = Events(sem("acc_done"), 3)
        ax_made = Events(sem("ax_made"), 3 * NT, before=NT)
        cur_made = Events(sem("cur_made"), 1)
        bblk_made = Events(sem("bblk_made"), 1)
        bcT_done = Events(sem("bcT_done"), 1)
        bcT_made = Events(sem("bcT_made"), 1)
        rot_made = Events(sem("rot_made"), 1)
        proj_read = Events(sem("proj_read"), PROJ_CHUNKS)
        scores_done = Events(sem("scores_done"), 2)
        s_made = Events(sem("s_made"), 2)
        negm_made = Events(sem("negm_made"), 1)
        exp_made = Events(sem("exp_made"), 1)
        rden_made = Events(sem("rden_made"), 1)
        probs_made = Events(sem("probs_made"), 2)
        pT_done = Events(sem("pT_done"), 6)
        pT_made = Events(sem("pT_made"), 6)
        pv_done = Events(sem("pv_done"), 2)
        ya_hi = Events(sem("ya_hi"), 2)
        ya_lo = Events(sem("ya_lo"), 2)
        bu_done = Events(sem("bu_done"), 4)
        bu_made = Events(sem("bu_made"), 4)
        wim_made = Events(sem("wim_made"), 4)
        z_made = Events(sem("z_made"), 4)
        xre_made = Events(sem("xre_made"), 4)
        xim_made = Events(sem("xim_made"), 4)
        c_done = Events(sem("c_done"), 4)
        yd_made = Events(sem("yd_made"), 1)
        gelu_made = Events(sem("gelu_made"), 1)
        glu_done = Events(sem("glu_done"), 1)
        glu_sig = Events(sem("glu_sig"), 1)
        ys_made = Events(sem("ys_made"), 1)
        ys_hi = Events(sem("ys_hi"), 1)
        ys_lo = Events(sem("ys_lo"), 1)
        cz_made = Events(sem("cz_made"), 1)
        yc_made = Events(sem("yc_made"), 1)
        yc_hi = Events(sem("yc_hi"), 1)
        yc_lo = Events(sem("yc_lo"), 1)
        br_read = Events(sem("br_read"), 12)
        sum_made = Events(sem("sum_made"), 4)
        sum_hi = Events(sem("sum_hi"), 4)
        sum_lo = Events(sem("sum_lo"), 4)
        carried = sem("carried")
        dve_chain, pool_chain = sem("dve_chain"), sem("pool_chain")

        def cols(slot):
            return slot[:, :].rearrange("p (c n) -> p c n", c=KC)

        def wide(slot):
            return slot[:, :].rearrange("p (c n) -> p c n", c=2)

        block = ctx.enter_context(nc.Block())

        @block.sync
        def _(sp):
            sp.dma_start(res[:, :, :], x[0].rearrange("(t p) d -> p t d", p=P)).then_inc(x_landed, 16)
            sp.sem_inc(lo_made.sem, SLOTS)
            sp.sem_inc(used.sem, SLOTS)
            def load(l, k, parts, slot=None):
                slot = k % SLOTS if slot is None else slot
                sp.wait_ge(lo_made.sem, lo_made.at(l, k - SLOTS + 1))
                sp.sem_inc(carried, 1)
                for dst, src in parts(raw[slot]):
                    sp.dma_start(dst, src).then_inc(landed[slot], 16)

            def at_layer(w, l):
                return w[bass.ds(l, 1)].rearrange("a r n -> (a r) n")

            def columns(w, l, c0):
                return lambda r: [(cols(r), at_layer(w, l).rearrange("(c p) n -> p c n", p=P)[:, :, bass.ds(c0, 256)])]

            def rows(w, l, r0):
                return lambda r: [(wide(r), at_layer(w, l)[bass.ds(r0, 256)].rearrange("(c p) n -> p c n", p=P))]

            def load_norm(l, g, b):
                for n, v in enumerate((g, b)):
                    sp.dma_start(gb[:, n, :], v[bass.ds(l, 1)].to_broadcast([P, D])).then_inc(gb_landed.sem, 16)

            def load_ffn(l, f, w_gate, w_up, w_down, after_two, after_step, before_last):
                k0 = FFN0[f]
                load(l, k0, columns(w_gate, l, 0))
                load(l, k0 + 1, columns(w_up, l, 0))
                after_two()
                load(l, k0 + 2, columns(w_gate, l, 256))
                load(l, k0 + 3, columns(w_up, l, 256))
                load(l, k0 + 4, rows(w_down, l, 0))
                after_step()
                with sp.Fori(2, STEPS) as i:
                    load(l, k0 + i * 3 - 1, columns(w_gate, l, i * 256), 2)
                    load(l, k0 + i * 3, columns(w_up, l, i * 256), 0)
                    load(l, k0 + i * 3 + 1, rows(w_down, l, i * 256 - 256), 1)
                before_last()
                load(l, k0 + FFN_CHUNKS - 1, rows(w_down, l, DFF - 256))

            def q_columns(l, a):
                def parts(r):
                    src = at_layer(w_in, l).rearrange("(c p) n -> p c n", p=P)
                    for m in range(2):
                        for hf in range(2):
                            c0, to = OFF_Q + (4 * hf + 2 * a + m) * HD, (2 * m + hf) * HD
                            yield cols(r)[:, :, to:to + HD], src[:, :, c0:c0 + HD]
                return parts

            def branch_columns(l, j):
                def parts(r):
                    n = slice(256 * j, 256 * j + 256)
                    yield cols(r)[:, 0:2, :], at_layer(w_br_conv, l).rearrange("(c p) n -> p c n", p=P)[:, :, n]
                    yield cols(r)[:, 2:4, :], at_layer(w_br_ssm, l).rearrange("(c p) n -> p c n", p=P)[:, :, n]
                    for hf in range(2):
                        src = at_layer(w_br_attn, l)[hf * 256:hf * 256 + 256]
                        yield cols(r)[hf * HD:hf * HD + HD, 4:8, :], src.rearrange("(m p) n -> p m n", p=HD)[:, :, n]
                return parts

            with sp.Fori(0, DEPTH) as l:
                def params_and_norm1():
                    sp.wait_ge(ax_made.sem, ax_made.at(l, 0))
                    small = layer_landed.sem
                    for n, v in enumerate((ssm_b_re, ssm_b_im)):
                        sp.dma_start(b_in[:, n], v[bass.ds(l, 1)].rearrange(
                            "a (t g) s c -> (a g s) t c", g=2)).then_inc(small, 16)
                    for n, v in enumerate((ssm_c_re, ssm_c_im)):
                        for twice in range(2):
                            sp.dma_start(c_in[:, :, n, twice, :], v[bass.ds(l, 1)].rearrange(
                                "a (u g) c s -> (a g c) u s", u=2)).then_inc(small, 16)
                    sp.dma_start(sinks[:, :], attn_sinks[bass.ds(l, 1)].to_broadcast([P, HEADS])).then_inc(small, 16)
                    load_norm(l, ln1_g, ln1_b)

                def nothing():
                    pass

                load_ffn(l, 0, ffn1_w_gate, ffn1_w_up, ffn1_w_down, nothing, params_and_norm1, nothing)
                for k, c0 in ((KV, OFF_K), (QA, None), (QB, None), (UU, OFF_U), (CC, OFF_C), (HH, OFF_H), (BB, OFF_B)):
                    load(l, MIX0 + k, q_columns(l, k - QA) if c0 is None else columns(w_in, l, c0))
                for g in range(12):
                    load(l, MIX0 + GATE0 + g, columns(w_in, l, OFF_G + 256 * g))
                    if g == 7:
                        sp.wait_ge(yc_made.sem, yc_made.at(l, 1))
                        sp.dma_start(w_glu[:, :, :], at_layer(ssm_w_glu, l).rearrange(
                            "(c p) n -> p c n", p=P)).then_inc(glu_landed.sem, 16)
                for k in range(PROJ_CHUNKS, MIX_CHUNKS):
                    if k in BRANCH:
                        load(l, MIX0 + k, branch_columns(l, BRANCH.index(k)))
                    else:
                        load(l, MIX0 + k, rows(w_out, l, 256 * OUT.index(k)))

                def norm2():
                    sp.wait_ge(sum_made.sem, sum_made.at(l, 4))
                    load_norm(l, ln2_g, ln2_b)

                def norm3():
                    sp.wait_ge(ax_made.sem, ax_made.at(l, 2 * NT))
                    load_norm(l, ln3_g, ln3_b)
                load_ffn(l, 1, ffn2_w_gate, ffn2_w_up, ffn2_w_down, norm2, nothing, norm3)

            for t in range(NT):
                sp.wait_ge(x_made.sem, x_made.at(DEPTH - 1, 2 * NT + t + 1))
                sp.dma_start(out[0, t * P:t * P + P, :], res[:, t, :]).then_inc(out_stored, 16)
            sp.wait_ge(out_stored, 16 * NT)

        @block.tensor
        def _(pe):
            mm = nc.tensor.matmul

            def take(l, k):
                pe.wait_ge(lo_made.sem, lo_made.at(l, k + 1))

            def project(slot, bank, done=None):
                h, w = cols(w_hi[slot]), cols(w_lo[slot])
                for m in range(2):
                    o = ps[:, bank, m * SEQ:m * SEQ + SEQ]
                    for c in range(KC):
                        n = slice(m * P, m * P + P)
                        mm(o, h[:, c, n], xT[:, c, 0, :], start=c == 0, stop=False)
                        mm(o, h[:, c, n], xT[:, c, 1, :], start=False, stop=False)
                        last = mm(o, w[:, c, n], xT[:, c, 0, :], start=False, stop=c == KC - 1)
                last.then_inc(used.sem, 1)

            def accumulate(slot, buf, start=False, stop=False, tiles=range(NT)):
                h, w = wide(w_hi[slot]), wide(w_lo[slot])
                for t in tiles:
                    for c in range(2):
                        tok = slice(t * P, t * P + P)
                        for left, right, first in ((rows_hi, h, True), (rows_hi, w, False), (rows_lo, h, False)):
                            for n in range(2):
                                last = mm(acc[:, t, n, :], left[:, buf, c, tok], right[:, c, n * 512:n * 512 + 512],
                                          start=start and first and c == 0, stop=stop and left is rows_lo and c == 1,
                                          skip_group_check=True)
                return last

            def both_done(last):
                last.then_inc(used.sem, 1)

            def transposes(l, norm, t, src):
                b = 6 - 2 * t
                for c in range(KC):
                    last = nc.tensor.transpose(ps[:, b + c // 4, (c % 4) * P:(c % 4) * P + P],
                                               src[:, t, c * P:c * P + P], ident[:, :])
                last.then_inc(tp_made.sem, 1)

            def open_acc(l, n):
                pe.wait_ge(res_made.sem, res_made.at(l, n))
                for t in range(NT):
                    for h in range(2):
                        mm(acc[:, t, h, :], zero_b[:, 0:P], zero_b[:, :], start=True, stop=False,
                           skip_group_check=True)

            def ffn(l, f, norm):
                k0, s0 = FFN0[f], f * STEPS
                take(l, k0)
                pe.wait_ge(x_lo.sem, x_lo.at(l, norm * NT))
                project(0, 4)
                take(l, k0 + 1)
                project(1, 5)

                def step(i):
                    take(l, k0 + i * 3 - 1)
                    pe.wait_ge(silu_made.sem, silu_made.at(l, s0 + i))
                    project(2, 4)
                    take(l, k0 + i * 3)
                    pe.wait_ge(h_made.sem, h_made.at(l, s0 + i))
                    project(0, 5)
                    take(l, k0 + i * 3 + 1)
                    pe.wait_ge(h_lo.sem, h_lo.at(l, s0 + i))

                with pe.Fori(1, STEPS - 1) as i:
                    step(i)
                    accumulate(1, 0).then_inc(used.sem, 1)
                step(STEPS - 1)
                accumulate(1, 0, tiles=(0,))
                take(l, k0 + FFN_CHUNKS - 1)
                pe.wait_ge(h_lo.sem, h_lo.at(l, s0 + STEPS))
                accumulate(2, 1, stop=True, tiles=(0,)).then_inc(acc_done.sem, 1)
                accumulate(1, 0, tiles=(1,)).then_inc(used.sem, 1)
                both_done(accumulate(2, 1, stop=True, tiles=(1,)))

            def norm_transposes(l, norm):
                for t in range(NT):
                    pe.wait_ge(xn_made.sem, xn_made.at(l, norm * NT + t + 1))
                    transposes(l, norm, t, res)

            pe.wait_ge(x_landed, 16)
            pe.wait_ge(consts_made, 1)
            for t in range(NT):
                transposes(0, 0, t, res)
            pe.wait_ge(rows_made, 1)
            pe.wait_ge(small_landed, 16 * 12)
            nc.tensor.transpose(ps[:, 0, 0:N_LN], ln_rows, ident[0:N_LN, 0:N_LN])
            nc.tensor.transpose(ps[:, 0, P:P + N_SMALL], small_rows, ident[0:N_SMALL, 0:N_SMALL]).then_inc(pro_tp, 1)
            pe.wait_ge(pro_small, 1)
            for t in range(NT):
                for h in range(2):
                    mm(acc[:, t, h, :], zero_b[:, 0:P], zero_b[:, :], start=True, stop=False, skip_group_check=True)

            with pe.Fori(0, DEPTH) as l:
                ffn(l, 0, 0)
                norm_transposes(l, 0)
                def chunk(k):
                    take(l, MIX0 + k)
                    if k >= 2:
                        pe.wait_ge(proj_read.sem, proj_read.at(l, k - 1))
                    if k != KV:
                        project((MIX0 + k) % SLOTS, 4 + k % 2)

                def project_kv(slot, bank):
                    h, w = cols(w_hi[slot]), cols(w_lo[slot])
                    o = ps[:, bank, 0:SEQ]
                    for c in range(KC):
                        mm(o, h[:, c, 0:P], xT[:, c, 0, :], start=c == 0, stop=False)
                        mm(o, h[:, c, 0:P], xT[:, c, 1, :], start=False, stop=False)
                        mm(o, w[:, c, 0:P], xT[:, c, 0, :], start=False, stop=c == KC - 1)
                    for t in range(NT):
                        o = ps[:, bank, SEQ + t * P:SEQ + t * P + P]
                        tok = slice(t * P, t * P + P)
                        for c in range(KC):
                            mm(o, xT[:, c, 0, tok], h[:, c, P:2 * P], start=c == 0, stop=False)
                            mm(o, xT[:, c, 0, tok], w[:, c, P:2 * P], start=False, stop=False)
                            last = mm(o, xT[:, c, 1, tok], h[:, c, P:2 * P], start=False, stop=c == KC - 1)
                    last.then_inc(used.sem, 1)

                def input_states(q):
                    if q >= 1:
                        pe.wait_ge(bu_made.sem, bu_made.at(l, q))
                    for t in range(2 * q, 2 * q + 2):
                        for ri in range(2):
                            last = mm(ps[:, t % 2, ri * SEQ:ri * SEQ + SEQ], bTz[:, t, ri, :], uT[:, t // 4, :],
                                      start=True, stop=True)
                    last.then_inc(bu_done.sem, 1)

                def output_states(q):
                    pe.wait_ge(xre_made.sem, xre_made.at(l, q + 1))
                    pe.wait_ge(xim_made.sem, xim_made.at(l, q + 1))
                    ct = q // 2
                    for t in range(2 * q, 2 * q + 2):
                        for ri in range(2):
                            last = mm(ps[:, 2, ct * SEQ:ct * SEQ + SEQ], cTz[:, t, ri, :], sw[:, ri, t % 2, :],
                                      start=t % 4 == 0 and ri == 0, stop=t % 4 == 3 and ri == 1)
                    last.then_inc(c_done.sem, 1)

                def transpose_probs(S, parts, g0, first):
                    for g in range(parts):
                        if g0 + g >= 2:
                            pe.wait_ge(pT_made.sem, pT_made.at(l, g0 + g - 1))
                        b = 6 + (g0 + g) % 2
                        for n in range(4):
                            i = 4 * g + n
                            src = S[:, i // 2, (i % 2) * P:(i % 2) * P + P] if parts == 4 else S[:, i, :]
                            last = nc.tensor.transpose(ps[:, b, n * P:n * P + P], src, ident[:, :])
                        last.then_inc(pT_done.sem, 1)

                def attend(blk):
                    pe.wait_ge(pT_made.sem, pT_made.at(l, 4 if blk else 6))
                    for m in range(4):
                        terms = [(j, kb) for j in range(2) for kb in range(blk + 1)]
                        for n, (j, kb) in enumerate(terms):
                            head = m + 4 * j
                            i = 2 * head + kb if blk else head
                            last = mm(ps[:, 3, m * P:m * P + P], vz[:, kb, j, :], probsT[:, i, :],
                                      start=n == 0, stop=n == len(terms) - 1)
                    last.then_inc(pv_done.sem, 1)

                pe.wait_ge(x_lo.sem, x_lo.at(l, NT))
                chunk(KV)
                project_kv((MIX0 + KV) % SLOTS, 4)
                pe.wait_ge(bblk_made.sem, bblk_made.at(l, 1))
                pe.wait_ge(layer_landed.sem, layer_landed.at(l, 7))
                for u in range(2):
                    for ri in range(2):
                        n = (2 * u + ri) * P
                        nc.tensor.transpose(ps[:, 0, n:n + P], b_blk[:, ri, 4 * u:4 * u + 4, :], ident[:, :])
                        last = nc.tensor.transpose(ps[:, 1, n:n + P], c_in[:, u, ri, :, :], ident[:, :])
                last.then_inc(bcT_done.sem, 1)
                chunk(QA)
                chunk(QB)
                chunk(UU)
                pe.wait_ge(proj_read.sem, proj_read.at(l, QB + 1))
                pe.wait_ge(bcT_made.sem, bcT_made.at(l, 1))
                for head in range(HEADS):
                    last = mm(ps[:, head // 2, (head % 2) * SEQ:(head % 2) * SEQ + SEQ],
                              qT[:, head % 4, P:2 * P], kz[:, head // 4, :], start=True, stop=True)
                last.then_inc(scores_done.sem, 1)
                for head in range(HEADS):
                    last = mm(ps[:, 6 + head // 4, (head % 4) * P:(head % 4) * P + P],
                              qT[:, head % 4, 0:P], kz[:, head // 4, 0:P], start=True, stop=True)
                last.then_inc(scores_done.sem, 1)
                chunk(CC)
                chunk(HH)
                pe.wait_ge(s_made.sem, s_made.at(l, 2))
                input_states(0)
                chunk(BB)
                chunk(7)
                input_states(1)
                chunk(8)
                output_states(0)
                chunk(9)
                input_states(2)
                pe.wait_ge(probs_made.sem, probs_made.at(l, 1))
                transpose_probs(S1, 4, 0, 0)
                chunk(10)
                output_states(1)
                attend(1)
                chunk(11)
                input_states(3)
                pe.wait_ge(probs_made.sem, probs_made.at(l, 2))
                transpose_probs(S0, 2, 4, 16)
                chunk(12)
                output_states(2)
                pe.wait_ge(ya_lo.sem, ya_lo.at(l, 1))
                attend(0)
                chunk(13)
                chunk(14)
                output_states(3)
                chunk(15)
                pe.wait_ge(gelu_made.sem, gelu_made.at(l, 1))
                pe.wait_ge(glu_landed.sem, glu_landed.at(l, 1))
                for co in range(2):
                    for c in range(2):
                        last = mm(ps[:, 0, co * SEQ:co * SEQ + SEQ], w_glu[:, c, co * P:co * P + P], sw[:, 0, c, :],
                                  start=c == 0, stop=c == 1)
                last.then_inc(glu_done.sem, 1)
                chunk(16)
                chunk(17)
                chunk(18)

                def branch(j):
                    k = MIX0 + BRANCH[j]
                    take(l, k)
                    h, w = cols(w_hi[k % SLOTS]), cols(w_lo[k % SLOTS])
                    for b, (y, kc, yc) in enumerate(((y_cs, (0, 1), 0), (y_cs, (2, 3), 0), (y_attn, (4, 5, 6, 7), 4))):
                        if j == 0:
                            pe.wait_ge((yc_lo, ys_lo, ya_lo)[b].sem, (yc_lo, ys_lo, ya_lo)[b].at(l, 2 if b == 2 else 1))
                        else:
                            pe.wait_ge(br_read.sem, br_read.at(l, 3 * (j - 1) + b + 1))
                        for m in range(2):
                            o = ps[:, 4 + b, m * SEQ:m * SEQ + SEQ]
                            n = slice(m * P, m * P + P)
                            for c in kc:
                                mm(o, h[:, c, n], y[:, c - yc, 0, :], start=c == kc[0], stop=False)
                                mm(o, h[:, c, n], y[:, c - yc, 1, :], start=False, stop=False)
                                last = mm(o, w[:, c, n], y[:, c - yc, 0, :], start=False, stop=c == kc[-1])
                    last.then_inc(used.sem, 1)

                def output(j, tiles=range(NT)):
                    k = MIX0 + OUT[j]
                    take(l, k)
                    pe.wait_ge(sum_lo.sem, sum_lo.at(l, j + 1))
                    return accumulate(k % SLOTS, j % 2, start=j == 0, stop=j == 3, tiles=tiles)

                pe.wait_ge(proj_read.sem, proj_read.at(l, PROJ_CHUNKS))
                branch(0)
                branch(1)
                output(0).then_inc(used.sem, 1)
                branch(2)
                output(1).then_inc(used.sem, 1)
                branch(3)
                output(2, (0,))
                output(3, (0,)).then_inc(acc_done.sem, 1)
                output(2, (1,)).then_inc(used.sem, 1)
                both_done(output(3, (1,)))
                norm_transposes(l, 1)
                open_acc(l, 2 * NT)
                ffn(l, 1, 2)
                norm_transposes(l, 2)
                open_acc(l, 3 * NT)

        @block.scalar
        def _(sc_):
            act_ = nc.scalar.activation

            def split(l, k, slot=None, land=None):
                s = k % SLOTS if slot is None else slot
                n = LANDED[k] if land is None else land
                sc_.wait_ge(landed[s], l * LANDED_LAYER[s] + n)
                sc_.wait_ge(used.sem, used.at(l, k - SLOTS + 1))
                nc.scalar.copy(w_hi[s][:, :], raw[s][:, :]).then_inc(hi_made.sem, 1)

            def silu(l, n, k):
                sc_.wait_ge(used.sem, used.at(l, k + 1))
                act_(act[:, :, :], ps[:, 4, :].rearrange("p (m t) -> p m t", m=2), ACT.Silu).then_inc(silu_made.sem, 1)

            def hidden_hi(l, n, k, buf=0):
                sc_.wait_ge(h_made.sem, h_made.at(l, n))
                sc_.wait_ge(used.sem, used.at(l, k + 1))
                nc.scalar.copy(rows_hi[:, buf], hid[:, :, :]).then_inc(h_hi.sem, 1)

            def ffn(l, f, ahead):
                k0, s0 = FFN0[f], f * STEPS
                if not ahead:
                    split(l, k0)
                    split(l, k0 + 1)
                split(l, k0 + 2)
                silu(l, 1, k0)
                split(l, k0 + 3)

                def step(i, last):
                    hidden_hi(l, s0 + i, k0 + i * 3 - 2)
                    split(l, k0 + i * 3 + 1, 1, LANDED[k0 + 1] + i * 16)
                    silu(l, i + 1, k0 + i * 3 - 1)
                    split(l, k0 + i * 3 + 2, 2, LANDED[k0 + 2] + i * 16)
                    if not last:
                        split(l, k0 + i * 3 + 3, 0, LANDED[k0] + i * 16 + 16)

                with sc_.Fori(1, STEPS - 1) as i:
                    step(i, False)
                step(STEPS - 1, True)
                hidden_hi(l, s0 + STEPS, k0 + FFN_CHUNKS - 3, 1)

            def x_split(l, n, t):
                sc_.wait_ge(xTf_act.sem, xTf_act.at(l, n))
                tok = slice(t * P, t * P + P)
                nc.scalar.copy(xT[:, :, 0, tok], xTf[:, :, tok]).then_inc(x_hi.sem, 1)

            def norm(l, n0, norm_):
                for t in range(NT):
                    n = norm_ * NT + t + 1
                    sc_.wait_ge(tp_made.sem, tp_made.at(l, n))
                    for c in range(4 * t, KC):
                        last = act_(xTf[:, c, t * P:t * P + P], ps[:, 6 - 2 * t + c // 4, (c % 4) * P:(c % 4 + 1) * P],
                                    ACT.Identity, scale=ln_cur[:, 2 * norm_, c:c + 1],
                                    bias=ln_cur[:, 2 * norm_ + 1, c:c + 1])
                    last.then_inc(xTf_act.sem, 1)
                    if t:
                        sc_.wait_ge(xTf_dve.sem, xTf_dve.at(l, norm_ + 1))
                    x_split(l, n, t)

            dma = nc.scalar.dma_start
            dma(dt_rows[:, :], ssm_log_dt.rearrange("l (t g) -> (l t) g", g=2)).then_inc(small_landed, 16)
            for row, v in ((ROW_ARE, ssm_a_re), (ROW_AIM, ssm_a_im)):
                dma(small_rows[row:row + 16, :],
                    v.rearrange("l (t g) s -> (l t) (g s)", g=2)).then_inc(small_landed, 16)
            dma(small_rows[ROW_CW:ROW_CW + 12, :],
                conv_w.rearrange("l w (c p) -> (l w c) p", p=P)).then_inc(small_landed, 16)
            for row, v in ((ROW_CB, conv_b), (ROW_D, ssm_d)):
                dma(small_rows[row:row + 4, :], v.rearrange("l (c p) -> (l c) p", p=P)).then_inc(small_landed, 16)
            for n, v in enumerate((ln1_g, ln1_b, ln2_g, ln2_b, ln3_g, ln3_b)):
                dma(ln_rows[16 * n:16 * n + 16, :], v.rearrange("l (c p) -> (l c) p", p=P)).then_inc(small_landed, 16)
            for t in range(NT):
                sc_.wait_ge(tp_made.sem, tp_made.at(0, t + 1 - NT))
                nc.scalar.copy(xTf[:, 4:KC, t * P:t * P + P],
                               ps[:, 7 - 2 * t, :].rearrange("p (c n) -> p c n", c=4)).then_inc(xTf_act.sem, 1)
                sc_.wait_ge(xTf_dve.sem, xTf_dve.at(0, t + 1 - NT))
                x_split(0, t + 1 - NT, t)
            sc_.wait_ge(pro_small, 1)
            act_(sc[:, 0, :], smallT[:, ROW_DT:ROW_DT + 16], ACT.Exp).then_inc(state_act, 1)
            sc_.wait_ge(state_pool, 1)
            act_(stat[:, 0].rearrange("p l t -> p (l t)"), sc[:, 1, :], ACT.Exp).then_inc(state_act, 1)
            sc_.wait_ge(state_pool, 2)
            act_(stat[:, 2].rearrange("p l t -> p (l t)"), sc[:, 2, :], ACT.Sin).then_inc(state_act, 1)
            act_(sc[:, 3, :], sc[:, 2, :], ACT.Sin, scale=0.5).then_inc(state_act, 1)

            with sc_.Fori(0, DEPTH) as l:
                ffn(l, 0, False)
                split(l, MIX0)
                split(l, MIX0 + 1)
                norm(l, 0, 0)
                def bank(k):
                    return ps[:, 4 + k % 2, :]

                def read(k, dst):
                    sc_.wait_ge(used.sem, used.at(l, MIX0 + k + 1))
                    nc.scalar.copy(dst, bank(k).rearrange("p (m t) -> p m t", m=2)).then_inc(proj_read.sem, 1)

                def gate(k):
                    sc_.wait_ge(used.sem, used.at(l, MIX0 + k + 1))
                    g = k - GATE0
                    act_(gates[:, g // 4, 2 * (g % 4):2 * (g % 4) + 2, :], bank(k).rearrange("p (m t) -> p m t", m=2),
                         ACT.Sigmoid).then_inc(proj_read.sem, 1)

                def states(q):
                    sc_.wait_ge(bu_done.sem, bu_done.at(l, q + 1))
                    if q:
                        sc_.wait_ge(xre_made.sem, xre_made.at(l, q))
                        sc_.wait_ge(xim_made.sem, xim_made.at(l, q))
                    nc.scalar.copy(bu[:, :, :, :], ps[:, 0:2, :].rearrange("p b (r t) -> p b r t", r=2)
                                   ).then_inc(bu_made.sem, 1)

                def probs_out(g0, n):
                    for g in range(g0, g0 + n):
                        sc_.wait_ge(pT_done.sem, pT_done.at(l, g + 1))
                        i = 4 * (g - g0)
                        nc.scalar.copy(probsT[:, i:i + 4, :], ps[:, 6 + g % 2, :].rearrange("p (c n) -> p c n", c=4)
                                       ).then_inc(pT_made.sem, 1)

                def attn_hi(n, blk):
                    sc_.wait_ge(pv_done.sem, pv_done.at(l, n))
                    nc.scalar.copy(y_attn[:, :, 0, blk * P:blk * P + P], ps[:, 3, :].rearrange("p (m q) -> p m q", m=4)
                                   ).then_inc(ya_hi.sem, 1)

                split(l, MIX0 + 2)
                sc_.wait_ge(used.sem, used.at(l, MIX0 + KV + 1))
                nc.scalar.copy(kz[0:HD, 0, :], ps[0:HD, 4, 0:SEQ])
                nc.scalar.copy(kz[HD:P, 1, :], ps[HD:P, 4, 0:SEQ])
                v = ps[:, 4, SEQ:2 * SEQ].rearrange("p (b n) -> p b n", b=2)
                nc.scalar.copy(vz[:, :, 0, 0:HD], v[:, :, 0:HD])
                nc.scalar.copy(vz[:, :, 1, HD:P], v[:, :, HD:P]).then_inc(proj_read.sem, 1)
                split(l, MIX0 + 3)
                sc_.wait_ge(bcT_done.sem, bcT_done.at(l, 1))
                b_ps = ps[:, 0, :].rearrange("p (u r s) -> p u r s", u=2, r=2)
                c_ps = ps[:, 1, :].rearrange("p (u r q h c) -> p u r q h c", u=2, r=2, q=4, h=2)
                for q in range(4):
                    rows_ = slice(32 * q, 32 * q + 32)
                    nc.scalar.copy(bTz[rows_, q::4, :, :], b_ps[rows_])
                for u in range(2):
                    for q in range(4):
                        for h in range(2):
                            half, n = slice(HD * h, HD * h + HD), 32 * q + 16 * h
                            nc.scalar.copy(cTz[half, 4 * u + q, 0, n:n + 16], c_ps[half, u, 0, q, h, :])
                            last = nc.scalar.mul(cTz[half, 4 * u + q, 1, n:n + 16], c_ps[half, u, 1, q, h, :], -1.0)
                last.then_inc(bcT_made.sem, 1)
                read(QA, qT[:, 0:2, :])
                split(l, MIX0 + 4)
                read(QB, qT[:, 2:4, :])
                split(l, MIX0 + 5)
                read(UU, uT[:, :, :])
                split(l, MIX0 + 6)
                read(CC, cv_c[:, :, :])
                split(l, MIX0 + 7)
                sc_.wait_ge(negm_made.sem, negm_made.at(l, 1))
                for blk, S in ((1, S1), (0, S0)):
                    for head in range(HEADS):
                        act_(S[:, head, :], S[:, head, :], ACT.Exp, bias=negm[:, blk, head:head + 1],
                             accum_out=psum_p[:, blk, head:head + 1])
                    if blk:
                        read(HH, cv_h[:, :, :])
                        split(l, MIX0 + 8)
                        states(0)
                act_(esink[:, :, :], esink[:, :, :], ACT.Exp).then_inc(exp_made.sem, 1)
                sc_.wait_ge(ax_made.sem, ax_made.at(l, NT))
                read(BB, cv_b[:, :, :])
                split(l, MIX0 + 9)
                gate(7)
                split(l, MIX0 + 10)
                states(1)
                gate(8)
                split(l, MIX0 + 11)
                gate(9)
                split(l, MIX0 + 12)
                probs_out(0, 4)
                states(2)
                gate(10)
                split(l, MIX0 + 13)
                attn_hi(1, 1)
                gate(11)
                split(l, MIX0 + 14)
                probs_out(4, 2)
                gate(12)
                split(l, MIX0 + 15)
                states(3)
                attn_hi(2, 0)
                gate(13)
                split(l, MIX0 + 16)
                sc_.wait_ge(yc_made.sem, yc_made.at(l, 1))
                nc.scalar.copy(y_cs[:, 0:2, 0, :], cv_h[:, :, :]).then_inc(yc_hi.sem, 1)
                gate(14)
                split(l, MIX0 + 17)
                sc_.wait_ge(yd_made.sem, yd_made.at(l, 1))
                act_(sw[:, 0], td[:, 0], ACT.Gelu_apprx_tanh).then_inc(gelu_made.sem, 1)
                gate(15)
                split(l, MIX0 + 18)
                sc_.wait_ge(glu_done.sem, glu_done.at(l, 1))
                act_(td[:, 0], ps[:, 0, :].rearrange("p (m t) -> p m t", m=2), ACT.Sigmoid).then_inc(glu_sig.sem, 1)
                gate(16)
                split(l, MIX0 + 19)
                sc_.wait_ge(ys_made.sem, ys_made.at(l, 1))
                nc.scalar.copy(y_cs[:, 2:4, 0, :], td[:, 1]).then_inc(ys_hi.sem, 1)
                gate(17)
                split(l, MIX0 + 20)
                gate(18)
                split(l, MIX0 + 21)

                def sum_hi_(j):
                    sc_.wait_ge(sum_made.sem, sum_made.at(l, j + 1))
                    if j >= 2:
                        sc_.wait_ge(used.sem, used.at(l, MIX0 + OUT[j - 2] + 1))
                    nc.scalar.copy(rows_hi[:, j % 2], hid[:, :, :]).then_inc(sum_hi.sem, 1)
                split(l, MIX0 + 22)
                sum_hi_(0)
                split(l, MIX0 + 23)
                sum_hi_(1)
                split(l, MIX0 + 24)
                split(l, MIX0 + 25)
                sum_hi_(2)
                split(l, MIX0 + 26)
                split(l, FFN0[1])
                sum_hi_(3)
                split(l, FFN0[1] + 1)
                norm(l, 0, 1)
                ffn(l, 1, True)
                norm(l, 0, 2)

        @block.gpsimd
        def _(pool):
            links = Chain(POOL_LINKS)
            tt, ts, memset = nc.gpsimd.tensor_tensor, nc.gpsimd.tensor_scalar, nc.gpsimd.memset

            for tile in (ident[:, :], mask[:, :], zero_b[:, :], kz[:, :, :], vz[:, :, :, :],
                         cTz[:, :, :, :], cv_z[:, :, :]):
                memset(tile, 0.0).then_inc(pool_chain, 1)
                pool.wait_ge(pool_chain, links.next())
            memset(mhalf[:, :], -0.5).then_inc(pool_chain, 1)
            pool.wait_ge(pool_chain, links.next())
            nc.gpsimd.affine_select(out=ident[:, :], in_=ident[:, :], compare_op=ALU.not_equal, fill=1.0,
                                    base=0, pattern=[[-1, P]], channel_multiplier=1).then_inc(pool_chain, 1)
            pool.wait_ge(pool_chain, links.next())
            nc.gpsimd.affine_select(out=mask[:, :], in_=mask[:, :], compare_op=ALU.is_ge, fill=MASKED,
                                    base=-1, pattern=[[1, 2 * P]], channel_multiplier=-1).then_inc(pool_chain, 1)
            pool.wait_ge(pool_chain, links.next())
            nc.gpsimd.affine_select(out=mask[:, :], in_=mask[:, :], compare_op=ALU.is_ge, fill=MASKED,
                                    base=P, pattern=[[-1, 2 * P]], channel_multiplier=1).then_inc(pool_chain, 1)
            pool.wait_ge(pool_chain, links.next())
            pool.sem_inc(consts_made, 1)
            pool.wait_ge(x_landed, 16)
            memset(alpha[:, :], ALPHA).then_inc(pool_chain, 1)
            pool.wait_ge(pool_chain, links.next())
            for t in range(NT):
                nc.gpsimd.tensor_scalar(ax[:, t, :], res[:, t, :], ALPHA, None, ALU.mult).then_inc(ax_made.sem, 1)

            lr, li = smallT[:, ROW_ARE:ROW_ARE + 16], smallT[:, ROW_AIM:ROW_AIM + 16]
            mag, cos, sin, coef_r, coef_i, norm2 = (stat[:, n].rearrange("p l t -> p (l t)") for n in range(6))
            pool.wait_ge(state_act, 1)
            tt(sc[:, 1, :], lr, sc[:, 0, :], ALU.mult).then_inc(state_pool, 1)
            tt(sc[:, 4, :], li, sc[:, 0, :], ALU.mult).then_inc(pool_chain, 1)
            pool.wait_ge(pool_chain, links.next())
            ts(sc[:, 5, :], sc[:, 4, :], 1.0 / (2 * 3.141592653589793), ROUND, ALU.mult, ALU.add).then_inc(pool_chain, 1)
            pool.wait_ge(pool_chain, links.next())
            ts(sc[:, 5, :], sc[:, 5, :], ROUND, None, ALU.subtract).then_inc(pool_chain, 1)
            pool.wait_ge(pool_chain, links.next())
            for part in (TWO_PI_A, TWO_PI_B, TWO_PI_C):
                ts(sc[:, 6, :], sc[:, 5, :], -part, None, ALU.mult).then_inc(pool_chain, 1)
                pool.wait_ge(pool_chain, links.next())
                tt(sc[:, 4, :], sc[:, 4, :], sc[:, 6, :], ALU.add).then_inc(pool_chain, 1)
                pool.wait_ge(pool_chain, links.next())
            ts(sc[:, 2, :], sc[:, 4, :], 3.1415925, -3.1415925, ALU.min, ALU.max).then_inc(state_pool, 1)
            pool.wait_ge(state_act, 4)
            tt(sc[:, 5, :], sc[:, 3, :], sc[:, 3, :], ALU.mult).then_inc(pool_chain, 1)
            pool.wait_ge(pool_chain, links.next())
            ts(cos, sc[:, 5, :], -2.0, 1.0, ALU.mult, ALU.add).then_inc(pool_chain, 1)
            pool.wait_ge(pool_chain, links.next())
            tt(sc[:, 5, :], mag, cos, ALU.mult).then_inc(pool_chain, 1)
            pool.wait_ge(pool_chain, links.next())
            ts(sc[:, 5, :], sc[:, 5, :], 1.0, None, ALU.subtract).then_inc(pool_chain, 1)
            pool.wait_ge(pool_chain, links.next())
            tt(sc[:, 6, :], mag, sin, ALU.mult).then_inc(pool_chain, 1)
            pool.wait_ge(pool_chain, links.next())
            tt(sc[:, 0, :], lr, lr, ALU.mult).then_inc(pool_chain, 1)
            pool.wait_ge(pool_chain, links.next())
            tt(sc[:, 1, :], li, li, ALU.mult).then_inc(pool_chain, 1)
            pool.wait_ge(pool_chain, links.next())
            tt(norm2, sc[:, 0, :], sc[:, 1, :], ALU.add).then_inc(pool_chain, 1)
            pool.wait_ge(pool_chain, links.next())
            for o, a, b, op in ((coef_r, 5, 6, ALU.add), (coef_i, 6, 5, ALU.subtract)):
                tt(sc[:, 0, :], sc[:, a, :], lr, ALU.mult).then_inc(pool_chain, 1)
                pool.wait_ge(pool_chain, links.next())
                tt(sc[:, 1, :], sc[:, b, :], li, ALU.mult).then_inc(pool_chain, 1)
                pool.wait_ge(pool_chain, links.next())
                tt(o, sc[:, 0, :], sc[:, 1, :], op).then_inc(pool_chain, 1)
                pool.wait_ge(pool_chain, links.next())
            pool.sem_inc(stat_made, 1)

            def norm(l, norm_):
                for t in range(NT):
                    pool.wait_ge(var_made.sem, var_made.at(l, norm_ * NT + t + 1))
                    tt(rstd[:, t:t + 1], veps[:, t:t + 1], mhalf[:, :], ALU.pow).then_inc(rstd_made.sem, 1)
                pool.wait_ge(gb_landed.sem, gb_landed.at(l, 2 * norm_ + 2))
                for t in range(NT):
                    pool.wait_ge(tp_made.sem, tp_made.at(l, norm_ * NT + t + 1))
                    tt(res[:, t, :], res[:, t, :], gb[:, 0, :], ALU.mult).then_inc(pool_chain, 1)
                    pool.wait_ge(pool_chain, links.next())
                    tt(res[:, t, :], res[:, t, :], gb[:, 1, :], ALU.add).then_inc(x_made.sem, 1)
                for t in range(NT):
                    pool.wait_ge(x_made.sem, x_made.at(l, norm_ * NT + t + 1))
                    tt(ax[:, t, :], res[:, t, :], alpha[:, :].to_broadcast([P, D]), ALU.mult).then_inc(ax_made.sem, 1)

            with pool.Fori(0, DEPTH) as l:
                links.enter(l)
                pool.wait_ge(cur_made.sem, cur_made.at(l, 1))
                n = 1
                while n < SEQ:
                    k = min(STATE_TILES, 512 // n)
                    for t in range(0, STATE_TILES, k):
                        tl = slice(t, t + k)
                        c, s = rot_c[:, tl, 0:n], rot_s[:, tl, 0:n]
                        cn = rot_c[:, tl, n - 1:n].to_broadcast([P, k, n])
                        sn = rot_s[:, tl, n - 1:n].to_broadcast([P, k, n])
                        t0, t1 = (tp[:, i].rearrange("p a t -> p (a t)")[:, 0:k * n].rearrange("p (k n) -> p k n", k=k)
                                  for i in range(2))
                        tt(t0, c, cn, ALU.mult).then_inc(pool_chain, 1)
                        pool.wait_ge(pool_chain, links.next())
                        tt(t1, s, sn, ALU.mult).then_inc(pool_chain, 1)
                        pool.wait_ge(pool_chain, links.next())
                        tt(rot_c[:, tl, n:2 * n], t0, t1, ALU.subtract).then_inc(pool_chain, 1)
                        pool.wait_ge(pool_chain, links.next())
                        tt(t0, s, cn, ALU.mult).then_inc(pool_chain, 1)
                        pool.wait_ge(pool_chain, links.next())
                        tt(t1, c, sn, ALU.mult).then_inc(pool_chain, 1)
                        pool.wait_ge(pool_chain, links.next())
                        tt(rot_s[:, tl, n:2 * n], t0, t1, ALU.add).then_inc(pool_chain, 1)
                        pool.wait_ge(pool_chain, links.next())
                    n *= 2
                pool.sem_inc(rot_made.sem, 1)
                norm(l, 0)

                def turn_in(q):
                    tl = slice(2 * q, 2 * q + 2)
                    pool.wait_ge(bu_made.sem, bu_made.at(l, q + 1))
                    tt(tp[:, 0], bu[:, :, 1, :], rot_c[:, tl, :], ALU.mult).then_inc(pool_chain, 1)
                    pool.wait_ge(pool_chain, links.next())
                    tt(tp[:, 1], bu[:, :, 0, :], rot_s[:, tl, :], ALU.mult).then_inc(pool_chain, 1)
                    pool.wait_ge(pool_chain, links.next())
                    if q:
                        pool.wait_ge(c_done.sem, c_done.at(l, q))
                    tt(sw[:, 1], tp[:, 0], tp[:, 1], ALU.subtract).then_inc(wim_made.sem, 1)

                def turn_out(q):
                    tl = slice(2 * q, 2 * q + 2)
                    pool.wait_ge(z_made.sem, z_made.at(l, q + 1))
                    tt(tp[:, 0], bu[:, :, 0, :], rot_s[:, tl, :], ALU.mult).then_inc(pool_chain, 1)
                    pool.wait_ge(pool_chain, links.next())
                    tt(tp[:, 1], bu[:, :, 1, :], rot_c[:, tl, :], ALU.mult).then_inc(pool_chain, 1)
                    pool.wait_ge(pool_chain, links.next())
                    tt(sw[:, 1], tp[:, 0], tp[:, 1], ALU.add).then_inc(xim_made.sem, 1)

                def normalise(S, blk, n):
                    tt(S[:, :, :], S[:, :, :], rden[:, blk, :].rearrange("p (h o) -> p h o", o=1)
                       .to_broadcast([P, HEADS, n]), ALU.mult).then_inc(probs_made.sem, 1)

                pool.wait_ge(proj_read.sem, proj_read.at(l, HH + 1))
                tt(cv_z[:, :, 2:SEQ + 2], cv_c[:, :, :], cv_h[:, :, :], ALU.mult).then_inc(cz_made.sem, 1)
                turn_in(0)
                turn_out(0)
                pool.wait_ge(rden_made.sem, rden_made.at(l, 1))
                normalise(S1, 1, 2 * P)
                turn_in(1)
                normalise(S0, 0, P)
                turn_out(1)
                for q in (2, 3):
                    turn_in(q)
                    turn_out(q)
                norm(l, 1)
                norm(l, 2)
                links.leave()

        @block.vector
        def _(dve):
            links = Chain(DVE_LINKS)
            tt, ts, stt = nc.vector.tensor_tensor, nc.vector.tensor_scalar, nc.vector.scalar_tensor_tensor
            copy = nc.vector.tensor_copy

            def f32(t):
                return t.bitcast(F32)

            def rest(l, k, slot=None):
                s = k % SLOTS if slot is None else slot
                dve.wait_ge(hi_made.sem, hi_made.at(l, k + 1))
                tt(w_lo[s][:, :], raw[s][:, :], f32(w_hi[s][:, :]), ALU.subtract).then_inc(lo_made.sem, 1)

            def hidden(l, n, k, waits=True):
                dve.wait_ge(used.sem, used.at(l, k + 1))
                if waits:
                    dve.wait_ge(h_lo.sem, h_lo.at(l, n - 1))
                dve.wait_ge(silu_made.sem, silu_made.at(l, n))
                tt(hid[:, :, :], act[:, :, :], ps[:, 5, :].rearrange("p (m t) -> p m t", m=2), ALU.mult
                   ).then_inc(h_made.sem, 1)

            def hidden_lo(l, n, buf=0):
                dve.wait_ge(h_hi.sem, h_hi.at(l, n))
                tt(rows_lo[:, buf], hid[:, :, :], f32(rows_hi[:, buf]), ALU.subtract).then_inc(h_lo.sem, 1)

            def ffn(l, f, ahead, between=None):
                k0, s0 = FFN0[f], f * STEPS
                if not ahead:
                    rest(l, k0)
                    rest(l, k0 + 1)
                rest(l, k0 + 2)
                rest(l, k0 + 3)
                hidden(l, s0 + 1, k0 + 1, False)

                def step(i, last):
                    hidden_lo(l, s0 + i)
                    rest(l, k0 + i * 3 + 1, 1)
                    rest(l, k0 + i * 3 + 2, 2)
                    hidden(l, s0 + 1 + i, k0 + i * 3)
                    if not last:
                        rest(l, k0 + i * 3 + 3, 0)

                with dve.Fori(1, STEPS - 1) as i:
                    step(i, False)
                if between:
                    between()
                step(STEPS - 1, True)
                hidden_lo(l, s0 + STEPS, 1)

            def x_rest(l, n, t):
                dve.wait_ge(x_hi.sem, x_hi.at(l, n))
                tok = slice(t * P, t * P + P)
                tt(xT[:, :, 1, tok], xTf[:, :, tok], f32(xT[:, :, 0, tok]), ALU.subtract).then_inc(x_lo.sem, 1)

            def norm(l, norm_, k, scale):
                def normalised(t):
                    if t:
                        dve.wait_ge(used.sem, used.at(l, k + 1))
                    else:
                        dve.wait_ge(acc_done.sem, acc_done.at(l, norm_ + 1))
                    dve.wait_ge(ax_made.sem, ax_made.at(l, norm_ * NT + t + 1 - NT))
                    stt(res[:, t, :], ps[:, 2 * t:2 * t + 2, :].rearrange("p b n -> p (b n)"), scale, ax[:, t, :],
                        ALU.mult, ALU.add).then_inc(res_made.sem, 1)
                    dve.wait_ge(res_made.sem, res_made.at(l, norm_ * NT + t + 1))
                    for h in range(2):
                        last = nc.vector.bn_stats(bnst[:, t, h, :], res[:, t, h * 512:h * 512 + 512])
                    last.then_inc(dve_chain, 1)
                    dve.wait_ge(dve_chain, links.next())
                    dve.sem_inc(carried, 1)
                    nc.vector.bn_aggr(mv[:, t, :], bnst[:, t, :, :]).then_inc(dve_chain, 1)
                    dve.wait_ge(dve_chain, links.next())
                    ts(veps[:, t:t + 1], mv[:, t, 1:2], EPS, None, ALU.add).then_inc(var_made.sem, 1)
                    dve.wait_ge(rstd_made.sem, rstd_made.at(l, norm_ * NT + t + 1))
                    ts(res[:, t, :], res[:, t, :], mv[:, t, 0:1], rstd[:, t:t + 1], ALU.subtract, ALU.mult
                       ).then_inc(xn_made.sem, 1)

                normalised(0)
                normalised(1)
                x_rest(l, norm_ * NT + 1, 0)
                dve.wait_ge(tp_made.sem, tp_made.at(l, norm_ * NT + 2))
                for c in range(4):
                    last = ts(xTf[:, c, P:2 * P], ps[:, 4, c * P:c * P + P],
                              ln_cur[:, 2 * norm_, c:c + 1], ln_cur[:, 2 * norm_ + 1, c:c + 1], ALU.mult, ALU.add)
                last.then_inc(xTf_dve.sem, 1)
                x_rest(l, norm_ * NT + 2, 1)

            dve.wait_ge(small_landed, 16 * 12)
            for g in range(2):
                last = copy(small_rows[ROW_DT:ROW_DT + 16, g * HD:g * HD + HD], dt_rows[:, g:g + 1].to_broadcast([16, HD]))
            last.then_inc(rows_made, 1)
            for t in range(NT):
                dve.wait_ge(tp_made.sem, tp_made.at(0, t + 1 - NT))
                copy(xTf[:, 0:4, t * P:t * P + P], ps[:, 6 - 2 * t, :].rearrange("p (c n) -> p c n", c=4)
                     ).then_inc(xTf_dve.sem, 1)
                x_rest(0, t + 1 - NT, t)
            dve.wait_ge(pro_tp, 1)
            copy(lnT[:, :, :, :].rearrange("p n l c -> p (n l c)"), ps[:, 0, 0:N_LN])
            copy(smallT[:, :], ps[:, 0, P:P + N_SMALL]).then_inc(pro_small, 1)
            with dve.Fori(0, DEPTH) as l:
                links.enter(l)
                rest(l, 0)
                rest(l, 1)
                dve.wait_ge(stat_made, 1)
                dve.wait_ge(pro_small, 1)
                copy(ln_cur[:, :, :], lnT[:, :, bass.ds(l, 1), :].rearrange("p n a c -> p n (a c)"))
                copy(cw_cur[:, :, :].rearrange("p w c -> p (w c)"), smallT[:, bass.ds(l * 6 + ROW_CW, 6)])
                copy(cb_cur[:, :], smallT[:, bass.ds(l * 2 + ROW_CB, 2)])
                copy(d_cur[:, :], smallT[:, bass.ds(l * 2 + ROW_D, 2)])
                copy(st_cur[:, :, :], stat[:, :, bass.ds(l, 1), :].rearrange("p n a t -> p n (a t)")
                     ).then_inc(dve_chain, 1)
                dve.wait_ge(dve_chain, links.next())
                copy(rot_c[:, :, 0], st_cur[:, 1, :])
                copy(rot_s[:, :, 0], st_cur[:, 2, :]).then_inc(cur_made.sem, 1)

                def input_matrices():
                    nc.vector.memset(b_blk[:, :, :, :], 0.0)
                    nc.vector.memset(bTz[:, :, :, :], 0.0).then_inc(zeros_made.sem, 1)
                    dve.wait_ge(cur_made.sem, cur_made.at(l, 1))
                    nc.vector.reciprocal(st_cur[:, 5, :], st_cur[:, 5, :]).then_inc(dve_chain, 1)
                    dve.wait_ge(dve_chain, links.next())
                    over = st_cur[:, 5:6, :].to_broadcast([P, 2, STATE_TILES])
                    tt(st_cur[:, 3:5, :], st_cur[:, 3:5, :], over, ALU.mult).then_inc(dve_chain, 1)
                    dve.wait_ge(dve_chain, links.next())
                    dve.wait_ge(layer_landed.sem, layer_landed.at(l, 7))
                    dve.wait_ge(zeros_made.sem, zeros_made.at(l, 1))
                    prod = [bu[:, i, j, 0:P].rearrange("p (t c) -> p t c", t=STATE_TILES) for i in range(2) for j in range(2)]
                    cre, cim = (st_cur[:, n, :].rearrange("p (t o) -> p t o", o=1).to_broadcast([P, STATE_TILES, 16])
                                for n in (3, 4))
                    tt(prod[0], b_in[:, 0], cre, ALU.mult)
                    tt(prod[1], b_in[:, 1], cim, ALU.mult)
                    tt(prod[2], b_in[:, 1], cre, ALU.mult)
                    tt(prod[3], b_in[:, 0], cim, ALU.mult).then_inc(dve_chain, 1)
                    dve.wait_ge(dve_chain, links.next())
                    for g in range(2):
                        half = slice(HD * g, HD * g + HD)
                        tt(b_blk[half, 0, :, 16 * g:16 * g + 16], prod[0][half], prod[1][half], ALU.subtract)
                        last = tt(b_blk[half, 1, :, 16 * g:16 * g + 16], prod[2][half], prod[3][half], ALU.add)
                    last.then_inc(bblk_made.sem, 1)

                ffn(l, 0, True, input_matrices)
                rest(l, MIX0)
                norm(l, 0, MIX0 - 1, 0.5)
                rest(l, MIX0 + 1)

                def turn_in(q):
                    tl = slice(2 * q, 2 * q + 2)
                    if not q:
                        dve.wait_ge(rot_made.sem, rot_made.at(l, 1))
                    dve.wait_ge(bu_made.sem, bu_made.at(l, q + 1))
                    tt(td[:, 0], bu[:, :, 0, :], rot_c[:, tl, :], ALU.mult)
                    tt(td[:, 1], bu[:, :, 1, :], rot_s[:, tl, :], ALU.mult).then_inc(dve_chain, 1)
                    dve.wait_ge(dve_chain, links.next())
                    if q:
                        dve.wait_ge(c_done.sem, c_done.at(l, q))
                    tt(sw[:, 0], td[:, 0], td[:, 1], ALU.add).then_inc(dve_chain, 1)
                    dve.wait_ge(dve_chain, links.next())

                def scan(q):
                    dve.wait_ge(wim_made.sem, wim_made.at(l, q + 1))
                    for ri in range(2):
                        for t in range(2):
                            last = nc.vector.tensor_tensor_scan(
                                bu[:, t, ri, :], st_cur[:, 0, 2 * q + t:2 * q + t + 1].to_broadcast([P, SEQ]),
                                sw[:, ri, t, :], 0.0, ALU.mult, ALU.add)
                    last.then_inc(z_made.sem, 1)

                def turn_out(q):
                    tl = slice(2 * q, 2 * q + 2)
                    dve.wait_ge(z_made.sem, z_made.at(l, q + 1))
                    tt(td[:, 0], bu[:, :, 0, :], rot_c[:, tl, :], ALU.mult)
                    tt(td[:, 1], bu[:, :, 1, :], rot_s[:, tl, :], ALU.mult).then_inc(dve_chain, 1)
                    dve.wait_ge(dve_chain, links.next())
                    tt(sw[:, 0], td[:, 0], td[:, 1], ALU.subtract).then_inc(xre_made.sem, 1)

                def scaled_scores(S, n, bank, keys):
                    dve.wait_ge(scores_done.sem, scores_done.at(l, n))
                    k = keys.stop - keys.start
                    band = mask[:, keys].rearrange("p (o k) -> p o k", o=1).to_broadcast([P, HEADS, k])
                    src = ps[:, bank:bank + HEADS * k // 512, :].rearrange("p b (h k) -> p (b h) k", k=k)
                    stt(S[:, :, :], src, HD ** -0.5, band, ALU.mult, ALU.add).then_inc(s_made.sem, 1)

                def attn_rest(n, blk):
                    dve.wait_ge(ya_hi.sem, ya_hi.at(l, n))
                    tok = slice(blk * P, blk * P + P)
                    tt(y_attn[:, :, 1, tok], ps[:, 3, :].rearrange("p (m q) -> p m q", m=4),
                       f32(y_attn[:, :, 0, tok]), ALU.subtract).then_inc(ya_lo.sem, 1)

                def branch_sum(j):
                    dve.wait_ge(used.sem, used.at(l, MIX0 + BRANCH[j] + 1))
                    if j:
                        dve.wait_ge(sum_lo.sem, sum_lo.at(l, j))
                    g = gates[:, :, 2 * j:2 * j + 2, :]
                    y = [ps[:, 4 + b, :].rearrange("p (m t) -> p m t", m=2) for b in range(3)]
                    tt(hid[:, :, :], g[:, 0], y[0], ALU.mult).then_inc(br_read.sem, 1)
                    tt(act[:, :, :], g[:, 1], y[1], ALU.mult).then_inc(br_read.sem, 1)
                    dve.wait_ge(br_read.sem, br_read.at(l, 3 * j + 2))
                    tt(hid[:, :, :], hid[:, :, :], act[:, :, :], ALU.add).then_inc(dve_chain, 1)
                    dve.wait_ge(dve_chain, links.next())
                    tt(act[:, :, :], g[:, 2], y[2], ALU.mult).then_inc(br_read.sem, 1)
                    dve.wait_ge(br_read.sem, br_read.at(l, 3 * j + 3))
                    tt(hid[:, :, :], hid[:, :, :], act[:, :, :], ALU.add).then_inc(sum_made.sem, 1)

                def sum_rest(j):
                    dve.wait_ge(sum_hi.sem, sum_hi.at(l, j + 1))
                    tt(rows_lo[:, j % 2], hid[:, :, :], f32(rows_hi[:, j % 2]), ALU.subtract).then_inc(sum_lo.sem, 1)

                def lo(k):
                    rest(l, MIX0 + k)

                for k in range(2, 6):
                    lo(k)
                scaled_scores(S1, 1, 0, slice(0, 2 * P))
                scaled_scores(S0, 2, 6, slice(P, 2 * P))
                dve.wait_ge(s_made.sem, s_made.at(l, 2))
                nc.vector.tensor_reduce(mx[:, 1, :], S1[:, :, :], AX.X, ALU.max)
                lo(6)
                nc.vector.tensor_reduce(mx[:, 0, :], S0[:, :, :], AX.X, ALU.max).then_inc(dve_chain, 1)
                dve.wait_ge(dve_chain, links.next())
                both = sinks[:, :].rearrange("p (o h) -> p o h", o=1).to_broadcast([P, 2, HEADS])
                tt(mx[:, :, :], mx[:, :, :], both, ALU.max).then_inc(dve_chain, 1)
                dve.wait_ge(dve_chain, links.next())
                ts(negm[:, :, :], mx[:, :, :], -1.0, None, ALU.mult).then_inc(dve_chain, 1)
                dve.wait_ge(dve_chain, links.next())
                tt(esink[:, :, :], both, negm[:, :, :], ALU.add).then_inc(negm_made.sem, 1)
                lo(7)
                lo(8)
                turn_in(0)
                scan(0)
                turn_out(0)
                dve.wait_ge(exp_made.sem, exp_made.at(l, 1))
                tt(psum_p[:, :, :], psum_p[:, :, :], esink[:, :, :], ALU.add).then_inc(dve_chain, 1)
                dve.wait_ge(dve_chain, links.next())
                nc.vector.reciprocal(rden[:, :, :], psum_p[:, :, :]).then_inc(rden_made.sem, 1)
                lo(9)
                lo(10)
                turn_in(1)
                scan(1)
                lo(11)
                turn_out(1)
                dve.wait_ge(cz_made.sem, cz_made.at(l, 1))
                dve.wait_ge(proj_read.sem, proj_read.at(l, BB + 1))
                for c in range(2):
                    y = cv_c[:, c, :]
                    ts(y, cv_z[:, c, 0:SEQ], cw_cur[:, 0, c:c + 1], cb_cur[:, c:c + 1], ALU.mult, ALU.add).then_inc(dve_chain, 1)
                    dve.wait_ge(dve_chain, links.next())
                    for w in (1, 2):
                        stt(y, cv_z[:, c, w:w + SEQ], cw_cur[:, w, c:c + 1], y, ALU.mult, ALU.add).then_inc(dve_chain, 1)
                        dve.wait_ge(dve_chain, links.next())
                tt(cv_h[:, :, :], cv_c[:, :, :], cv_b[:, :, :], ALU.mult).then_inc(yc_made.sem, 1)
                lo(12)
                turn_in(2)
                scan(2)
                lo(13)
                turn_out(2)
                attn_rest(1, 1)
                lo(14)
                turn_in(3)
                scan(3)
                lo(15)
                turn_out(3)
                attn_rest(2, 0)
                lo(16)
                dve.wait_ge(yc_hi.sem, yc_hi.at(l, 1))
                tt(y_cs[:, 0:2, 1, :], cv_h[:, :, :], f32(y_cs[:, 0:2, 0, :]), ALU.subtract).then_inc(yc_lo.sem, 1)
                dve.wait_ge(c_done.sem, c_done.at(l, 4))
                for c in range(2):
                    last = stt(td[:, 0, c, :], uT[:, c, :], d_cur[:, c:c + 1], ps[:, 2, c * SEQ:c * SEQ + SEQ],
                               ALU.mult, ALU.add)
                last.then_inc(yd_made.sem, 1)
                lo(17)
                lo(18)
                dve.wait_ge(glu_sig.sem, glu_sig.at(l, 1))
                tt(td[:, 1], sw[:, 0], td[:, 0], ALU.mult).then_inc(ys_made.sem, 1)
                lo(19)
                dve.wait_ge(ys_hi.sem, ys_hi.at(l, 1))
                tt(y_cs[:, 2:4, 1, :], td[:, 1], f32(y_cs[:, 2:4, 0, :]), ALU.subtract).then_inc(ys_lo.sem, 1)
                lo(20)
                lo(21)
                dve.wait_ge(proj_read.sem, proj_read.at(l, PROJ_CHUNKS))
                branch_sum(0)
                lo(22)
                sum_rest(0)
                lo(23)
                branch_sum(1)
                sum_rest(1)
                lo(24)
                lo(25)
                branch_sum(2)
                sum_rest(2)
                lo(26)
                branch_sum(3)
                rest(l, FFN0[1])
                sum_rest(3)
                norm(l, 1, FFN0[1] - 1, 1.0)
                rest(l, FFN0[1] + 1)
                ffn(l, 1, True)
                norm(l, 2, LAYER_CHUNKS - 1, 0.5)
                links.leave()


_INPUTS = ["x", "ffn1_w_gate", "ffn1_w_up", "ffn1_w_down", "ln1_g", "ln1_b", "w_in", "conv_w", "conv_b",
           "ssm_a_re", "ssm_a_im", "ssm_log_dt", "ssm_b_re", "ssm_b_im", "ssm_c_re", "ssm_c_im", "ssm_d",
           "ssm_w_glu", "attn_sinks", "w_br_conv", "w_br_ssm", "w_br_attn", "w_out", "ln2_g", "ln2_b",
           "ffn2_w_gate", "ffn2_w_up", "ffn2_w_down", "ln3_g", "ln3_b"]


def kernel(**inputs):
    import numpy as np
    import concourse.bacc as bacc
    from concourse.bass_utils import run_bass_kernel_spmd

    nc = bacc.Bacc("TRN2", target_bir_lowering=False, num_devices=1)
    arrays, args = {}, []
    for name in _INPUTS:
        a = np.ascontiguousarray(inputs[name])
        arrays[f"in_{name}"] = a
        args.append(nc.dram_tensor(f"in_{name}", a.shape, mybir.dt.from_np(a.dtype), kind="ExternalInput").ap())
    args.append(nc.dram_tensor("out", (1, SEQ, D), F32, kind="ExternalOutput").ap())
    trunk(nc, *args)
    return run_bass_kernel_spmd(nc, [arrays], core_ids=[0]).results[0]["out"]
```

```python
import math
from contextlib import ExitStack

import concourse.bass as bass
from concourse import mybir

F32 = mybir.dt.float32
F32R = mybir.dt.float32r
BF16 = mybir.dt.bfloat16
ALU = mybir.AluOpType
ACT = mybir.ActivationFunctionType
AX = mybir.AxisListType

P = 128
DEPTH, D, SEQ, DFF = 2, 1024, 256, 2816
KC = D // P
NT = SEQ // P
ALPHA = (2 * DEPTH) ** 0.25
EPS = 1e-5
UPPER_FIRST = (4, 5, 6, 7, 0, 1, 2, 3)
SLOTS = 3
CHUNK = 2048
STEPS = DFF // 256
FFN_CHUNKS = 3 * STEPS
PROJ_CHUNKS = 19
MIX_CHUNKS = PROJ_CHUNKS + 8
LAYER_CHUNKS = 2 * FFN_CHUNKS + MIX_CHUNKS
MIX0 = FFN_CHUNKS
FFN0 = (0, FFN_CHUNKS + MIX_CHUNKS)
KV, QA, QB, UU, CC, HH, BB, GATE0 = range(8)
BRANCH = (19, 20, 21, 23)
OUT = (22, 24, 25, 26)
BRANCH_BANKS = ((0, 1, 2), (4, 5, 6), (7, 4, 5), (4, 5, 6))
OFF_B, OFF_C, OFF_H, OFF_U, OFF_Q, OFF_K, OFF_G = 0, 256, 512, 768, 1024, 1536, 1792
HD, HEADS = 64, 8
STATE_TILES = 8
MASKED = -3.0e38
TWO_PI_A = 6.28125
TWO_PI_B = 1.934051513671875e-3
TWO_PI = 2 * math.pi
TWO_PI_C = TWO_PI - TWO_PI_A - TWO_PI_B
ROUND = 1.5 * 2.0 ** 23
DMAS = [1] * LAYER_CHUNKS
for _k in (QA, QB):
    DMAS[MIX0 + _k] = 4
for _k in BRANCH:
    DMAS[MIX0 + _k] = 4
LANDED = [16 * sum(DMAS[_j] for _j in range(_k % SLOTS, _k + 1, SLOTS)) for _k in range(LAYER_CHUNKS)]
LANDED_LAYER = [16 * sum(DMAS[_s::SLOTS]) for _s in range(SLOTS)]
N_LN = 96
ROW_ARE, ROW_AIM, ROW_DT, ROW_CW, ROW_CB, ROW_D, N_SMALL = 0, 16, 32, 48, 60, 64, 68


POOL_LINKS, DVE_LINKS = 76, 59


class Events:

    def __init__(self, sem, layer, before=0, unit=1):
        self.sem, self.layer, self.before, self.unit = sem, layer, before, unit

    def at(self, l, n):
        return l * (self.layer * self.unit) + (n + self.before) * self.unit


class Chain:

    def __init__(self, layer):
        self.layer, self.n, self.base = layer, 0, 0

    def enter(self, l):
        self.before = self.n
        self.base = l * self.layer

    def leave(self):
        assert self.n - self.before == self.layer, (self.n - self.before, self.layer)
        self.base = self.layer * (DEPTH - 1)

    def next(self):
        self.n += 1
        return self.base + self.n


def trunk(nc, x, ffn1_w_gate, ffn1_w_up, ffn1_w_down, ln1_g, ln1_b, w_in, conv_w, conv_b,
          ssm_a_re, ssm_a_im, ssm_log_dt, ssm_b_re, ssm_b_im, ssm_c_re, ssm_c_im, ssm_d,
          ssm_w_glu, attn_sinks, w_br_conv, w_br_ssm, w_br_attn, w_out, ln2_g, ln2_b,
          ffn2_w_gate, ffn2_w_up, ffn2_w_down, ln3_g, ln3_b, out):
    ctx = ExitStack()
    with ctx:
        def sb(name, shape, dt=F32):
            return ctx.enter_context(nc.sbuf_tensor(name, shape, dt))

        def overlay(first, second):
            size = [sum(4 * math.prod(shape[1:]) for _, shape, _ in s) for s in (first, second)]
            held, brief = (second, first) if size[1] >= size[0] else (first, second)
            with ExitStack() as own:
                over = [own.enter_context(nc.sbuf_tensor(*a)) for a in brief]
            kept = [sb(*a) for a in held]
            return over + kept if held is second else kept + over

        raw = [sb(f"raw{s}", [P, CHUNK]) for s in range(SLOTS)]
        w_hi = [sb(f"w_hi{s}", [P, CHUNK], F32R) for s in range(SLOTS)]
        w_lo = [sb(f"w_lo{s}", [P, CHUNK], F32R) for s in range(SLOTS)]
        xT = sb("xT", [P, KC, 2, SEQ], F32R)
        ax = sb("ax", [P, NT, D])
        gates, res, xTf, gb = overlay(
            [("gates", [P, 3, KC, SEQ], F32)],
            [("res", [P, NT, D], F32), ("xTf", [P, KC, SEQ], F32), ("gb", [P, 2, D], F32)])
        probsT, rows_hi, rows_lo = overlay(
            [("probsT", [P, 2 * HEADS, P], F32)],
            [("rows_hi", [P, 2, 2, SEQ], F32R), ("rows_lo", [P, 2, 2, SEQ], F32R)])
        S1, y_attn = overlay([("S1", [P, HEADS, 2 * P], F32)], [("y_attn", [P, 4, 2, SEQ], F32R)])
        S0, b_in, b_blk, c_in = overlay(
            [("S0", [P, HEADS, P], F32)],
            [("b_in", [P, 2, STATE_TILES, 16], F32), ("b_blk", [P, 2, STATE_TILES, 32], F32),
             ("c_in", [P, 2, 2, 2, HD], F32)])
        bTz, y_cs = overlay([("bTz", [P, STATE_TILES, 2, P], F32)], [("y_cs", [P, 4, 2, SEQ], F32R)])
        td, act, hid = overlay([("td", [P, 2, 2, SEQ], F32)], [("act", [P, 2, SEQ], F32), ("hid", [P, 2, SEQ], F32)])
        qT, cv_c, cv_h = overlay([("qT", [P, 4, SEQ], F32)], [("cv_c", [P, 2, SEQ], F32), ("cv_h", [P, 2, SEQ], F32)])
        kz = sb("kz", [P, 2, SEQ])
        vz = sb("vz", [P, 2, 2, P])
        mask = sb("mask", [P, 2 * P])
        sinks = sb("sinks", [P, HEADS])
        mx = sb("mx", [P, 2, HEADS])
        negm = sb("negm", [P, 2, HEADS])
        esink = sb("esink", [P, 2, HEADS])
        psum_p = sb("psum_p", [P, 2, HEADS])
        rden = sb("rden", [P, 2, HEADS])
        rot_c = sb("rot_c", [P, STATE_TILES, SEQ])
        rot_s = sb("rot_s", [P, STATE_TILES, SEQ])
        bu = sb("bu", [P, 2, 2, SEQ])
        sw = sb("sw", [P, 2, 2, SEQ])
        tp = sb("tp", [P, 2, 2, SEQ])
        k_tok = sw[:, 0, :, 0:P]
        uT = sb("uT", [P, 2, SEQ])
        cTz = sb("cTz", [P, STATE_TILES, 2, P])
        cv_b, w_glu = overlay([("cv_b", [P, 2, SEQ], F32)], [("w_glu", [P, 2, 256], F32)])
        cv_z = sb("cv_z", [P, 2, SEQ + 2])
        ln_rows = td[:, 0].rearrange("p a t -> p (a t)")[0:N_LN, 0:P]
        small_rows = td[:, 1].rearrange("p a t -> p (a t)")[0:N_SMALL, 0:P]
        dt_rows = td[:, 1].rearrange("p a t -> p (a t)")[ROW_DT:ROW_DT + 16, P:P + 2]
        lnT = sb("lnT", [P, 6, DEPTH, KC])
        smallT = sb("smallT", [P, N_SMALL])
        sc, bnst, mv, veps, rstd = overlay(
            [("sc", [P, 7, STATE_TILES], F32)],
            [("bnst", [P, NT, 2, 6], F32), ("mv", [P, NT, 2], F32), ("veps", [P, NT], F32), ("rstd", [P, NT], F32)])
        ln_cur = sb("ln_cur", [P, 6, KC])
        in_cur = sb("in_cur", [P, 3, STATE_TILES])
        st_cur = sb("st_cur", [P, 5, STATE_TILES])
        cw_cur = sb("cw_cur", [P, 3, 2])
        cb_cur = sb("cb_cur", [P, 2])
        d_cur = sb("d_cur", [P, 2])
        ident = sb("ident", [P, P])
        zero_b = sb("zero_b", [P, 512], BF16)
        powers = sb("powers", [P, 2])
        mhalf, alpha = powers[:, 0:1], powers[:, 1:2]

        ps = ctx.enter_context(nc.psum_tensor("ps", [P, 8, 512], F32))
        acc = ps[:, 0:4, :].rearrange("p (t h) n -> p t h n", t=NT)

        def sem(name):
            return ctx.enter_context(nc.semaphore(name))

        x_landed, small_landed, out_stored = sem("x_landed"), sem("small_landed"), sem("out_stored")
        landed = [sem(f"landed{s}") for s in range(SLOTS)]
        layer_landed = Events(sem("layer_landed"), 7, unit=16)
        glu_landed = Events(sem("glu_landed"), 1, unit=16)
        zeros_made = Events(sem("zeros_made"), 1)
        gb_landed = Events(sem("gb_landed"), 6, before=1, unit=16)
        consts_made = sem("consts_made")
        rows_made, pro_tp, pro_small = (
            sem("rows_made"), sem("pro_tp"), sem("pro_small"))
        hi_made = Events(sem("hi_made"), LAYER_CHUNKS)
        lo_made = Events(sem("lo_made"), LAYER_CHUNKS, before=SLOTS)
        used = Events(sem("used"), LAYER_CHUNKS, before=SLOTS)
        silu_made = Events(sem("silu_made"), 2 * STEPS)
        h_made = Events(sem("h_made"), 2 * STEPS)
        h_hi = Events(sem("h_hi"), 2 * STEPS)
        h_lo = Events(sem("h_lo"), 2 * STEPS)
        res_made = Events(sem("res_made"), 3 * NT, before=NT)
        var_made = Events(sem("var_made"), 3 * NT)
        rstd_made = Events(sem("rstd_made"), 3 * NT)
        xn_made = Events(sem("xn_made"), 3 * 3, before=3)
        tp_made = Events(sem("tp_made"), 3 * NT, before=NT)
        tp_upper = Events(sem("tp_upper"), 3 * NT, before=NT)
        xTf_dve = Events(sem("xTf_dve"), 3, before=1)
        xTf_act = Events(sem("xTf_act"), 3 * 3, before=3)
        x_hi = Events(sem("x_hi"), 3 * 4, before=4)
        x_lo = Events(sem("x_lo"), 3 * 4, before=4)
        x_made = Events(sem("x_made"), 3 * NT, before=NT)
        out_made = [sem(f"out_made{t}") for t in range(NT)]
        acc_done = Events(sem("acc_done"), 3 * 2)
        ax_made = Events(sem("ax_made"), 3 * NT, before=NT)
        in_made = Events(sem("in_made"), 1)
        state_act = Events(sem("state_act"), 4)
        state_dve = Events(sem("state_dve"), 2)
        coef_made = Events(sem("coef_made"), 2)
        cur_made = Events(sem("cur_made"), 1)
        bblk_made = Events(sem("bblk_made"), 1)
        bcT_done = Events(sem("bcT_done"), 1)
        bcT_made = Events(sem("bcT_made"), 1)
        rot_made = Events(sem("rot_made"), 1)
        kT_done = Events(sem("kT_done"), 1)
        kz_made = Events(sem("kz_made"), 1)
        proj_read = Events(sem("proj_read"), PROJ_CHUNKS)
        scores_done = Events(sem("scores_done"), 2)
        s_made = Events(sem("s_made"), 2)
        negm_made = Events(sem("negm_made"), 1)
        exp_made = Events(sem("exp_made"), 1)
        rden_made = Events(sem("rden_made"), 1)
        probs_made = Events(sem("probs_made"), 2)
        pT_done = Events(sem("pT_done"), 6)
        pT_made = Events(sem("pT_made"), 6)
        pv_done = Events(sem("pv_done"), 2)
        ya_hi = Events(sem("ya_hi"), 2)
        ya_lo = Events(sem("ya_lo"), 2)
        bu_done = Events(sem("bu_done"), 4)
        bu_made = Events(sem("bu_made"), 4)
        wim_made = Events(sem("wim_made"), 4)
        z_made = Events(sem("z_made"), 4)
        xre_made = Events(sem("xre_made"), 4)
        xim_made = Events(sem("xim_made"), 4)
        c_done = Events(sem("c_done"), 4)
        yd_made = Events(sem("yd_made"), 1)
        gelu_made = Events(sem("gelu_made"), 1)
        glu_done = Events(sem("glu_done"), 1)
        glu_sig = Events(sem("glu_sig"), 1)
        ys_made = Events(sem("ys_made"), 1)
        ys_hi = Events(sem("ys_hi"), 1)
        ys_lo = Events(sem("ys_lo"), 1)
        cz_made = Events(sem("cz_made"), 1)
        yc_made = Events(sem("yc_made"), 1)
        yc_hi = Events(sem("yc_hi"), 1)
        yc_lo = Events(sem("yc_lo"), 1)
        br_read = Events(sem("br_read"), 12)
        sum_made = Events(sem("sum_made"), 4)
        sum_hi = Events(sem("sum_hi"), 4)
        sum_lo = Events(sem("sum_lo"), 4)
        carried = sem("carried")
        dve_chain, pool_chain = sem("dve_chain"), sem("pool_chain")

        def cols(slot):
            return slot[:, :].rearrange("p (c n) -> p c n", c=KC)

        def wide(slot):
            return slot[:, :].rearrange("p (c n) -> p c n", c=2)

        block = ctx.enter_context(nc.Block())

        @block.sync
        def _(sp):
            sp.dma_start(res[:, :, :], x[0].rearrange("(t p) d -> p t d", p=P)).then_inc(x_landed, 16)
            sp.sem_inc(lo_made.sem, SLOTS)
            sp.sem_inc(used.sem, SLOTS)
            sp.wait_ge(small_landed, 16 * 12)
            def load(l, k, parts, slot=None):
                slot = k % SLOTS if slot is None else slot
                sp.wait_ge(lo_made.sem, lo_made.at(l, k - SLOTS + 1))
                sp.sem_inc(carried, 1)
                for dst, src in parts(raw[slot]):
                    sp.dma_start(dst, src).then_inc(landed[slot], 16)

            def at_layer(w, l):
                return w[bass.ds(l, 1)].rearrange("a r n -> (a r) n")

            def columns(w, l, c0):
                return lambda r: [(cols(r), at_layer(w, l).rearrange("(c p) n -> p c n", p=P)[:, :, bass.ds(c0, 256)])]

            def rows(w, l, r0):
                return lambda r: [(wide(r), at_layer(w, l)[bass.ds(r0, 256)].rearrange("(c p) n -> p c n", p=P))]

            def load_norm(l, g, b):
                for n, v in enumerate((g, b)):
                    sp.dma_start(gb[:, n, :], v[bass.ds(l, 1)].to_broadcast([P, D])).then_inc(gb_landed.sem, 16)

            def load_ffn(l, f, w_gate, w_up, w_down, after_two, after_step, before_last):
                k0 = FFN0[f]
                load(l, k0, columns(w_gate, l, 0))
                load(l, k0 + 1, columns(w_up, l, 0))
                after_two()
                load(l, k0 + 2, columns(w_gate, l, 256))
                load(l, k0 + 3, columns(w_up, l, 256))
                load(l, k0 + 4, rows(w_down, l, 0))
                after_step()
                with sp.Fori(2, STEPS) as i:
                    load(l, k0 + i * 3 - 1, columns(w_gate, l, i * 256), 2)
                    load(l, k0 + i * 3, columns(w_up, l, i * 256), 0)
                    load(l, k0 + i * 3 + 1, rows(w_down, l, i * 256 - 256), 1)
                before_last()
                load(l, k0 + FFN_CHUNKS - 1, rows(w_down, l, DFF - 256))

            def q_columns(l, a):
                def parts(r):
                    src = at_layer(w_in, l).rearrange("(c p) n -> p c n", p=P)
                    for m in range(2):
                        for hf in range(2):
                            c0, to = OFF_Q + (4 * hf + 2 * a + m) * HD, (2 * m + hf) * HD
                            yield cols(r)[:, :, to:to + HD], src[:, :, c0:c0 + HD]
                return parts

            def branch_columns(l, j):
                def parts(r):
                    n = slice(256 * j, 256 * j + 256)
                    yield cols(r)[:, 0:2, :], at_layer(w_br_conv, l).rearrange("(c p) n -> p c n", p=P)[:, :, n]
                    yield cols(r)[:, 2:4, :], at_layer(w_br_ssm, l).rearrange("(c p) n -> p c n", p=P)[:, :, n]
                    for hf in range(2):
                        src = at_layer(w_br_attn, l)[hf * 256:hf * 256 + 256]
                        yield cols(r)[hf * HD:hf * HD + HD, 4:8, :], src.rearrange("(m p) n -> p m n", p=HD)[:, :, n]
                return parts

            with sp.Fori(0, DEPTH) as l:
                def params_and_norm1():
                    sp.wait_ge(ax_made.sem, ax_made.at(l, 0))
                    small = layer_landed.sem
                    for n, v in enumerate((ssm_b_re, ssm_b_im)):
                        sp.dma_start(b_in[:, n], v[bass.ds(l, 1)].rearrange(
                            "a (t g) s c -> (a g s) t c", g=2)).then_inc(small, 16)
                    for n, v in enumerate((ssm_c_re, ssm_c_im)):
                        for twice in range(2):
                            sp.dma_start(c_in[:, :, n, twice, :], v[bass.ds(l, 1)].rearrange(
                                "a (u g) c s -> (a g c) u s", u=2)).then_inc(small, 16)
                    sp.dma_start(sinks[:, :], attn_sinks[bass.ds(l, 1)].to_broadcast([P, HEADS])).then_inc(small, 16)
                    load_norm(l, ln1_g, ln1_b)

                def nothing():
                    pass

                load_ffn(l, 0, ffn1_w_gate, ffn1_w_up, ffn1_w_down, nothing, params_and_norm1, nothing)
                for k, c0 in ((KV, OFF_K), (QA, None), (QB, None), (UU, OFF_U), (CC, OFF_C), (HH, OFF_H), (BB, OFF_B)):
                    load(l, MIX0 + k, q_columns(l, k - QA) if c0 is None else columns(w_in, l, c0))
                for g in range(12):
                    load(l, MIX0 + GATE0 + g, columns(w_in, l, OFF_G + 256 * g))
                    if g == 7:
                        sp.wait_ge(yc_made.sem, yc_made.at(l, 1))
                        sp.dma_start(w_glu[:, :, :], at_layer(ssm_w_glu, l).rearrange(
                            "(c p) n -> p c n", p=P)).then_inc(glu_landed.sem, 16)
                for k in range(PROJ_CHUNKS, MIX_CHUNKS):
                    if k in BRANCH:
                        load(l, MIX0 + k, branch_columns(l, BRANCH.index(k)))
                    else:
                        load(l, MIX0 + k, rows(w_out, l, 256 * OUT.index(k)))

                def norm2():
                    sp.wait_ge(sum_made.sem, sum_made.at(l, 4))
                    load_norm(l, ln2_g, ln2_b)

                def norm3():
                    sp.wait_ge(ax_made.sem, ax_made.at(l, 2 * NT))
                    load_norm(l, ln3_g, ln3_b)
                load_ffn(l, 1, ffn2_w_gate, ffn2_w_up, ffn2_w_down, norm2, nothing, norm3)

            for t in (1, 0):
                sp.wait_ge(out_made[t], 2 - t)
                sp.dma_start(out[0, t * P:t * P + P, :], res[:, t, :]).then_inc(out_stored, 16)
            sp.wait_ge(out_stored, 16 * NT)

        @block.tensor
        def _(pe):
            mm = nc.tensor.matmul

            def take(l, k):
                pe.wait_ge(lo_made.sem, lo_made.at(l, k + 1))

            def project(slot, bank, l=None, fresh=None):
                h, w = cols(w_hi[slot]), cols(w_lo[slot])
                for m in range(2):
                    o = ps[:, bank, m * SEQ:m * SEQ + SEQ]
                    for i, c in enumerate(UPPER_FIRST):
                        if fresh is not None and m == 0 and c in (4, 0):
                            pe.wait_ge(x_lo.sem, x_lo.at(l, 4 * fresh - (1 if c else 0)))
                        n = slice(m * P, m * P + P)
                        mm(o, h[:, c, n], xT[:, c, 0, :], start=i == 0, stop=False)
                        mm(o, h[:, c, n], xT[:, c, 1, :], start=False, stop=False)
                        last = mm(o, w[:, c, n], xT[:, c, 0, :], start=False, stop=i == KC - 1)
                last.then_inc(used.sem, 1)

            def accumulate(slot, buf, start=False, stop=False, tiles=range(NT), halves=((0, 1),)):
                h, w = wide(w_hi[slot]), wide(w_lo[slot])
                for t in tiles:
                    for half in halves:
                        for c in range(2):
                            tok = slice(t * P, t * P + P)
                            for left, right, first in ((rows_hi, h, True), (rows_hi, w, False), (rows_lo, h, False)):
                                for n in half:
                                    last = mm(acc[:, t, n, :], left[:, buf, c, tok], right[:, c, n * 512:n * 512 + 512],
                                              start=start and first and c == 0,
                                              stop=stop and left is rows_lo and c == 1, skip_group_check=True)
                        if half == (0,):
                            last.then_inc(acc_done.sem, 1)
                return last

            def transposes(l, norm, t, src):
                b = 6 - 2 * t
                for c in UPPER_FIRST:
                    if c == 4:
                        pe.wait_ge(xn_made.sem, xn_made.at(l, norm * 3 + t + 1))
                    elif t and c == 0:
                        pe.wait_ge(xn_made.sem, xn_made.at(l, norm * 3 + 3))
                    last = nc.tensor.transpose(ps[:, b + c // 4, (c % 4) * P:(c % 4) * P + P],
                                               src[:, t, c * P:c * P + P], ident[:, :])
                    if c == KC - 1:
                        last.then_inc(tp_upper.sem, 1)
                last.then_inc(tp_made.sem, 1)

            def open_acc(l, n):
                pe.wait_ge(res_made.sem, res_made.at(l, n))
                for t in range(NT):
                    for h in range(2):
                        mm(acc[:, t, h, :], zero_b[:, 0:P], zero_b[:, :], start=True, stop=False,
                           skip_group_check=True)

            def ffn(l, f, norm):
                k0, s0 = FFN0[f], f * STEPS
                take(l, k0)
                project(0, 4, l, norm)
                take(l, k0 + 1)
                project(1, 5)

                def step(i):
                    take(l, k0 + i * 3 - 1)
                    pe.wait_ge(silu_made.sem, silu_made.at(l, s0 + i))
                    project(2, 4)
                    take(l, k0 + i * 3)
                    pe.wait_ge(h_made.sem, h_made.at(l, s0 + i))
                    project(0, 5)
                    take(l, k0 + i * 3 + 1)
                    pe.wait_ge(h_lo.sem, h_lo.at(l, s0 + i))

                with pe.Fori(1, STEPS - 1) as i:
                    step(i)
                    accumulate(1, 0).then_inc(used.sem, 1)
                step(STEPS - 1)
                accumulate(1, 0, tiles=(0,))
                take(l, k0 + FFN_CHUNKS - 1)
                pe.wait_ge(h_lo.sem, h_lo.at(l, s0 + STEPS))
                accumulate(2, 1, stop=True, tiles=(0,)).then_inc(acc_done.sem, 1)
                accumulate(1, 0, tiles=(1,)).then_inc(used.sem, 1)
                accumulate(2, 1, stop=True, tiles=(1,), halves=((0,), (1,))).then_inc(used.sem, 1)

            def norm_transposes(l, norm):
                for t in range(NT):
                    transposes(l, norm, t, res)

            pe.wait_ge(consts_made, 1)
            pe.wait_ge(small_landed, 16 * 12)
            pe.wait_ge(rows_made, 1)
            nc.tensor.transpose(ps[:, 0, 0:N_LN], ln_rows, ident[0:N_LN, 0:N_LN])
            nc.tensor.transpose(ps[:, 0, P:P + N_SMALL], small_rows, ident[0:N_SMALL, 0:N_SMALL]).then_inc(pro_tp, 1)

            with pe.Fori(0, DEPTH) as l:
                norm_transposes(l, -1)
                pe.wait_ge(pro_small, 1)
                open_acc(l, 0)
                ffn(l, 0, 0)
                transposes(l, 0, 0, res)
                pe.wait_ge(bblk_made.sem, bblk_made.at(l, 1))
                pe.wait_ge(layer_landed.sem, layer_landed.at(l, 7))
                for u in range(2):
                    for ri in range(2):
                        n = (2 * u + ri) * P
                        nc.tensor.transpose(ps[:, 0, n:n + P], b_blk[:, ri, 4 * u:4 * u + 4, :], ident[:, :])
                        last = nc.tensor.transpose(ps[:, 1, n:n + P], c_in[:, u, ri, :, :], ident[:, :])
                last.then_inc(bcT_done.sem, 1)
                transposes(l, 0, 1, res)
                def chunk(k):
                    take(l, MIX0 + k)
                    if k >= 2:
                        pe.wait_ge(proj_read.sem, proj_read.at(l, k - 1))
                    if k != KV:
                        project((MIX0 + k) % SLOTS, 4 + k % 2)

                def project_kv(slot):
                    h, w = cols(w_hi[slot]), cols(w_lo[slot])
                    for t in range(NT):
                        o = ps[:, 2 + t, 0:SEQ]
                        tok = slice(t * P, t * P + P)
                        for i, c in enumerate(UPPER_FIRST):
                            if c in (4, 0):
                                pe.wait_ge(x_lo.sem, x_lo.at(l, 2 * t + (1 if c else 2)))
                            mm(o, xT[:, c, 0, tok], h[:, c, :], start=i == 0, stop=False)
                            mm(o, xT[:, c, 0, tok], w[:, c, :], start=False, stop=False)
                            last = mm(o, xT[:, c, 1, tok], h[:, c, :], start=False, stop=i == KC - 1)
                    last.then_inc(used.sem, 1)

                def input_states(q):
                    if q >= 1:
                        pe.wait_ge(bu_made.sem, bu_made.at(l, q))
                    for t in range(2 * q, 2 * q + 2):
                        for ri in range(2):
                            last = mm(ps[:, t % 2, ri * SEQ:ri * SEQ + SEQ], bTz[:, t, ri, :], uT[:, t // 4, :],
                                      start=True, stop=True)
                    last.then_inc(bu_done.sem, 1)

                def output_states(q):
                    pe.wait_ge(xre_made.sem, xre_made.at(l, q + 1))
                    pe.wait_ge(xim_made.sem, xim_made.at(l, q + 1))
                    ct = q // 2
                    for t in range(2 * q, 2 * q + 2):
                        for ri in range(2):
                            last = mm(ps[:, 2, ct * SEQ:ct * SEQ + SEQ], cTz[:, t, ri, :], sw[:, ri, t % 2, :],
                                      start=t % 4 == 0 and ri == 0, stop=t % 4 == 3 and ri == 1)
                    last.then_inc(c_done.sem, 1)

                def transpose_probs(S, parts, g0, first):
                    for g in range(parts):
                        if g0 + g >= 2:
                            pe.wait_ge(pT_made.sem, pT_made.at(l, g0 + g - 1))
                        b = 6 + (g0 + g) % 2
                        for n in range(4):
                            i = 4 * g + n
                            src = S[:, i // 2, (i % 2) * P:(i % 2) * P + P] if parts == 4 else S[:, i, :]
                            last = nc.tensor.transpose(ps[:, b, n * P:n * P + P], src, ident[:, :])
                        last.then_inc(pT_done.sem, 1)

                def attend(blk):
                    pe.wait_ge(pT_made.sem, pT_made.at(l, 4 if blk else 6))
                    for m in range(4):
                        terms = [(j, kb) for j in range(2) for kb in range(blk + 1)]
                        for n, (j, kb) in enumerate(terms):
                            head = m + 4 * j
                            i = 2 * head + kb if blk else head
                            last = mm(ps[:, 3, m * P:m * P + P], vz[:, kb, j, :], probsT[:, i, :],
                                      start=n == 0, stop=n == len(terms) - 1)
                    last.then_inc(pv_done.sem, 1)

                chunk(KV)
                project_kv((MIX0 + KV) % SLOTS)
                chunk(QA)
                pe.wait_ge(proj_read.sem, proj_read.at(l, 1))
                for t in range(NT):
                    last = nc.tensor.transpose(ps[:, 2, t * P:t * P + P], k_tok[:, t, :], ident[:, :])
                last.then_inc(kT_done.sem, 1)
                chunk(QB)
                chunk(UU)
                pe.wait_ge(proj_read.sem, proj_read.at(l, QB + 1))
                pe.wait_ge(bcT_made.sem, bcT_made.at(l, 1))
                pe.wait_ge(kz_made.sem, kz_made.at(l, 1))
                for head in range(HEADS):
                    last = mm(ps[:, head // 2, (head % 2) * SEQ:(head % 2) * SEQ + SEQ],
                              qT[:, head % 4, P:2 * P], kz[:, head // 4, :], start=True, stop=True)
                last.then_inc(scores_done.sem, 1)
                for head in range(HEADS):
                    last = mm(ps[:, 6 + head // 4, (head % 4) * P:(head % 4) * P + P],
                              qT[:, head % 4, 0:P], kz[:, head // 4, 0:P], start=True, stop=True)
                last.then_inc(scores_done.sem, 1)
                chunk(CC)
                chunk(HH)
                pe.wait_ge(s_made.sem, s_made.at(l, 2))
                input_states(0)
                chunk(BB)
                chunk(7)
                input_states(1)
                chunk(8)
                output_states(0)
                chunk(9)
                input_states(2)
                pe.wait_ge(probs_made.sem, probs_made.at(l, 1))
                transpose_probs(S1, 4, 0, 0)
                chunk(10)
                output_states(1)
                attend(1)
                chunk(11)
                input_states(3)
                pe.wait_ge(probs_made.sem, probs_made.at(l, 2))
                transpose_probs(S0, 2, 4, 16)
                chunk(12)
                output_states(2)
                pe.wait_ge(ya_lo.sem, ya_lo.at(l, 1))
                attend(0)
                chunk(13)
                chunk(14)
                output_states(3)
                chunk(15)
                pe.wait_ge(gelu_made.sem, gelu_made.at(l, 1))
                pe.wait_ge(glu_landed.sem, glu_landed.at(l, 1))
                for co in range(2):
                    for c in range(2):
                        last = mm(ps[:, 0, co * SEQ:co * SEQ + SEQ], w_glu[:, c, co * P:co * P + P], sw[:, 0, c, :],
                                  start=c == 0, stop=c == 1)
                last.then_inc(glu_done.sem, 1)
                chunk(16)
                chunk(17)
                chunk(18)

                def branch(j):
                    k = MIX0 + BRANCH[j]
                    take(l, k)
                    h, w = cols(w_hi[k % SLOTS]), cols(w_lo[k % SLOTS])
                    for b, (y, kc, yc) in enumerate(((y_cs, (0, 1), 0), (y_cs, (2, 3), 0), (y_attn, (4, 5, 6, 7), 4))):
                        if j == 0:
                            y_lo = (yc_lo, ys_lo, ya_lo)[b]
                            pe.wait_ge(y_lo.sem, y_lo.at(l, 2 if b == 2 else 1))
                        elif j == 1 and b < 2:
                            pe.wait_ge(proj_read.sem, proj_read.at(l, PROJ_CHUNKS))
                        elif j == 2 and b:
                            pe.wait_ge(br_read.sem, br_read.at(l, 3 + b))
                        elif j == 3:
                            pe.wait_ge(br_read.sem, br_read.at(l, 8 if b == 0 else 9))
                        for m in range(2):
                            o = ps[:, BRANCH_BANKS[j][b], m * SEQ:m * SEQ + SEQ]
                            n = slice(m * P, m * P + P)
                            for c in kc:
                                mm(o, h[:, c, n], y[:, c - yc, 0, :], start=c == kc[0], stop=False)
                                mm(o, h[:, c, n], y[:, c - yc, 1, :], start=False, stop=False)
                                last = mm(o, w[:, c, n], y[:, c - yc, 0, :], start=False, stop=c == kc[-1])
                    last.then_inc(used.sem, 1)

                def output(j, tiles=range(NT), halves=((0, 1),)):
                    k = MIX0 + OUT[j]
                    take(l, k)
                    pe.wait_ge(sum_lo.sem, sum_lo.at(l, j + 1))
                    return accumulate(k % SLOTS, j % 2, start=j == 0, stop=j == 3, tiles=tiles, halves=halves)

                branch(0)
                branch(1)
                branch(2)
                pe.wait_ge(br_read.sem, br_read.at(l, 3))
                output(0).then_inc(used.sem, 1)
                branch(3)
                output(1).then_inc(used.sem, 1)
                output(2, (0,))
                output(3, (0,)).then_inc(acc_done.sem, 1)
                output(2, (1,)).then_inc(used.sem, 1)
                output(3, (1,), ((0,), (1,))).then_inc(used.sem, 1)
                norm_transposes(l, 1)
                open_acc(l, 2 * NT)
                ffn(l, 1, 2)

        @block.scalar
        def _(sc_):
            act_ = nc.scalar.activation

            def split(l, k, slot=None, land=None):
                s = k % SLOTS if slot is None else slot
                n = LANDED[k] if land is None else land
                sc_.wait_ge(landed[s], l * LANDED_LAYER[s] + n)
                sc_.wait_ge(used.sem, used.at(l, k - SLOTS + 1))
                nc.scalar.copy(w_hi[s][:, :], raw[s][:, :]).then_inc(hi_made.sem, 1)

            def silu(l, n, k):
                sc_.wait_ge(used.sem, used.at(l, k + 1))
                act_(act[:, :, :], ps[:, 4, :].rearrange("p (m t) -> p m t", m=2), ACT.Silu).then_inc(silu_made.sem, 1)

            def hidden_hi(l, n, k, buf=0):
                sc_.wait_ge(h_made.sem, h_made.at(l, n))
                sc_.wait_ge(used.sem, used.at(l, k + 1))
                nc.scalar.copy(rows_hi[:, buf], hid[:, :, :]).then_inc(h_hi.sem, 1)

            def discretise(l):
                sc_.wait_ge(in_made.sem, in_made.at(l, 1))
                act_(sc[:, 0, :], in_cur[:, 2, :], ACT.Exp).then_inc(state_act.sem, 1)
                sc_.wait_ge(state_dve.sem, state_dve.at(l, 1))
                act_(st_cur[:, 0], sc[:, 1, :], ACT.Exp).then_inc(state_act.sem, 1)
                sc_.wait_ge(state_dve.sem, state_dve.at(l, 2))
                act_(st_cur[:, 2], sc[:, 2, :], ACT.Sin).then_inc(state_act.sem, 1)
                act_(sc[:, 3, :], sc[:, 2, :], ACT.Sin, scale=0.5).then_inc(state_act.sem, 1)

            def ffn(l, f, ahead):
                k0, s0 = FFN0[f], f * STEPS
                if not ahead:
                    split(l, k0)
                    split(l, k0 + 1)
                split(l, k0 + 2)
                silu(l, 1, k0)
                split(l, k0 + 3)

                def step(i, last):
                    hidden_hi(l, s0 + i, k0 + i * 3 - 2)
                    split(l, k0 + i * 3 + 1, 1, LANDED[k0 + 1] + i * 16)
                    silu(l, i + 1, k0 + i * 3 - 1)
                    split(l, k0 + i * 3 + 2, 2, LANDED[k0 + 2] + i * 16)
                    if not last:
                        split(l, k0 + i * 3 + 3, 0, LANDED[k0] + i * 16 + 16)

                step(1, False)
                if not f:
                    discretise(l)
                with sc_.Fori(2, STEPS - 1) as i:
                    step(i, False)
                step(STEPS - 1, True)
                hidden_hi(l, s0 + STEPS, k0 + FFN_CHUNKS - 3, 1)

            def x_split(ks, t):
                tok = slice(t * P, t * P + P)
                nc.scalar.copy(xT[:, ks, 0, tok], xTf[:, ks, tok]).then_inc(x_hi.sem, 1)

            def norm(l, norm_, between=None):
                def evacuate(t, ks, n):
                    for c in ks:
                        last = act_(xTf[:, c, t * P:t * P + P], ps[:, 6 - 2 * t + c // 4, (c % 4) * P:(c % 4 + 1) * P],
                                    ACT.Identity, scale=ln_cur[:, 2 * (norm_ % 3), c:c + 1],
                                    bias=ln_cur[:, 2 * (norm_ % 3) + 1, c:c + 1])
                    last.then_inc(xTf_act.sem, 1)
                    sc_.wait_ge(xTf_act.sem, xTf_act.at(l, norm_ * 3 + n))
                    x_split(slice(ks[0], ks[-1] + 1), t)

                sc_.wait_ge(tp_upper.sem, tp_upper.at(l, norm_ * NT + 1))
                evacuate(0, range(4, KC), 1)
                sc_.wait_ge(tp_made.sem, tp_made.at(l, norm_ * NT + 1))
                evacuate(0, range(4), 2)
                if between:
                    between()
                sc_.wait_ge(tp_upper.sem, tp_upper.at(l, norm_ * NT + 2))
                evacuate(1, range(4, KC), 3)
                sc_.wait_ge(xTf_dve.sem, xTf_dve.at(l, norm_ + 1))
                x_split(slice(0, 4), 1)

            dma = nc.scalar.dma_start
            dma(dt_rows[:, :], ssm_log_dt.rearrange("l (t g) -> (l t) g", g=2)).then_inc(small_landed, 16)
            for row, v in ((ROW_ARE, ssm_a_re), (ROW_AIM, ssm_a_im)):
                dma(small_rows[row:row + 16, :],
                    v.rearrange("l (t g) s -> (l t) (g s)", g=2)).then_inc(small_landed, 16)
            dma(small_rows[ROW_CW:ROW_CW + 12, :],
                conv_w.rearrange("l w (c p) -> (l w c) p", p=P)).then_inc(small_landed, 16)
            for row, v in ((ROW_CB, conv_b), (ROW_D, ssm_d)):
                dma(small_rows[row:row + 4, :], v.rearrange("l (c p) -> (l c) p", p=P)).then_inc(small_landed, 16)
            for n, v in enumerate((ln1_g, ln1_b, ln2_g, ln2_b, ln3_g, ln3_b)):
                dma(ln_rows[16 * n:16 * n + 16, :], v.rearrange("l (c p) -> (l c) p", p=P)).then_inc(small_landed, 16)
            sc_.wait_ge(consts_made, 1)

            with sc_.Fori(0, DEPTH) as l:
                norm(l, -1, lambda: split(l, 0))
                split(l, 1)
                ffn(l, 0, True)
                split(l, MIX0)
                split(l, MIX0 + 1)
                norm(l, 0)
                def bank(k):
                    return ps[:, 4 + k % 2, :]

                def read(k, dst):
                    sc_.wait_ge(used.sem, used.at(l, MIX0 + k + 1))
                    nc.scalar.copy(dst, bank(k).rearrange("p (m t) -> p m t", m=2)).then_inc(proj_read.sem, 1)

                def gate(k):
                    sc_.wait_ge(used.sem, used.at(l, MIX0 + k + 1))
                    g = k - GATE0
                    act_(gates[:, g // 4, 2 * (g % 4):2 * (g % 4) + 2, :], bank(k).rearrange("p (m t) -> p m t", m=2),
                         ACT.Sigmoid).then_inc(proj_read.sem, 1)

                def states(q):
                    sc_.wait_ge(bu_done.sem, bu_done.at(l, q + 1))
                    if q:
                        sc_.wait_ge(xre_made.sem, xre_made.at(l, q))
                        sc_.wait_ge(xim_made.sem, xim_made.at(l, q))
                    nc.scalar.copy(bu[:, :, :, :], ps[:, 0:2, :].rearrange("p b (r t) -> p b r t", r=2)
                                   ).then_inc(bu_made.sem, 1)

                def probs_out(g0, n):
                    for g in range(g0, g0 + n):
                        sc_.wait_ge(pT_done.sem, pT_done.at(l, g + 1))
                        i = 4 * (g - g0)
                        nc.scalar.copy(probsT[:, i:i + 4, :], ps[:, 6 + g % 2, :].rearrange("p (c n) -> p c n", c=4)
                                       ).then_inc(pT_made.sem, 1)

                def attn_hi(n, blk):
                    sc_.wait_ge(pv_done.sem, pv_done.at(l, n))
                    nc.scalar.copy(y_attn[:, :, 0, blk * P:blk * P + P], ps[:, 3, :].rearrange("p (m q) -> p m q", m=4)
                                   ).then_inc(ya_hi.sem, 1)

                split(l, MIX0 + 2)
                sc_.wait_ge(used.sem, used.at(l, MIX0 + KV + 1))
                kv = ps[:, 2:4, 0:SEQ]
                nc.scalar.copy(k_tok, kv[:, :, 0:P])
                nc.scalar.copy(vz[:, :, 0, 0:HD], kv[:, :, P:P + HD])
                nc.scalar.copy(vz[:, :, 1, HD:P], kv[:, :, P + HD:2 * P]).then_inc(proj_read.sem, 1)
                split(l, MIX0 + 3)
                sc_.wait_ge(bcT_done.sem, bcT_done.at(l, 1))
                b_ps = ps[:, 0, :].rearrange("p (u r s) -> p u r s", u=2, r=2)
                c_ps = ps[:, 1, :].rearrange("p (u r q h c) -> p u r q h c", u=2, r=2, q=4, h=2)
                for q in range(4):
                    rows_ = slice(32 * q, 32 * q + 32)
                    nc.scalar.copy(bTz[rows_, q::4, :, :], b_ps[rows_])
                for u in range(2):
                    for q in range(4):
                        for h in range(2):
                            half, n = slice(HD * h, HD * h + HD), 32 * q + 16 * h
                            nc.scalar.copy(cTz[half, 4 * u + q, 0, n:n + 16], c_ps[half, u, 0, q, h, :])
                            last = nc.scalar.mul(cTz[half, 4 * u + q, 1, n:n + 16], c_ps[half, u, 1, q, h, :], -1.0)
                last.then_inc(bcT_made.sem, 1)
                sc_.wait_ge(kT_done.sem, kT_done.at(l, 1))
                nc.scalar.copy(kz[0:HD, 0, :], ps[0:HD, 2, 0:SEQ])
                nc.scalar.copy(kz[HD:P, 1, :], ps[HD:P, 2, 0:SEQ]).then_inc(kz_made.sem, 1)
                read(QA, qT[:, 0:2, :])
                split(l, MIX0 + 4)
                read(QB, qT[:, 2:4, :])
                split(l, MIX0 + 5)
                read(UU, uT[:, :, :])
                split(l, MIX0 + 6)
                read(CC, cv_c[:, :, :])
                split(l, MIX0 + 7)
                sc_.wait_ge(negm_made.sem, negm_made.at(l, 1))
                for blk, S in ((1, S1), (0, S0)):
                    for head in range(HEADS):
                        act_(S[:, head, :], S[:, head, :], ACT.Exp, bias=negm[:, blk, head:head + 1],
                             accum_out=psum_p[:, blk, head:head + 1])
                    if blk:
                        read(HH, cv_h[:, :, :])
                        split(l, MIX0 + 8)
                        states(0)
                act_(esink[:, :, :], esink[:, :, :], ACT.Exp).then_inc(exp_made.sem, 1)
                sc_.wait_ge(ax_made.sem, ax_made.at(l, NT))
                read(BB, cv_b[:, :, :])
                split(l, MIX0 + 9)
                gate(7)
                split(l, MIX0 + 10)
                states(1)
                gate(8)
                split(l, MIX0 + 11)
                gate(9)
                split(l, MIX0 + 12)
                probs_out(0, 4)
                states(2)
                gate(10)
                split(l, MIX0 + 13)
                attn_hi(1, 1)
                gate(11)
                split(l, MIX0 + 14)
                probs_out(4, 2)
                gate(12)
                split(l, MIX0 + 15)
                states(3)
                attn_hi(2, 0)
                gate(13)
                split(l, MIX0 + 16)
                sc_.wait_ge(yc_made.sem, yc_made.at(l, 1))
                nc.scalar.copy(y_cs[:, 0:2, 0, :], cv_h[:, :, :]).then_inc(yc_hi.sem, 1)
                gate(14)
                split(l, MIX0 + 17)
                sc_.wait_ge(yd_made.sem, yd_made.at(l, 1))
                act_(sw[:, 0], td[:, 0], ACT.Gelu_apprx_tanh).then_inc(gelu_made.sem, 1)
                gate(15)
                split(l, MIX0 + 18)
                sc_.wait_ge(glu_done.sem, glu_done.at(l, 1))
                act_(td[:, 0], ps[:, 0, :].rearrange("p (m t) -> p m t", m=2), ACT.Sigmoid).then_inc(glu_sig.sem, 1)
                gate(16)
                split(l, MIX0 + 19)
                sc_.wait_ge(ys_made.sem, ys_made.at(l, 1))
                nc.scalar.copy(y_cs[:, 2:4, 0, :], td[:, 1]).then_inc(ys_hi.sem, 1)
                gate(17)
                split(l, MIX0 + 20)
                gate(18)
                split(l, MIX0 + 21)

                def sum_hi_(j):
                    sc_.wait_ge(sum_made.sem, sum_made.at(l, j + 1))
                    if j >= 2:
                        sc_.wait_ge(used.sem, used.at(l, MIX0 + OUT[j - 2] + 1))
                    nc.scalar.copy(rows_hi[:, j % 2], hid[:, :, :]).then_inc(sum_hi.sem, 1)
                split(l, MIX0 + 22)
                sum_hi_(0)
                split(l, MIX0 + 23)
                sum_hi_(1)
                split(l, MIX0 + 24)
                sum_hi_(2)
                split(l, MIX0 + 25)
                split(l, MIX0 + 26)
                sum_hi_(3)
                split(l, FFN0[1])
                split(l, FFN0[1] + 1)
                norm(l, 1)
                ffn(l, 1, True)

        @block.gpsimd
        def _(pool):
            links = Chain(POOL_LINKS)
            tt, memset = nc.gpsimd.tensor_tensor, nc.gpsimd.memset

            for tile in (ident[:, :], mask[:, :], zero_b[:, :], kz[:, :, :], vz[:, :, :, :],
                         cTz[:, :, :, :], cv_z[:, :, :]):
                memset(tile, 0.0).then_inc(pool_chain, 1)
                pool.wait_ge(pool_chain, links.next())
            memset(mhalf[:, :], -0.5).then_inc(pool_chain, 1)
            pool.wait_ge(pool_chain, links.next())
            nc.gpsimd.affine_select(out=ident[:, :], in_=ident[:, :], compare_op=ALU.not_equal, fill=1.0,
                                    base=0, pattern=[[-1, P]], channel_multiplier=1).then_inc(pool_chain, 1)
            pool.wait_ge(pool_chain, links.next())
            nc.gpsimd.affine_select(out=mask[:, :], in_=mask[:, :], compare_op=ALU.is_ge, fill=MASKED,
                                    base=-1, pattern=[[1, 2 * P]], channel_multiplier=-1).then_inc(pool_chain, 1)
            pool.wait_ge(pool_chain, links.next())
            nc.gpsimd.affine_select(out=mask[:, :], in_=mask[:, :], compare_op=ALU.is_ge, fill=MASKED,
                                    base=P, pattern=[[-1, 2 * P]], channel_multiplier=1).then_inc(pool_chain, 1)
            pool.wait_ge(pool_chain, links.next())
            for tile, value in ((ln_cur[:, 4, :], 1.0), (ln_cur[:, 5, :], 0.0), (alpha[:, :], ALPHA)):
                memset(tile, value).then_inc(pool_chain, 1)
                pool.wait_ge(pool_chain, links.next())
            pool.sem_inc(consts_made, 1)
            pool.wait_ge(x_landed, 16)
            pool.sem_inc(xn_made.sem, 3)
            pool.sem_inc(res_made.sem, NT)
            for n, value in ((0, 1.0), (1, 0.0)):
                memset(gb[:, n, :], value).then_inc(pool_chain, 1)
                pool.wait_ge(pool_chain, links.next())
            pool.sem_inc(gb_landed.sem, 16)

            def deviations(l, norm_):
                for t in range(NT):
                    pool.wait_ge(var_made.sem, var_made.at(l, norm_ * NT + t + 1))
                    tt(rstd[:, t:t + 1], veps[:, t:t + 1], mhalf[:, :], ALU.pow).then_inc(rstd_made.sem, 1)

            def apply(l, norm_):
                pool.wait_ge(gb_landed.sem, gb_landed.at(l, 2 * norm_ + 2))
                for t in range(NT):
                    pool.wait_ge(tp_made.sem, tp_made.at(l, norm_ * NT + t + 1))
                    tt(res[:, t, :], res[:, t, :], gb[:, 0, :], ALU.mult).then_inc(pool_chain, 1)
                    pool.wait_ge(pool_chain, links.next())
                    tt(res[:, t, :], res[:, t, :], gb[:, 1, :], ALU.add).then_inc(x_made.sem, 1)
                for t in range(NT):
                    pool.wait_ge(x_made.sem, x_made.at(l, norm_ * NT + t + 1))
                    tt(ax[:, t, :], res[:, t, :], alpha[:, :].to_broadcast([P, D]), ALU.mult).then_inc(ax_made.sem, 1)

            with pool.Fori(0, DEPTH) as l:
                links.enter(l)
                apply(l, -1)
                pool.wait_ge(cur_made.sem, cur_made.at(l, 1))
                n = 1
                while n < SEQ:
                    k = min(STATE_TILES, 512 // n)
                    for t in range(0, STATE_TILES, k):
                        tl = slice(t, t + k)
                        c, s = rot_c[:, tl, 0:n], rot_s[:, tl, 0:n]
                        cn = rot_c[:, tl, n - 1:n].to_broadcast([P, k, n])
                        sn = rot_s[:, tl, n - 1:n].to_broadcast([P, k, n])
                        t0, t1 = (tp[:, i].rearrange("p a t -> p (a t)")[:, 0:k * n].rearrange("p (k n) -> p k n", k=k)
                                  for i in range(2))
                        tt(t0, c, cn, ALU.mult).then_inc(pool_chain, 1)
                        pool.wait_ge(pool_chain, links.next())
                        tt(t1, s, sn, ALU.mult).then_inc(pool_chain, 1)
                        pool.wait_ge(pool_chain, links.next())
                        tt(rot_c[:, tl, n:2 * n], t0, t1, ALU.subtract).then_inc(pool_chain, 1)
                        pool.wait_ge(pool_chain, links.next())
                        tt(t0, s, cn, ALU.mult).then_inc(pool_chain, 1)
                        pool.wait_ge(pool_chain, links.next())
                        tt(t1, c, sn, ALU.mult).then_inc(pool_chain, 1)
                        pool.wait_ge(pool_chain, links.next())
                        tt(rot_s[:, tl, n:2 * n], t0, t1, ALU.add).then_inc(pool_chain, 1)
                        pool.wait_ge(pool_chain, links.next())
                    n *= 2
                pool.sem_inc(rot_made.sem, 1)
                deviations(l, 0)
                apply(l, 0)

                def turn_in(q):
                    tl = slice(2 * q, 2 * q + 2)
                    pool.wait_ge(bu_made.sem, bu_made.at(l, q + 1))
                    tt(tp[:, 0], bu[:, :, 1, :], rot_c[:, tl, :], ALU.mult).then_inc(pool_chain, 1)
                    pool.wait_ge(pool_chain, links.next())
                    tt(tp[:, 1], bu[:, :, 0, :], rot_s[:, tl, :], ALU.mult).then_inc(pool_chain, 1)
                    pool.wait_ge(pool_chain, links.next())
                    if q:
                        pool.wait_ge(c_done.sem, c_done.at(l, q))
                    tt(sw[:, 1], tp[:, 0], tp[:, 1], ALU.subtract).then_inc(wim_made.sem, 1)

                def turn_out(q):
                    tl = slice(2 * q, 2 * q + 2)
                    pool.wait_ge(z_made.sem, z_made.at(l, q + 1))
                    tt(tp[:, 0], bu[:, :, 0, :], rot_s[:, tl, :], ALU.mult).then_inc(pool_chain, 1)
                    pool.wait_ge(pool_chain, links.next())
                    tt(tp[:, 1], bu[:, :, 1, :], rot_c[:, tl, :], ALU.mult).then_inc(pool_chain, 1)
                    pool.wait_ge(pool_chain, links.next())
                    tt(sw[:, 1], tp[:, 0], tp[:, 1], ALU.add).then_inc(xim_made.sem, 1)

                def normalise(S, blk, n):
                    tt(S[:, :, :], S[:, :, :], rden[:, blk, :].rearrange("p (h o) -> p h o", o=1)
                       .to_broadcast([P, HEADS, n]), ALU.mult).then_inc(probs_made.sem, 1)

                pool.wait_ge(proj_read.sem, proj_read.at(l, HH + 1))
                tt(cv_z[:, :, 2:SEQ + 2], cv_c[:, :, :], cv_h[:, :, :], ALU.mult).then_inc(cz_made.sem, 1)
                turn_in(0)
                turn_out(0)
                pool.wait_ge(rden_made.sem, rden_made.at(l, 1))
                normalise(S1, 1, 2 * P)
                turn_in(1)
                normalise(S0, 0, P)
                turn_out(1)
                for q in (2, 3):
                    turn_in(q)
                    turn_out(q)
                deviations(l, 1)
                apply(l, 1)
                deviations(l, 2)
                links.leave()

            pool.wait_ge(gb_landed.sem, gb_landed.at(DEPTH, 0))
            pool.wait_ge(xn_made.sem, xn_made.at(DEPTH, -2))
            low = slice(0, D // 2)
            tt(res[:, 0, low], res[:, 0, low], gb[:, 0, low], ALU.mult).then_inc(pool_chain, 1)
            pool.wait_ge(pool_chain, links.next())
            tt(res[:, 0, low], res[:, 0, low], gb[:, 1, low], ALU.add).then_inc(out_made[0], 1)

        @block.vector
        def _(dve):
            links = Chain(DVE_LINKS)
            tt, ts, stt = nc.vector.tensor_tensor, nc.vector.tensor_scalar, nc.vector.scalar_tensor_tensor
            copy = nc.vector.tensor_copy

            def f32(t):
                return t.bitcast(F32)

            def rest(l, k, slot=None):
                s = k % SLOTS if slot is None else slot
                dve.wait_ge(hi_made.sem, hi_made.at(l, k + 1))
                tt(w_lo[s][:, :], raw[s][:, :], f32(w_hi[s][:, :]), ALU.subtract).then_inc(lo_made.sem, 1)

            def hidden(l, n, k, waits=True):
                dve.wait_ge(used.sem, used.at(l, k + 1))
                if waits:
                    dve.wait_ge(h_lo.sem, h_lo.at(l, n - 1))
                dve.wait_ge(silu_made.sem, silu_made.at(l, n))
                tt(hid[:, :, :], act[:, :, :], ps[:, 5, :].rearrange("p (m t) -> p m t", m=2), ALU.mult
                   ).then_inc(h_made.sem, 1)

            def hidden_lo(l, n, buf=0):
                dve.wait_ge(h_hi.sem, h_hi.at(l, n))
                tt(rows_lo[:, buf], hid[:, :, :], f32(rows_hi[:, buf]), ALU.subtract).then_inc(h_lo.sem, 1)

            def ffn(l, f, ahead, early=None, late=None):
                k0, s0 = FFN0[f], f * STEPS
                if not ahead:
                    rest(l, k0)
                    rest(l, k0 + 1)
                rest(l, k0 + 2)
                rest(l, k0 + 3)
                hidden(l, s0 + 1, k0 + 1, False)

                def step(i, last):
                    hidden_lo(l, s0 + i)
                    rest(l, k0 + i * 3 + 1, 1)
                    rest(l, k0 + i * 3 + 2, 2)
                    hidden(l, s0 + 1 + i, k0 + i * 3)
                    if not last:
                        rest(l, k0 + i * 3 + 3, 0)

                step(1, False)
                if early:
                    early()
                with dve.Fori(2, STEPS - 1) as i:
                    step(i, False)
                if late:
                    late()
                step(STEPS - 1, True)
                hidden_lo(l, s0 + STEPS, 1)

            def x_rest(l, n, ks, t):
                dve.wait_ge(x_hi.sem, x_hi.at(l, n))
                tok = slice(t * P, t * P + P)
                tt(xT[:, ks, 1, tok], xTf[:, ks, tok], f32(xT[:, ks, 0, tok]), ALU.subtract).then_inc(x_lo.sem, 1)

            def norm(l, norm_, k, scale):
                def residual(t, ns):
                    dve.wait_ge(ax_made.sem, ax_made.at(l, norm_ * NT + t + 1 - NT))
                    at = slice(512 * ns.start, 512 * ns.stop)
                    return stt(res[:, t, at], ps[:, 2 * t + ns.start:2 * t + ns.stop, :].rearrange("p b n -> p (b n)"),
                               scale, ax[:, t, at], ALU.mult, ALU.add)

                def stats(t, h):
                    return nc.vector.bn_stats(bnst[:, t, h, :], res[:, t, h * 512:h * 512 + 512])

                def deviation(t):
                    dve.wait_ge(dve_chain, links.next())
                    dve.sem_inc(carried, 1)
                    nc.vector.bn_aggr(mv[:, t, :], bnst[:, t, :, :]).then_inc(dve_chain, 1)
                    dve.wait_ge(dve_chain, links.next())
                    ts(veps[:, t:t + 1], mv[:, t, 1:2], EPS, None, ALU.add).then_inc(var_made.sem, 1)
                    dve.wait_ge(rstd_made.sem, rstd_made.at(l, norm_ * NT + t + 1))

                def normalise(t, at):
                    ts(res[:, t, at], res[:, t, at], mv[:, t, 0:1], rstd[:, t:t + 1], ALU.subtract, ALU.mult
                       ).then_inc(xn_made.sem, 1)

                dve.wait_ge(acc_done.sem, acc_done.at(l, 2 * norm_ + 1))
                residual(0, slice(0, 2)).then_inc(res_made.sem, 1)
                dve.wait_ge(res_made.sem, res_made.at(l, norm_ * NT + 1))
                stats(0, 0)
                stats(0, 1).then_inc(dve_chain, 1)
                deviation(0)
                normalise(0, slice(0, D))
                dve.wait_ge(acc_done.sem, acc_done.at(l, 2 * norm_ + 2))
                residual(1, slice(0, 1)).then_inc(dve_chain, 1)
                dve.wait_ge(dve_chain, links.next())
                stats(1, 0)
                dve.wait_ge(used.sem, used.at(l, k + 1))
                residual(1, slice(1, 2)).then_inc(res_made.sem, 1)
                dve.wait_ge(res_made.sem, res_made.at(l, norm_ * NT + 2))
                stats(1, 1).then_inc(dve_chain, 1)
                deviation(1)
                normalise(1, slice(D // 2, D))
                normalise(1, slice(0, D // 2))

            def turned(l, norm_, between=None):
                x_rest(l, norm_ * 4 + 1, slice(4, KC), 0)
                x_rest(l, norm_ * 4 + 2, slice(0, 4), 0)
                dve.wait_ge(tp_made.sem, tp_made.at(l, norm_ * NT + 2))
                for c in range(4):
                    last = ts(xTf[:, c, P:2 * P], ps[:, 4, c * P:c * P + P],
                              ln_cur[:, 2 * (norm_ % 3), c:c + 1], ln_cur[:, 2 * (norm_ % 3) + 1, c:c + 1],
                              ALU.mult, ALU.add)
                last.then_inc(xTf_dve.sem, 1)
                if between:
                    between()
                x_rest(l, norm_ * 4 + 3, slice(4, KC), 1)
                x_rest(l, norm_ * 4 + 4, slice(0, 4), 1)

            dve.wait_ge(small_landed, 16 * 12)
            for g in range(2):
                last = copy(small_rows[ROW_DT:ROW_DT + 16, g * HD:g * HD + HD], dt_rows[:, g:g + 1].to_broadcast([16, HD]))
            last.then_inc(rows_made, 1)
            dve.wait_ge(pro_tp, 1)
            copy(lnT[:, :, :, :].rearrange("p n l c -> p (n l c)"), ps[:, 0, 0:N_LN])
            copy(smallT[:, :], ps[:, 0, P:P + N_SMALL]).then_inc(pro_small, 1)
            dve.wait_ge(pro_small, 1)

            with dve.Fori(0, DEPTH) as l:
                links.enter(l)
                turned(l, -1, lambda: rest(l, 0))
                rest(l, 1)
                copy(ln_cur[:, :, :], lnT[:, :, bass.ds(l, 1), :].rearrange("p n a c -> p n (a c)"))
                copy(cw_cur[:, :, :].rearrange("p w c -> p (w c)"), smallT[:, bass.ds(l * 6 + ROW_CW, 6)])
                copy(cb_cur[:, :], smallT[:, bass.ds(l * 2 + ROW_CB, 2)])
                copy(d_cur[:, :], smallT[:, bass.ds(l * 2 + ROW_D, 2)])
                states = smallT[:, 0:ROW_CW].rearrange("p (n l t) -> p n l t", n=3, l=DEPTH)
                copy(in_cur[:, :, :], states[:, :, bass.ds(l, 1), :].rearrange("p n a t -> p n (a t)")
                     ).then_inc(in_made.sem, 1)

                def discretise():
                    lr, li = in_cur[:, 0, :], in_cur[:, 1, :]
                    mag, cos, sin, coef_r, coef_i = (st_cur[:, n, :] for n in range(5))

                    def after(instruction):
                        instruction.then_inc(dve_chain, 1)
                        return links.next()

                    dve.wait_ge(state_act.sem, state_act.at(l, 1))
                    dve.wait_ge(in_made.sem, in_made.at(l, 1))
                    tt(sc[:, 1, :], lr, sc[:, 0, :], ALU.mult).then_inc(state_dve.sem, 1)
                    dve.wait_ge(dve_chain, after(tt(sc[:, 4, :], li, sc[:, 0, :], ALU.mult)))
                    dve.wait_ge(dve_chain, after(ts(sc[:, 5, :], sc[:, 4, :], 1.0 / TWO_PI, ROUND, ALU.mult, ALU.add)))
                    dve.wait_ge(dve_chain, after(ts(sc[:, 5, :], sc[:, 5, :], ROUND, None, ALU.subtract)))
                    for part in (TWO_PI_A, TWO_PI_B, TWO_PI_C):
                        dve.wait_ge(dve_chain, after(
                            stt(sc[:, 4, :], sc[:, 5, :], -part, sc[:, 4, :], ALU.mult, ALU.add)))
                    ts(sc[:, 2, :], sc[:, 4, :], 3.1415925, -3.1415925, ALU.min, ALU.max).then_inc(state_dve.sem, 1)
                    tt(sc[:, 5, :], lr, lr, ALU.mult)
                    dve.wait_ge(dve_chain, after(tt(sc[:, 6, :], li, li, ALU.mult)))
                    dve.wait_ge(dve_chain, after(tt(sc[:, 5, :], sc[:, 5, :], sc[:, 6, :], ALU.add)))
                    dve.wait_ge(dve_chain, after(nc.vector.reciprocal(sc[:, 4, :], sc[:, 5, :])))
                    dve.wait_ge(state_act.sem, state_act.at(l, 4))
                    dve.wait_ge(dve_chain, after(tt(sc[:, 5, :], sc[:, 3, :], sc[:, 3, :], ALU.mult)))
                    dve.wait_ge(dve_chain, after(ts(cos, sc[:, 5, :], -2.0, 1.0, ALU.mult, ALU.add)))
                    copy(rot_c[:, :, 0], cos)
                    copy(rot_s[:, :, 0], sin).then_inc(cur_made.sem, 1)
                    tt(sc[:, 6, :], mag, sin, ALU.mult)
                    dve.wait_ge(dve_chain, after(tt(sc[:, 5, :], mag, cos, ALU.mult)))
                    dve.wait_ge(dve_chain, after(ts(sc[:, 5, :], sc[:, 5, :], 1.0, None, ALU.subtract)))
                    for o, a, b, op in ((coef_r, 5, 6, ALU.add), (coef_i, 6, 5, ALU.subtract)):
                        tt(sc[:, 0, :], sc[:, a, :], lr, ALU.mult)
                        dve.wait_ge(dve_chain, after(tt(sc[:, 1, :], sc[:, b, :], li, ALU.mult)))
                        dve.wait_ge(dve_chain, after(tt(sc[:, 0, :], sc[:, 0, :], sc[:, 1, :], op)))
                        tt(o, sc[:, 0, :], sc[:, 4, :], ALU.mult).then_inc(coef_made.sem, 1)
                        if o is coef_r:
                            dve.wait_ge(coef_made.sem, coef_made.at(l, 1))

                def input_matrices():
                    nc.vector.memset(b_blk[:, :, :, :], 0.0)
                    nc.vector.memset(bTz[:, :, :, :], 0.0).then_inc(zeros_made.sem, 1)
                    dve.wait_ge(coef_made.sem, coef_made.at(l, 2))
                    dve.wait_ge(layer_landed.sem, layer_landed.at(l, 7))
                    dve.wait_ge(zeros_made.sem, zeros_made.at(l, 1))
                    prod = [bu[:, i, j, 0:P].rearrange("p (t c) -> p t c", t=STATE_TILES) for i in range(2) for j in range(2)]
                    cre, cim = (st_cur[:, n, :].rearrange("p (t o) -> p t o", o=1).to_broadcast([P, STATE_TILES, 16])
                                for n in (3, 4))
                    tt(prod[0], b_in[:, 0], cre, ALU.mult)
                    tt(prod[1], b_in[:, 1], cim, ALU.mult)
                    tt(prod[2], b_in[:, 1], cre, ALU.mult)
                    tt(prod[3], b_in[:, 0], cim, ALU.mult).then_inc(dve_chain, 1)
                    dve.wait_ge(dve_chain, links.next())
                    for g in range(2):
                        half = slice(HD * g, HD * g + HD)
                        tt(b_blk[half, 0, :, 16 * g:16 * g + 16], prod[0][half], prod[1][half], ALU.subtract)
                        last = tt(b_blk[half, 1, :, 16 * g:16 * g + 16], prod[2][half], prod[3][half], ALU.add)
                    last.then_inc(bblk_made.sem, 1)

                ffn(l, 0, True, discretise, input_matrices)
                rest(l, MIX0)
                norm(l, 0, MIX0 - 1, 0.5)
                turned(l, 0)
                rest(l, MIX0 + 1)

                def turn_in(q):
                    tl = slice(2 * q, 2 * q + 2)
                    if not q:
                        dve.wait_ge(rot_made.sem, rot_made.at(l, 1))
                    dve.wait_ge(bu_made.sem, bu_made.at(l, q + 1))
                    tt(td[:, 0], bu[:, :, 0, :], rot_c[:, tl, :], ALU.mult)
                    tt(td[:, 1], bu[:, :, 1, :], rot_s[:, tl, :], ALU.mult).then_inc(dve_chain, 1)
                    dve.wait_ge(dve_chain, links.next())
                    if q:
                        dve.wait_ge(c_done.sem, c_done.at(l, q))
                    tt(sw[:, 0], td[:, 0], td[:, 1], ALU.add).then_inc(dve_chain, 1)
                    dve.wait_ge(dve_chain, links.next())

                def scan(q):
                    dve.wait_ge(wim_made.sem, wim_made.at(l, q + 1))
                    for ri in range(2):
                        for t in range(2):
                            last = nc.vector.tensor_tensor_scan(
                                bu[:, t, ri, :], st_cur[:, 0, 2 * q + t:2 * q + t + 1].to_broadcast([P, SEQ]),
                                sw[:, ri, t, :], 0.0, ALU.mult, ALU.add)
                    last.then_inc(z_made.sem, 1)

                def turn_out(q):
                    tl = slice(2 * q, 2 * q + 2)
                    dve.wait_ge(z_made.sem, z_made.at(l, q + 1))
                    tt(td[:, 0], bu[:, :, 0, :], rot_c[:, tl, :], ALU.mult)
                    tt(td[:, 1], bu[:, :, 1, :], rot_s[:, tl, :], ALU.mult).then_inc(dve_chain, 1)
                    dve.wait_ge(dve_chain, links.next())
                    tt(sw[:, 0], td[:, 0], td[:, 1], ALU.subtract).then_inc(xre_made.sem, 1)

                def scaled_scores(S, n, bank, keys):
                    dve.wait_ge(scores_done.sem, scores_done.at(l, n))
                    k = keys.stop - keys.start
                    band = mask[:, keys].rearrange("p (o k) -> p o k", o=1).to_broadcast([P, HEADS, k])
                    src = ps[:, bank:bank + HEADS * k // 512, :].rearrange("p b (h k) -> p (b h) k", k=k)
                    stt(S[:, :, :], src, HD ** -0.5, band, ALU.mult, ALU.add).then_inc(s_made.sem, 1)

                def attn_rest(n, blk):
                    dve.wait_ge(ya_hi.sem, ya_hi.at(l, n))
                    tok = slice(blk * P, blk * P + P)
                    tt(y_attn[:, :, 1, tok], ps[:, 3, :].rearrange("p (m q) -> p m q", m=4),
                       f32(y_attn[:, :, 0, tok]), ALU.subtract).then_inc(ya_lo.sem, 1)

                def branch_sum(j):
                    dve.wait_ge(used.sem, used.at(l, MIX0 + BRANCH[j] + 1))
                    if j:
                        dve.wait_ge(sum_lo.sem, sum_lo.at(l, j))
                    g = gates[:, :, 2 * j:2 * j + 2, :]
                    y = [ps[:, b, :].rearrange("p (m t) -> p m t", m=2) for b in BRANCH_BANKS[j]]
                    tt(hid[:, :, :], g[:, 0], y[0], ALU.mult).then_inc(br_read.sem, 1)
                    tt(act[:, :, :], g[:, 1], y[1], ALU.mult).then_inc(br_read.sem, 1)
                    dve.wait_ge(br_read.sem, br_read.at(l, 3 * j + 2))
                    tt(hid[:, :, :], hid[:, :, :], act[:, :, :], ALU.add).then_inc(dve_chain, 1)
                    dve.wait_ge(dve_chain, links.next())
                    tt(act[:, :, :], g[:, 2], y[2], ALU.mult).then_inc(br_read.sem, 1)
                    dve.wait_ge(br_read.sem, br_read.at(l, 3 * j + 3))
                    tt(hid[:, :, :], hid[:, :, :], act[:, :, :], ALU.add).then_inc(sum_made.sem, 1)

                def sum_rest(j):
                    dve.wait_ge(sum_hi.sem, sum_hi.at(l, j + 1))
                    tt(rows_lo[:, j % 2], hid[:, :, :], f32(rows_hi[:, j % 2]), ALU.subtract).then_inc(sum_lo.sem, 1)

                def lo(k):
                    rest(l, MIX0 + k)

                for k in range(2, 6):
                    lo(k)
                scaled_scores(S1, 1, 0, slice(0, 2 * P))
                scaled_scores(S0, 2, 6, slice(P, 2 * P))
                dve.wait_ge(s_made.sem, s_made.at(l, 2))
                nc.vector.tensor_reduce(mx[:, 1, :], S1[:, :, :], AX.X, ALU.max)
                lo(6)
                nc.vector.tensor_reduce(mx[:, 0, :], S0[:, :, :], AX.X, ALU.max).then_inc(dve_chain, 1)
                dve.wait_ge(dve_chain, links.next())
                both = sinks[:, :].rearrange("p (o h) -> p o h", o=1).to_broadcast([P, 2, HEADS])
                tt(mx[:, :, :], mx[:, :, :], both, ALU.max).then_inc(dve_chain, 1)
                dve.wait_ge(dve_chain, links.next())
                ts(negm[:, :, :], mx[:, :, :], -1.0, None, ALU.mult).then_inc(dve_chain, 1)
                dve.wait_ge(dve_chain, links.next())
                tt(esink[:, :, :], both, negm[:, :, :], ALU.add).then_inc(negm_made.sem, 1)
                lo(7)
                lo(8)
                turn_in(0)
                scan(0)
                turn_out(0)
                dve.wait_ge(exp_made.sem, exp_made.at(l, 1))
                tt(psum_p[:, :, :], psum_p[:, :, :], esink[:, :, :], ALU.add).then_inc(dve_chain, 1)
                dve.wait_ge(dve_chain, links.next())
                nc.vector.reciprocal(rden[:, :, :], psum_p[:, :, :]).then_inc(rden_made.sem, 1)
                lo(9)
                lo(10)
                turn_in(1)
                scan(1)
                lo(11)
                turn_out(1)
                dve.wait_ge(cz_made.sem, cz_made.at(l, 1))
                dve.wait_ge(proj_read.sem, proj_read.at(l, BB + 1))
                for c in range(2):
                    y = cv_c[:, c, :]
                    ts(y, cv_z[:, c, 0:SEQ], cw_cur[:, 0, c:c + 1], cb_cur[:, c:c + 1], ALU.mult, ALU.add).then_inc(dve_chain, 1)
                    dve.wait_ge(dve_chain, links.next())
                    for w in (1, 2):
                        stt(y, cv_z[:, c, w:w + SEQ], cw_cur[:, w, c:c + 1], y, ALU.mult, ALU.add).then_inc(dve_chain, 1)
                        dve.wait_ge(dve_chain, links.next())
                tt(cv_h[:, :, :], cv_c[:, :, :], cv_b[:, :, :], ALU.mult).then_inc(yc_made.sem, 1)
                lo(12)
                turn_in(2)
                scan(2)
                lo(13)
                turn_out(2)
                attn_rest(1, 1)
                lo(14)
                turn_in(3)
                scan(3)
                lo(15)
                turn_out(3)
                attn_rest(2, 0)
                lo(16)
                dve.wait_ge(yc_hi.sem, yc_hi.at(l, 1))
                tt(y_cs[:, 0:2, 1, :], cv_h[:, :, :], f32(y_cs[:, 0:2, 0, :]), ALU.subtract).then_inc(yc_lo.sem, 1)
                dve.wait_ge(c_done.sem, c_done.at(l, 4))
                for c in range(2):
                    last = stt(td[:, 0, c, :], uT[:, c, :], d_cur[:, c:c + 1], ps[:, 2, c * SEQ:c * SEQ + SEQ],
                               ALU.mult, ALU.add)
                last.then_inc(yd_made.sem, 1)
                lo(17)
                lo(18)
                dve.wait_ge(glu_sig.sem, glu_sig.at(l, 1))
                tt(td[:, 1], sw[:, 0], td[:, 0], ALU.mult).then_inc(ys_made.sem, 1)
                lo(19)
                dve.wait_ge(ys_hi.sem, ys_hi.at(l, 1))
                tt(y_cs[:, 2:4, 1, :], td[:, 1], f32(y_cs[:, 2:4, 0, :]), ALU.subtract).then_inc(ys_lo.sem, 1)
                lo(20)
                lo(21)
                dve.wait_ge(proj_read.sem, proj_read.at(l, PROJ_CHUNKS))
                branch_sum(0)
                lo(22)
                sum_rest(0)
                branch_sum(1)
                lo(23)
                sum_rest(1)
                branch_sum(2)
                lo(24)
                sum_rest(2)
                lo(25)
                branch_sum(3)
                lo(26)
                sum_rest(3)
                rest(l, FFN0[1])
                norm(l, 1, FFN0[1] - 1, 1.0)
                turned(l, 1)
                rest(l, FFN0[1] + 1)
                ffn(l, 1, True)
                norm(l, 2, LAYER_CHUNKS - 1, 0.5)
                links.leave()

            dve.wait_ge(gb_landed.sem, gb_landed.at(DEPTH, 0))
            dve.wait_ge(xn_made.sem, xn_made.at(DEPTH, 0))
            for t, part in ((1, slice(0, D)), (0, slice(D // 2, D))):
                tt(res[:, t, part], res[:, t, part], gb[:, 0, part], ALU.mult).then_inc(dve_chain, 1)
                dve.wait_ge(dve_chain, links.next())
                tt(res[:, t, part], res[:, t, part], gb[:, 1, part], ALU.add).then_inc(out_made[t], 1)


_INPUTS = ["x", "ffn1_w_gate", "ffn1_w_up", "ffn1_w_down", "ln1_g", "ln1_b", "w_in", "conv_w", "conv_b",
           "ssm_a_re", "ssm_a_im", "ssm_log_dt", "ssm_b_re", "ssm_b_im", "ssm_c_re", "ssm_c_im", "ssm_d",
           "ssm_w_glu", "attn_sinks", "w_br_conv", "w_br_ssm", "w_br_attn", "w_out", "ln2_g", "ln2_b",
           "ffn2_w_gate", "ffn2_w_up", "ffn2_w_down", "ln3_g", "ln3_b"]


def kernel(**inputs):
    import numpy as np
    import concourse.bacc as bacc
    from concourse.bass_utils import run_bass_kernel_spmd

    nc = bacc.Bacc("TRN2", target_bir_lowering=False, num_devices=1)
    arrays, args = {}, []
    for name in _INPUTS:
        a = np.ascontiguousarray(inputs[name])
        arrays[f"in_{name}"] = a
        args.append(nc.dram_tensor(f"in_{name}", a.shape, mybir.dt.from_np(a.dtype), kind="ExternalInput").ap())
    args.append(nc.dram_tensor("out", (1, SEQ, D), F32, kind="ExternalOutput").ap())
    trunk(nc, *args)
    return run_bass_kernel_spmd(nc, [arrays], core_ids=[0]).results[0]["out"]
```
